# Optimizing a Trainium2 kernel written in Bass

```python
import math
import jax
import jax.numpy as jnp
from jax import lax
import numpy as np

D_MODEL = 1024
BATCH = 1
SEQ = 256
DEPTH = 2

GRID_W = 64
CTX_LEN = 256
N_MIXERS = 3
EPS = 1e-6
N_MOD = 6

HEAD_DIM = 128
N_HEADS = D_MODEL // HEAD_DIM
N_KV_HEADS = max(1, N_HEADS // 4)
Q_GROUP = N_HEADS // N_KV_HEADS
Q_BLOCK = 128
ROPE_AXIS_DIM = HEAD_DIM // 2
ROPE_THETA = 10000.0

SSD_D_INNER = 2 * D_MODEL
SSD_HEAD_DIM = 64
SSD_N_HEADS = SSD_D_INNER // SSD_HEAD_DIM
SSD_N_GROUPS = 4
SSD_HPG = SSD_N_HEADS // SSD_N_GROUPS
SSD_D_STATE = 128
SSD_CONV = 3
SSD_CHUNK = 128
SSD_CONV_CH = SSD_D_INNER + 2 * SSD_N_GROUPS * SSD_D_STATE
SSD_IN_DIM = SSD_D_INNER + SSD_CONV_CH + 2 * SSD_N_HEADS
DT_MIN = 1e-3
DT_MAX = 0.1

CMLP_CHUNK = 128
CMLP_D = 2 * D_MODEL
CMLP_GROUPS = 8
CMLP_GROUP_W = CMLP_D // CMLP_GROUPS

D_FF = 7 * D_MODEL // 2
N_EXPERTS = 8
TOP_K = 2
D_FF_EXPERT = 7 * D_MODEL // 2

kernel_name = 'hybrid_diffusion_gqa_ssd_gmlp_moe'

def _rms_norm(x, g):
    xf = x.astype(jnp.float32)
    y = xf * lax.rsqrt(jnp.mean(xf * xf, axis=-1, keepdims=True) + EPS)
    return (y * g.astype(jnp.float32)).astype(x.dtype)

def _modulate(h, shift, scale):
    return h * (1 + scale) + shift

def _axial_rope_tables(n_tok):
    rows = n_tok // GRID_W
    row_ids = jnp.broadcast_to(jnp.arange(rows)[:, None], (rows, GRID_W)).reshape(-1)
    col_ids = jnp.broadcast_to(jnp.arange(GRID_W)[None, :], (rows, GRID_W)).reshape(-1)
    inv_freq = 1.0 / (ROPE_THETA ** (jnp.arange(0, ROPE_AXIS_DIM, 2, dtype=jnp.float32) / ROPE_AXIS_DIM))
    ang_r = row_ids.astype(jnp.float32)[:, None] * inv_freq
    ang_c = col_ids.astype(jnp.float32)[:, None] * inv_freq
    return (jnp.cos(ang_r), jnp.sin(ang_r), jnp.cos(ang_c), jnp.sin(ang_c))

def _rope_1d(x, cos, sin):
    x1, x2 = jnp.split(x, 2, axis=-1)
    cos = cos[:, None, :]
    sin = sin[:, None, :]
    return jnp.concatenate([x1 * cos - x2 * sin, x2 * cos + x1 * sin], axis=-1)

def _apply_axial_rope(x, tabs):
    cos_r, sin_r, cos_c, sin_c = tabs
    xf = x.astype(jnp.float32)
    x_row, x_col = jnp.split(xf, 2, axis=-1)
    out = jnp.concatenate([_rope_1d(x_row, cos_r, sin_r), _rope_1d(x_col, cos_c, sin_c)], axis=-1)
    return out.astype(x.dtype)

def _attend(q, k, v):
    s = jnp.einsum('bqkgd,bskd->bkgqs', q, k, preferred_element_type=jnp.float32) * (HEAD_DIM ** -0.5)
    p = jax.nn.softmax(s, axis=-1).astype(v.dtype)
    return jnp.einsum('bkgqs,bskd->bqkgd', p, v)

def _attention_mixer(a_c, a_l, w_qkv, q_g, k_g, w_o, rope_tabs, need_ctx):
    def project(a):
        b, n, _ = a.shape
        qkv = a @ w_qkv
        q, k, v = jnp.split(qkv, [N_HEADS * HEAD_DIM, (N_HEADS + N_KV_HEADS) * HEAD_DIM], axis=-1)
        q = _rms_norm(q.reshape(b, n, N_HEADS, HEAD_DIM), q_g)
        k = _rms_norm(k.reshape(b, n, N_KV_HEADS, HEAD_DIM), k_g)
        v = v.reshape(b, n, N_KV_HEADS, HEAD_DIM)
        return q, k, v

    q_c, k_c, v_c = project(a_c)
    q_l, k_l, v_l = project(a_l)
    q_l = _apply_axial_rope(q_l, rope_tabs)
    k_l = _apply_axial_rope(k_l, rope_tabs)
    k_all = jnp.concatenate([k_c, k_l], axis=1)
    v_all = jnp.concatenate([v_c, v_l], axis=1)
    b, n_lat = a_l.shape[:2]
    n_blk = n_lat // Q_BLOCK
    q_blocks = q_l.reshape(b, n_blk, Q_BLOCK, N_KV_HEADS, Q_GROUP, HEAD_DIM).transpose(1, 0, 2, 3, 4, 5)
    o_l = lax.map(lambda qb: _attend(qb, k_all, v_all), q_blocks)
    o_l = o_l.transpose(1, 0, 2, 3, 4, 5).reshape(b, n_lat, N_HEADS * HEAD_DIM)
    y_l = o_l @ w_o
    y_c = None
    if need_ctx:
        n_ctx = a_c.shape[1]
        o_c = _attend(q_c.reshape(b, n_ctx, N_KV_HEADS, Q_GROUP, HEAD_DIM), k_c, v_c)
        y_c = o_c.reshape(b, n_ctx, N_HEADS * HEAD_DIM) @ w_o
    return y_c, y_l

def _dwconv_centred(x, w, b):
    pad = SSD_CONV // 2
    y = lax.conv_general_dilated(x, w[:, None, :].astype(x.dtype), window_strides=(1,),
                                 padding=[(pad, pad)], dimension_numbers=('NWC', 'WIO', 'NWC'),
                                 feature_group_count=x.shape[-1])
    return y + b

def _ssd_scan(xh, dt, A, Bm, Cm, h0):
    b, n = xh.shape[:2]
    nc = n // SSD_CHUNK
    ln = SSD_CHUNK

    def chunk(t):
        return t.reshape((b, nc, ln) + t.shape[2:])

    x_, dt_, B_, C_ = chunk(xh), chunk(dt), chunk(Bm), chunk(Cm)
    dA_cs = jnp.cumsum(dt_ * A, axis=2)
    seg = dA_cs[:, :, :, None] - dA_cs[:, :, None, :]
    lower = jnp.tril(jnp.ones((ln, ln), dtype=bool))[None, None, :, :, None, None]
    decay = jnp.exp(jnp.where(lower, seg, -jnp.inf))
    cb = jnp.einsum('bclgn,bcsgn->bclsg', C_, B_)
    y_diag = jnp.einsum('bclsg,bclsgr,bcsgrp->bclgrp', cb, decay, x_ * dt_[..., None])
    last = dA_cs[:, :, -1:]
    w_state = jnp.exp(last - dA_cs) * dt_
    states = jnp.einsum('bclgn,bclgr,bclgrp->bcgrpn', B_, w_state, x_)
    chunk_decay = jnp.exp(last[:, :, 0])

    def step(h, inp):
        dec, st = inp
        return h * dec[..., None, None] + st, h

    h_final, h_in = lax.scan(step, h0, (jnp.moveaxis(chunk_decay, 1, 0), jnp.moveaxis(states, 1, 0)))
    h_in = jnp.moveaxis(h_in, 0, 1)
    y_off = jnp.einsum('bclgn,bcgrpn,bclgr->bclgrp', C_, h_in, jnp.exp(dA_cs))
    return (y_diag + y_off).reshape(xh.shape), h_final

def _ssd_mixer(a_c, a_l, w_in, conv_w, conv_b, dt_bias_f, dt_bias_b, a_log_f, a_log_b,
               d_skip, norm_g, w_out, need_ctx):
    f32 = jnp.float32

    def project(a):
        b, n, _ = a.shape
        zxbcdt = a @ w_in
        z, xbc, dt = jnp.split(zxbcdt, [SSD_D_INNER, SSD_D_INNER + SSD_CONV_CH], axis=-1)
        xbc = jax.nn.silu(_dwconv_centred(xbc, conv_w, conv_b))
        xs, Bm, Cm = jnp.split(xbc, [SSD_D_INNER, SSD_D_INNER + SSD_N_GROUPS * SSD_D_STATE], axis=-1)
        xs = xs.reshape(b, n, SSD_N_GROUPS, SSD_HPG, SSD_HEAD_DIM).astype(f32)
        Bm = Bm.reshape(b, n, SSD_N_GROUPS, SSD_D_STATE).astype(f32)
        Cm = Cm.reshape(b, n, SSD_N_GROUPS, SSD_D_STATE).astype(f32)
        dt = dt.astype(f32)
        dt_f = jax.nn.softplus(dt[..., :SSD_N_HEADS] + dt_bias_f.astype(f32)).reshape(b, n, SSD_N_GROUPS, SSD_HPG)
        dt_b = jax.nn.softplus(dt[..., SSD_N_HEADS:] + dt_bias_b.astype(f32)).reshape(b, n, SSD_N_GROUPS, SSD_HPG)
        return z, xs, Bm, Cm, dt_f, dt_b

    A_f = -jnp.exp(a_log_f.astype(f32)).reshape(SSD_N_GROUPS, SSD_HPG)
    A_b = -jnp.exp(a_log_b.astype(f32)).reshape(SSD_N_GROUPS, SSD_HPG)
    z_c, x_c, B_c, C_c, df_c, db_c = project(a_c)
    z_l, x_l, B_l, C_l, df_l, db_l = project(a_l)
    b = a_l.shape[0]
    h0 = jnp.zeros((b, SSD_N_GROUPS, SSD_HPG, SSD_HEAD_DIM, SSD_D_STATE), f32)

    def flip(t):
        return jnp.flip(t, axis=1)

    yf_c, sf_c = _ssd_scan(x_c, df_c, A_f, B_c, C_c, h0)
    yf_l, _ = _ssd_scan(x_l, df_l, A_f, B_l, C_l, sf_c)
    yb_c, sb_c = _ssd_scan(flip(x_c), flip(db_c), A_b, flip(B_c), flip(C_c), h0)
    yb_l, _ = _ssd_scan(flip(x_l), flip(db_l), A_b, flip(B_l), flip(C_l), sb_c)
    d = d_skip.astype(f32).reshape(SSD_N_GROUPS, SSD_HPG, 1)

    def finish(y_f, y_b_rev, xs, z):
        n = xs.shape[1]
        y = (y_f + flip(y_b_rev) + xs * d).reshape(b, n, SSD_D_INNER)
        gated = (y * jax.nn.silu(z.astype(f32))).reshape(b, n, SSD_N_GROUPS, SSD_D_INNER // SSD_N_GROUPS)
        gated = gated * lax.rsqrt(jnp.mean(gated * gated, axis=-1, keepdims=True) + EPS)
        gated = gated.reshape(b, n, SSD_D_INNER) * norm_g.astype(f32)
        return gated.astype(z.dtype) @ w_out

    y_l = finish(yf_l, yb_l, x_l, z_l)
    y_c = finish(yf_c, yb_c, x_c, z_c) if need_ctx else None
    return y_c, y_l

def _chunk_mlp_mixer(a_c, a_l, w_in, b_in, v_g, w_s, b_s, w_out, need_ctx):
    def mix(a):
        b, n, _ = a.shape
        nc = n // CMLP_CHUNK
        uv = jax.nn.gelu(a @ w_in + b_in, approximate=False)
        u, v = jnp.split(uv, 2, axis=-1)
        v = _rms_norm(v, v_g).reshape(b, nc, CMLP_CHUNK, CMLP_GROUPS, CMLP_GROUP_W)
        v = jnp.einsum('gts,bcsgd->bctgd', w_s, v) + b_s.T[None, None, :, :, None]
        return (u * v.reshape(b, n, CMLP_D)) @ w_out

    y_l = mix(a_l)
    y_c = mix(a_c) if need_ctx else None
    return y_c, y_l

def _swiglu(x, w_gate, w_up, w_down):
    return (jax.nn.silu(x @ w_gate) * (x @ w_up)) @ w_down

def _moe(x, router, w_gate, w_up, w_down):
    logits = (x @ router).astype(jnp.float32)
    top_v, top_i = lax.top_k(logits, TOP_K)
    top_w = jax.nn.softmax(top_v, axis=-1)
    gates = jnp.sum(jax.nn.one_hot(top_i, N_EXPERTS, dtype=jnp.float32) * top_w[..., None], axis=-2)
    gates = gates.astype(x.dtype)
    out = jnp.zeros_like(x)
    for e in range(N_EXPERTS):
        out = out + gates[..., e:e + 1] * _swiglu(x, w_gate[e], w_up[e], w_down[e])
    return out

def setup_inputs(seed: int = 0) -> dict:
    key = jax.random.key(seed)
    keys = jax.random.split(key, 48)
    kit = iter(range(48))
    f32 = jnp.float32

    def nk():
        return keys[next(kit)]

    def normal(shape, scale):
        return scale * jax.random.normal(nk(), shape, f32)

    def dense(shape, fan_in, mult=1.0):
        return normal(shape, mult * fan_in ** -0.5)

    def gain(shape):
        return 1.0 + normal(shape, 0.02)

    def bias(shape):
        return normal(shape, 0.02)

    n_attn = len(range(0, DEPTH, N_MIXERS))
    n_ssd = len(range(1, DEPTH, N_MIXERS))
    n_cmlp = len(range(2, DEPTH, N_MIXERS))
    n_dense = len(range(0, DEPTH, 2))
    n_moe = len(range(1, DEPTH, 2))

    x = jax.random.normal(nk(), (BATCH, SEQ, D_MODEL), f32)
    c = jax.random.normal(nk(), (BATCH, D_MODEL), f32)
    ctx = jax.random.normal(nk(), (BATCH, CTX_LEN, D_MODEL), f32)
    c_ctx = jax.random.normal(nk(), (D_MODEL,), f32)

    u = jax.random.uniform(nk(), (2, n_ssd, SSD_N_HEADS), f32)
    dt0 = jnp.exp(u * (math.log(DT_MAX) - math.log(DT_MIN)) + math.log(DT_MIN))
    dt_bias = dt0 + jnp.log(-jnp.expm1(-dt0))
    a_log = jnp.log(jax.random.uniform(nk(), (2, n_ssd, SSD_N_HEADS), f32, 1.0, 16.0))

    return {
        'x': x,
        'c': c,
        'ctx': ctx,
        'c_ctx': c_ctx,
        'w_mod': dense((DEPTH, D_MODEL, N_MOD * D_MODEL), D_MODEL, 0.5),
        'b_mod': bias((DEPTH, N_MOD * D_MODEL)),
        'norm1_g': gain((DEPTH, D_MODEL)),
        'norm2_g': gain((DEPTH, D_MODEL)),
        'attn_w_qkv': dense((n_attn, D_MODEL, (N_HEADS + 2 * N_KV_HEADS) * HEAD_DIM), D_MODEL),
        'attn_q_g': gain((n_attn, HEAD_DIM)),
        'attn_k_g': gain((n_attn, HEAD_DIM)),
        'attn_w_o': dense((n_attn, N_HEADS * HEAD_DIM, D_MODEL), N_HEADS * HEAD_DIM),
        'ssd_w_in': dense((n_ssd, D_MODEL, SSD_IN_DIM), D_MODEL),
        'ssd_conv_w': dense((n_ssd, SSD_CONV, SSD_CONV_CH), SSD_CONV),
        'ssd_conv_b': bias((n_ssd, SSD_CONV_CH)),
        'ssd_dt_bias_f': dt_bias[0],
        'ssd_dt_bias_b': dt_bias[1],
        'ssd_a_log_f': a_log[0],
        'ssd_a_log_b': a_log[1],
        'ssd_d_skip': gain((n_ssd, SSD_N_HEADS)),
        'ssd_norm_g': gain((n_ssd, SSD_D_INNER)),
        'ssd_w_out': dense((n_ssd, SSD_D_INNER, D_MODEL), SSD_D_INNER),
        'cmlp_w_in': dense((n_cmlp, D_MODEL, 2 * CMLP_D), D_MODEL),
        'cmlp_b_in': bias((n_cmlp, 2 * CMLP_D)),
        'cmlp_v_g': gain((n_cmlp, CMLP_D)),
        'cmlp_w_s': dense((n_cmlp, CMLP_GROUPS, CMLP_CHUNK, CMLP_CHUNK), CMLP_CHUNK),
        'cmlp_b_s': gain((n_cmlp, CMLP_GROUPS, CMLP_CHUNK)),
        'cmlp_w_out': dense((n_cmlp, CMLP_D, D_MODEL), CMLP_D),
        'ffn_w_gate': dense((n_dense, D_MODEL, D_FF), D_MODEL),
        'ffn_w_up': dense((n_dense, D_MODEL, D_FF), D_MODEL),
        'ffn_w_down': dense((n_dense, D_FF, D_MODEL), D_FF),
        'moe_router': dense((n_moe, D_MODEL, N_EXPERTS), D_MODEL),
        'moe_w_gate': dense((n_moe, N_EXPERTS, D_MODEL, D_FF_EXPERT), D_MODEL),
        'moe_w_up': dense((n_moe, N_EXPERTS, D_MODEL, D_FF_EXPERT), D_MODEL),
        'moe_w_down': dense((n_moe, N_EXPERTS, D_FF_EXPERT, D_MODEL), D_FF_EXPERT),
        'final_g': gain((D_MODEL,)),
    }

def reference(x, c, ctx, c_ctx, w_mod, b_mod, norm1_g, norm2_g,
              attn_w_qkv, attn_q_g, attn_k_g, attn_w_o,
              ssd_w_in, ssd_conv_w, ssd_conv_b, ssd_dt_bias_f, ssd_dt_bias_b,
              ssd_a_log_f, ssd_a_log_b, ssd_d_skip, ssd_norm_g, ssd_w_out,
              cmlp_w_in, cmlp_b_in, cmlp_v_g, cmlp_w_s, cmlp_b_s, cmlp_w_out,
              ffn_w_gate, ffn_w_up, ffn_w_down,
              moe_router, moe_w_gate, moe_w_up, moe_w_down, final_g):
    n_lat = x.shape[1]
    rope_tabs = _axial_rope_tables(n_lat)
    silu_c = jax.nn.silu(c)
    silu_cc = jax.nn.silu(c_ctx)
    h_lat, h_ctx = x, ctx
    for i in range(DEPTH):
        need_ctx = i < DEPTH - 1
        mod_l = silu_c @ w_mod[i] + b_mod[i]
        mod_c = silu_cc @ w_mod[i] + b_mod[i]
        sh1_l, sc1_l, g1_l, sh2_l, sc2_l, g2_l = jnp.split(mod_l[:, None, :], N_MOD, axis=-1)
        sh1_c, sc1_c, g1_c, sh2_c, sc2_c, g2_c = jnp.split(mod_c, N_MOD, axis=-1)

        a_l = _modulate(_rms_norm(h_lat, norm1_g[i]), sh1_l, sc1_l)
        a_c = _modulate(_rms_norm(h_ctx, norm1_g[i]), sh1_c, sc1_c)
        kind, j = i % N_MIXERS, i // N_MIXERS
        if kind == 0:
            y_c, y_l = _attention_mixer(a_c, a_l, attn_w_qkv[j], attn_q_g[j], attn_k_g[j], attn_w_o[j],
                                        rope_tabs, need_ctx)
        elif kind == 1:
            y_c, y_l = _ssd_mixer(a_c, a_l, ssd_w_in[j], ssd_conv_w[j], ssd_conv_b[j],
                                  ssd_dt_bias_f[j], ssd_dt_bias_b[j], ssd_a_log_f[j], ssd_a_log_b[j],
                                  ssd_d_skip[j], ssd_norm_g[j], ssd_w_out[j], need_ctx)
        else:
            y_c, y_l = _chunk_mlp_mixer(a_c, a_l, cmlp_w_in[j], cmlp_b_in[j], cmlp_v_g[j], cmlp_w_s[j],
                                        cmlp_b_s[j], cmlp_w_out[j], need_ctx)
        h_lat = h_lat + g1_l * y_l
        a_l = _modulate(_rms_norm(h_lat, norm2_g[i]), sh2_l, sc2_l)
        if need_ctx:
            h_ctx = h_ctx + g1_c * y_c
            a_c = _modulate(_rms_norm(h_ctx, norm2_g[i]), sh2_c, sc2_c)
            tokens = jnp.concatenate([a_c, a_l], axis=1)
        else:
            tokens = a_l

        k = i // 2
        if i % 2 == 0:
            f = _swiglu(tokens, ffn_w_gate[k], ffn_w_up[k], ffn_w_down[k])
        else:
            f = _moe(tokens, moe_router[k], moe_w_gate[k], moe_w_up[k], moe_w_down[k])
        h_lat = h_lat + g2_l * f[:, f.shape[1] - n_lat:]
        if need_ctx:
            h_ctx = h_ctx + g2_c * f[:, :f.shape[1] - n_lat]
    return _rms_norm(h_lat, final_g)


_drawn_inputs = setup_inputs


def setup_inputs(seed=0):
    import zlib

    import numpy as np

    out = dict(_drawn_inputs(seed))
    spreads = {}
    factors = {'norm1_g': 5.232,
     'norm2_g': 4.157,
     'attn_q_g': 8.0,
     'attn_k_g': 8.0,
     'ssd_conv_b': 14.292,
     'ssd_d_skip': 64.0,
     'ssd_norm_g': 17.882,
     'final_g': 7.989}
    for name, (base, spread) in spreads.items():
        noise = np.random.default_rng([zlib.crc32(name.encode()), seed]).standard_normal(out[name].shape)
        drawn = base * np.exp(spread * noise) if base else spread * noise
        out[name] = jnp.asarray(drawn.astype(out[name].dtype))
    for name, factor in factors.items():
        out[name] = (out[name] * factor).astype(out[name].dtype)
    return out
```

```python
from contextlib import ExitStack

import numpy as np

import concourse.bass as bass
from concourse import mybir

P = 128
ALU = mybir.AluOpType
ACT = mybir.ActivationFunctionType
F32 = mybir.dt.float32
I32 = mybir.dt.int32
F32R = mybir.dt.float32r
AX = mybir.AxisListType


def constants(seq, grid_w, head_dim, n_experts):
    p = np.arange(P)[:, None]
    f = np.arange(P)[None, :]
    parts = [p == f, p <= f, p >= f, p < f, p > f, np.broadcast_to(f + 1, (P, P))]
    e = np.arange(n_experts)[None, :]
    parts += [np.broadcast_to(n_experts - e, (P, n_experts)), np.broadcast_to(e, (P, n_experts))]
    axis_dim = head_dim // 2
    inv_freq = (1.0 / (10000.0 ** (np.arange(0, axis_dim, 2, dtype=np.float32) / axis_dim))).astype(np.float32)
    tok = np.arange(seq)
    tables = []
    for ids in (tok // grid_w, tok % grid_w):
        ang = ids.astype(np.float32)[:, None] * inv_freq
        tables.append((np.cos(ang), np.sin(ang)))
    cos = np.concatenate([np.concatenate([c, c], 1) for c, _ in tables], 1)
    sin = np.concatenate([np.concatenate([-s, s], 1) for _, s in tables], 1)
    for table in (cos, sin):
        parts.append(table.reshape(seq // P, P, head_dim).transpose(1, 0, 2).reshape(P, -1))
    return np.ascontiguousarray(np.concatenate([np.asarray(x, np.float32) for x in parts], 1))


def backbone(nc, consts, x, c, ctx_tok, c_ctx, w_mod, b_mod, norm1_g, norm2_g,
             w_qkv, q_g, k_g, w_o,
             ssd_w_in, conv_w, conv_b, dt_bias_f, dt_bias_b, a_log_f, a_log_b, d_skip, ssd_norm_g, ssd_w_out,
             ffn_gate, ffn_up, ffn_down, router, moe_gate, moe_up, moe_down, final_g, out):
    _, SEQ, D = x.shape
    CTX = ctx_tok.shape[1]
    KD = D // P
    CT, LT = CTX // P, SEQ // P
    T = CT + LT
    NTOK = CTX + SEQ
    N = 512
    HD = q_g.shape[1]
    NH = w_o.shape[1] // HD
    NKV = (w_qkv.shape[2] // HD - NH) // 2
    QG = NH // NKV
    QKVW = w_qkv.shape[2]
    DFF = ffn_gate.shape[2]
    FC = DFF // N
    INNER = ssd_w_out.shape[1]
    CONV_CH = conv_w.shape[2]
    GN = (CONV_CH - INNER) // 2
    SG = GN // P
    SH = dt_bias_f.shape[1]
    HP = SH // SG
    HDIM = INNER // SH
    NE = router.shape[2]
    EPS = 1e-6
    EXTRA = (2 * SEQ) // (P + 1)
    assert D == 1024 and T == 4 and CT == 2 and LT == 2 and HD == P and QKVW == 3 * N and GN == N and HP * HDIM == N

    es = ExitStack()
    with es:
        def sb(name, shape, dt=F32):
            return es.enter_context(nc.sbuf_tensor(name, shape, dt))

        def sem(name):
            return es.enter_context(nc.semaphore(name))

        NC_ = consts.shape[1]
        const = sb("const", [P, NC_])
        ident = const[:, 0:P]
        LE, GE, LTm, GTm = (const[:, P * i:P * i + P] for i in range(1, 5))
        iota1 = const[:, 5 * P:6 * P]
        o = 6 * P
        rev_e = const[:, o:o + NE]
        fwd_e = const[:, o + NE:o + 2 * NE]
        o += 2 * NE
        rope_c = const[:, o:o + LT * HD].rearrange("p (t d) -> p t d", t=LT)
        rope_s = const[:, o + LT * HD:o + 2 * LT * HD].rearrange("p (t d) -> p t d", t=LT)
        ones = sb("ones", [P, P])
        rows1 = sb("rows1", [64, P])
        rows2 = sb("rows2", [4 * CONV_CH // P, P])
        cols1 = sb("cols1", [P, 64])
        cols2 = sb("cols2", [P, 4 * CONV_CH // P])
        cstat = sb("cstat", [P, KD, 32])
        qg_b = sb("qg_b", [P, HD])
        kg_b = sb("kg_b", [P, HD])
        dskip_b = sb("dskip_b", [P, SH])
        dtb_b = sb("dtb_b", [P, 2 * SH])
        alog_b = sb("alog_b", [P, 2 * SH])
        rout = sb("rout", [P, KD, NE])
        w_dt = sb("w_dt", [P, KD, 2 * SH])
        mod_all = sb("mod_all", [P, 24 * P])
        modr = mod_all[:, 0:12 * P].rearrange("p (u n) -> p u n", u=12)
        biasr = mod_all[:, 12 * P:24 * P].rearrange("p (u n) -> p u n", u=12)
        modc = sb("modc", [P, 48, 2])
        gcol = sb("gcol", [P, 2, KD, 2])
        stat = sb("stat", [P, 64])
        H = sb("H", [P, T, D])
        modb = sb("modb", [P, 4, D])
        AT_ = sb("AT", [P, 4096])
        aT_at = nc.sbuf_base - 4 * 4096
        aT = AT_[:, :].rearrange("p (k n) -> p k n", k=KD)
        slab = sb("slab", [P, 8 * 4096])
        slab_at = nc.sbuf_base - 4 * 8 * 4096

        def at(name, o, shape, dt=F32):
            return nc.alloc_sbuf_tensor_at(name, [P] + shape, dt, offset=slab_at + 4 * o)

        WR = slab[:, 0:3 * 4096].rearrange("p (a n) -> p a n", a=3)
        AR0 = 3 * 4096
        AR = slab[:, 3 * 4096:8 * 4096]

        def ar(o, *dims):
            n = 1
            for d_ in dims:
                n *= d_
            v = AR[:, o:o + n]
            if len(dims) == 2:
                v = v.rearrange("p (a b) -> p a b", a=dims[0])
            if len(dims) == 3:
                v = v.rearrange("p (a b c) -> p a b c", a=dims[0], b=dims[1])
            return v

        QKW = (NH + NKV) * HD
        qk = ar(0, T, QKW)
        pbuf = ar(0, 8, N)
        vv = ar(5120, T, NKV * HD)
        qT = ar(6144, NH, NTOK)
        kT = ar(10240, NKV, NTOK)
        oT = ar(11264, NH, NTOK)
        pT = ar(15360, 2, T, N)
        xn = ar(15360, T, D)
        rope_t = ar(11264, 10, HD)
        sq_t = ar(12544, 10, HD)
        HALF = 2048
        hT = ar(0, 4, N)
        facc = ar(4096, T, D)
        h_lo = at("h_lo", AR0, [4, N], F32R)
        h_hi = at("h_hi", AR0 + 8192, [4, N], F32R)
        a_lo = nc.alloc_sbuf_tensor_at("a_lo", [P, KD, NTOK], F32R, offset=aT_at)
        a_hi = at("a_hi", AR0 + 10240, [KD, NTOK], F32R)
        f_raw = at("f_raw", 0, [3, HALF])
        f_lo = at("f_lo", 0, [3, HALF], F32R)
        f_hi = at("f_hi", 3 * HALF, [3, HALF], F32R)
        mod_unit = ar(16384, KD, N)

        xt = ar(0, T, INNER)
        btok = ar(8192, T, GN)
        bT = ar(10240, SG, SEQ)
        cT = ar(11264, SG, SEQ)
        zs = ar(12288, LT, INNER)
        raw = ar(16384, 2, 2, CTX + 2)
        conv = ar(17416, 2, NTOK)
        convs = ar(18440, 2, NTOK)
        xw = ar(16384, 2, INNER)
        hs = [[WR[:, 1, 0:INNER], WR[:, 1, INNER:2 * INNER]], [WR[:, 2, 0:INNER], WR[:, 2, INNER:2 * INNER]]]
        yacc = AT_[:, :].rearrange("p (t n) -> p t n", t=LT)
        xdt = [ar(0, 2, INNER), ar(16384, 2, INNER)]
        ld = [modb[:, 1, :].rearrange("p (h s) -> p h s", h=HP), modb[:, 3, :].rearrange("p (h s) -> p h s", h=HP)]
        mm = [H[:, 0:CT, :].rearrange("p a (h s) -> p a h s", h=HP), ar(8192, 2, HP, P)]
        cbm = mod_all[:, 0:16 * P].rearrange("p (d t g l) -> p d t g l", d=2, t=LT, g=SG)
        spare = mod_all[:, 16 * P:24 * P]
        yoff_t = spare.rearrange("p (b n) -> p b n", b=2)
        gT = ar(0, INNER // P, SEQ)
        sp_a, sp_u, sp_s = (spare[:, 256 * i:256 * i + 256] for i in range(3))
        dt_ = sb("dt", [P, T, 2 * SH])
        da = sb("da", [P, T, 2 * SH])
        ex = sb("ex", [P, 384])
        wsc = sb("wsc", [P, 192])
        aTl = AT_[:, 0:2048].rearrange("p (k n) -> p k n", k=KD)
        y2 = AT_[:, 2048:4096].rearrange("p (t d) -> p t d", t=LT)
        fin_g = AT_[:, 0:D]
        RS, HS_, LEAD, NHU = 7, 6, 3, 2 * 3 * FC
        m_raw = at("m_raw", 0, [RS, HALF])
        m_lo = at("m_lo", 0, [RS, HALF], F32R)
        m_hi = at("m_hi", RS * HALF, [HS_, HALF], F32R)
        o_m = (RS + HS_) * HALF
        hT_hi = at("hT_hi", o_m, [3, 4, P], F32R)
        hT_lo = at("hT_lo", o_m + 1536, [3, 4, P], F32R)
        xe_hi = at("xe_hi", o_m + 3072, [KD, P], F32R)
        xe_lo = at("xe_lo", o_m + 4096, [KD, P], F32R)
        assert o_m + 5120 <= 8 * 4096 and NHU % RS == 0 and NHU % HS_ == 0
        xe = H[:, 0, :].rearrange("p (k s) -> p k s", k=KD)
        ye = H[:, 1, :]
        hm = modb[:, 1, :].rearrange("p (b n) -> p b n", b=2)
        sgm = modb[:, 3, :].rearrange("p (b n) -> p b n", b=2)
        macc = mod_all[:, 0:2 * D].rearrange("p (t d) -> p t d", t=LT)
        perm = spare[:, 0:2 * P].rearrange("p (t s) -> p t s", t=LT)
        permg = spare[:, 2 * P:4 * P].rearrange("p (t s) -> p t s", t=LT)
        permT = spare[:, 4 * P:6 * P]
        NJ = NE + EXTRA
        rt = sb("rt", [P, 24, NE])
        rankj = sb("rankj", [P, LT, NJ])
        gatej = sb("gatej", [P, LT, NJ])
        tabf = sb("tabf", [P, 8])
        tabi = sb("tabi", [P, 8], I32)

        PS = es.enter_context(nc.psum_tensor("PS", [P, 8, N], F32))

        params_in = sem("params_in")
        rows_in = sem("rows_in")
        tokens_in = sem("tokens_in")
        bias_in = sem("bias_in")
        unit_in = [sem(f"unit_in{i}") for i in range(3)]
        unit_used = sem("unit_used")
        zeroed = sem("zeroed")
        v_full, v_free, a_full, a_free = sem("v_full"), sem("v_free"), sem("a_full"), sem("a_free")
        cols_ready, csil_ready = sem("cols_ready"), sem("csil_ready")
        modr_ready, modc_ready, modb_ready = sem("modr_ready"), sem("modc_ready"), sem("modb_ready")
        sumsq_ready, meansq_ready, rms_ready = sem("sumsq_ready"), sem("meansq_ready"), sem("rms_ready")
        xn_ready, at_dve, at_act = sem("xn_ready"), sem("at_dve"), sem("at_act")
        h_ready = sem("h_ready")
        qkv_copied, qsum_ready, qsq_ready, qrms_ready = sem("qkv_copied"), sem("qsum_ready"), sem("qsq_ready"), sem("qrms_ready")
        qk_ready, qkT_ready = sem("qk_ready"), sem("qkT_ready")
        nmax_ready, p_exp, p_norm, p_used, pT_ready, oT_ready = (sem(n) for n in (
            "nmax_ready", "p_exp", "p_norm", "p_used", "pT_ready", "oT_ready"))
        fa_full, fa_free = sem("fa_full"), sem("fa_free")
        f_in = [sem(f"f_in{i}") for i in range(3)]
        fhi_ready, flo_ready, ahi_ready, alo_ready, hhi_ready, hlo_ready = (sem(n) for n in (
            "fhi_ready", "flo_ready", "ahi_ready", "alo_ready", "hhi_ready", "hlo_ready"))
        modu_in, modu_used, modu_added = sem("modu_in"), sem("modu_used"), sem("modu_added")
        dve_step, act_step = sem("dve_step"), sem("act_step")
        pads_ready, raw_ready, conv_ready, convs_ready, bT_ready = (sem(n) for n in (
            "pads_ready", "raw_ready", "conv_ready", "convs_ready", "bT_ready"))
        sp_in, sp_exp, alog_ready, da_ready, ex_ready = (sem(n) for n in ("sp_in", "sp_exp", "alog_ready", "da_ready", "ex_ready"))
        xw_ready, xw_used, ld_ready, states_used, m_ready = (sem(n) for n in ("xw_ready", "xw_used", "ld_ready", "states_used", "m_ready"))
        y_sum, y_sq, y_ms, y_rms, yn_ready = (sem(n) for n in ("y_sum", "y_sq", "y_ms", "y_rms", "yn_ready"))
        mask_ready, gap_ready, gap_exp, tables_ready = (sem(n) for n in ("mask_ready", "gap_ready", "gap_exp", "tables_ready"))
        moe_in = [sem(f"moe_in{i}") for i in range(RS)]
        moe_free, moe_hi, moe_lo = sem("moe_free"), sem("moe_hi"), sem("moe_lo")
        xe_ready, xhi_ready, xlo_ready, th_ready = sem("xe_ready"), sem("xhi_ready"), sem("xlo_ready"), sem("th_ready")
        permg_ready, zero_out = sem("permg_ready"), sem("zero_out")
        mv_full, mv_free, ma_full, ma_free = sem("mv_full"), sem("mv_free"), sem("ma_full"), sem("ma_free")
        perm_ready, down_full, ye_ready, fin_in = sem("perm_ready"), sem("down_full"), sem("ye_ready"), sem("fin_in")
        out_written = sem("out_written")

        units = []

        def cols_unit(w, c0):
            return w[:, c0:c0 + N].rearrange("(k p) n -> p k n", p=P)

        def rows_unit(w, r0):
            return w[r0:r0 + 4 * P, :].rearrange("(k p) n -> p k n", p=P)

        first = {}
        first["mod0"] = len(units)
        units += [cols_unit(w_mod[0], N * u) for u in range(4)]
        first["qkv"] = len(units)
        units += [cols_unit(w_qkv[0], N * u) for u in range(3)]
        first["mod0b"] = len(units)
        units += [cols_unit(w_mod[0], N * u) for u in range(4, 12)]
        first["wo"] = len(units)
        units += [cols_unit(w_o[0], N * u) for u in range(2)]
        units_b = []
        first["xbc"] = len(units)
        units_b += [cols_unit(ssd_w_in[0], INNER + N * u) for u in range(CONV_CH // N)]
        first["z"] = first["xbc"] + CONV_CH // N
        units_b += [cols_unit(ssd_w_in[0], N * u) for u in range(INNER // N)]
        first["sout"] = first["z"] + INNER // N
        units_b += [rows_unit(ssd_w_out[0], 4 * P * u) for u in range(INNER // (4 * P))]
        NCT = CONV_CH // P
        NXB = (INNER + GN) // P

        TSEQ = []
        NPAIR = T * NH
        for m in range(NPAIR + 3):
            if m < NPAIR:
                TSEQ.append(("S", m))
            if m >= 3:
                TSEQ.append(("T", m - 3))
                if (m - 3) % QG == QG - 1:
                    TSEQ.append(("M", 4 + (m - 3) // QG))
                if m - 3 >= 5 and (m - 3) % QG == 1:
                    TSEQ.append(("O", (m - 3) // QG - 1))
        TSEQ.append(("O", NPAIR // QG - 1))
        n_s = sum(k == "S" for k, _ in TSEQ)
        n_t = sum(k in "TM" for k, _ in TSEQ)
        n_o = sum(k == "O" for k, _ in TSEQ)
        NFV = 4 + 4 * T
        v0, a0 = {}, {}
        nv = na = 0
        for stage, more_v, more_a in (("prep", 1, 0), ("mod0", 2, 0), ("norm0", 4, 4), ("qkv", 0, 3 * T), ("qkT", 0, 3 * T),
                              ("attn", n_t, n_s + n_o), ("mod0t", 2, 8), ("wo", 2 * T, 0), ("norm1", 4, 4),
                              ("ffn", NFV * FC, 0), ("mod1", 3, 4), ("norm2", 4, 4),
                              ("dt", 1, 0), ("xbc", NXB, NCT), ("dec", 0, 1), ("z", 0, LT * INNER // N),
                              ("cb", LT, 0), ("st", 0, 2 * SG), ("st2", 2 * SG, 0), ("yoff", 2 * LT * SG, 0),
                              ("seg", 0, 4 * LT * SG), ("ydiag", LT * SG, 0), ("gT", LT * INNER // N, 0),
                              ("sout", 2 * LT, 0), ("norm3", 4, 4), ("route", 2, 0), ("end", 0, 0)):
            v0[stage], a0[stage] = nv, na
            nv, na = nv + more_v, na + more_a
        att_a, att_v = {}, {}
        for item in TSEQ:
            if item[0] in "TM":
                att_v[item] = v0["attn"] + len(att_v)
            else:
                att_a[item] = a0["attn"] + len(att_a)

        def v_bank(g):
            return PS[:, g % 4, :]

        def a_bank(g):
            return PS[:, 4 + g % 4, :]

        NTILES = {0: range(T), 1: range(T), 2: range(T), 3: range(CT, T), 4: range(CT, T)}
        sq_done = {0: 0, 1: T, 2: 2 * T, 3: 3 * T, 4: 3 * T + LT}
        H_DONE = {1: 0, 2: T, 3: 2 * T, 4: 2 * T + LT}
        aTs = [aT, aT, aT, aTl]
        aOff = [0, 0, 0, CTX]

        def pair(m):
            batch, hh = m // QG, m % QG
            t, g = batch // NKV, batch % NKV
            return t, g, QG * g + hh, (CT if t < CT else T)

        MSEQ = []
        for cc in range(FC):
            MSEQ += [("G", cc), ("U", cc)]
            if cc == 0:
                MSEQ += [("C", i) for i in range(2 * LT)]
            if cc >= 1:
                MSEQ.append(("T", cc - 1))
            if cc == 3:
                MSEQ.append(("P", 0))
            if cc >= 2:
                MSEQ.append(("D", cc - 2))
        MSEQ += [("X", 0), ("X", 1), ("T", FC - 1), ("D", FC - 2), ("D", FC - 1)]
        m_a = {it: i for i, it in enumerate(x_ for x_ in MSEQ if x_[0] in "XGP")}
        m_v = {it: i for i, it in enumerate(x_ for x_ in MSEQ if x_[0] in "UTC")}
        m_u = {it: i for i, it in enumerate(x_ for x_ in MSEQ if x_[0] in "GUD")}
        NMA, NMV, NMU = len(m_a), len(m_v), len(m_u)
        assert NMA % 2 == 0 and NMV % 3 == 0 and 2 * NMU == NHU

        def mv_bank(it):
            return PS[:, m_v[it] % 3, :]

        def ma_bank(it):
            return PS[:, 3 + m_a[it] % 2, :]

        NFH = 6

        def half_used(v, i):
            if v < 0:
                v, i = v + NFH, i - 1
            V = v0["ffn"] + NFV * i
            return {0: (fa_full, 2 + 4 * i), 1: (v_full, V + 2), 2: (fa_full, 4 + 4 * i), 3: (v_full, V + 4),
                    4: (v_full, V + 4 + 2 * T), 5: (v_full, V + 4 + 4 * T)}[v]

        block = es.enter_context(nc.Block())

        @block.sync
        def _(sp):
            def load(n, src):
                if n >= 3:
                    sp.wait_ge(unit_used, n - 2)
                dst = WR[:, n % 3, :].rearrange("p (k n) -> p k n", k=src.shape[1])
                sp.dma_start(dst, src).then_inc(unit_in[n % 3], 16)

            for n, src in enumerate(units):
                load(n, src)
            sp.wait_ge(v_full, v0["norm1"] + 4)
            sp.wait_ge(a_full, a0["norm1"] + 4)

            def chunk(i, more):
                for v in range(NFH):
                    w = (ffn_gate, ffn_up, ffn_gate, ffn_up, ffn_down, ffn_down)[v][0]
                    o_ = i * N + (N // 2) * (v // 2 % 2 if v < 4 else v - 4)
                    src = w[:, bass.ds(o_, N // 2)] if v < 4 else w[bass.ds(o_, N // 2), :]
                    src = src.rearrange("(k p) n -> p k n", p=P)
                    sp.wait_ge(*half_used(v - 3, i))
                    sp.dma_start(f_raw[:, v % 3, :].rearrange("p (k n) -> p k n", k=src.shape[1]), src).then_inc(f_in[v % 3], 16)
                    if more and v in (1, 3):
                        u = 2 * i + v // 2
                        sp.wait_ge(modu_used, u + 1)
                        sp.dma_start(mod_unit, w_mod[1][:, bass.ds(u * N, N)].rearrange("(k p) n -> p k n", p=P))\
                            .then_inc(modu_in, 16)

            sp.sem_inc(modu_used, 1)
            with sp.Fori(0, FC - 1) as i:
                chunk(i, True)
            chunk(FC - 1, False)
            sp.wait_ge(v_full, v0["ffn"] + NFV * FC)
            for n, src in enumerate(units_b):
                if n + first["xbc"] == first["sout"] + 1:
                    sp.wait_ge(states_used, 1)
                load(n + first["xbc"], src)
            def expert_loads(j, e):
                for it, u in m_u.items():
                    w = {"G": moe_gate, "U": moe_up, "D": moe_down}[it[0]][0][bass.ds(e, 1), :, :]\
                        .rearrange("a k n -> (a k) n")
                    for half in range(2):
                        v = 2 * u + half
                        if it[0] == "D":
                            r = 4 * P * it[1] + 2 * P * half
                            src = w[r:r + 2 * P, :]
                        else:
                            src = w[4 * P * half:4 * P * half + 4 * P, N * it[1]:N * it[1] + N]
                        src = src.rearrange("(k p) n -> p k n", p=P)
                        sp.wait_ge(moe_free, v + 1 + NHU * j)
                        sp.dma_start(m_raw[:, v % RS, :].rearrange("p (k n) -> p k n", k=src.shape[1]), src)\
                            .then_inc(moe_in[v % RS], 16)

            with sp.Fori(0, NE) as j:
                expert_loads(j, j)
            sp.wait_ge(tables_ready, 1)
            jobs = sp.value_load(tabi[0:1, EXTRA:EXTRA + 1], min_val=NE, max_val=NJ)
            with sp.If(jobs > NE):
                with sp.Fori(NE, jobs) as j:
                    e = sp.value_load(tabi[0:1, bass.ds(j - NE, 1)], min_val=0, max_val=NE - 1)
                    expert_loads(j, e)
            sp.wait_ge(h_ready, 2 * T + 3 * LT)
            sp.dma_start(out[0].rearrange("(t p) d -> p t d", p=P), H[:, CT:T, :]).then_inc(out_written, 16)
            sp.wait_ge(out_written, 16)

        @block.gpsimd
        def _(pool):
            pool.memset(cstat[:, :, :], 0.0).then_inc(zeroed, 1)
            pool.memset(ones[:, :], 1.0).then_inc(zeroed, 1)
            pool.memset(biasr, 0.0).then_inc(zeroed, 1)
            pool.wait_ge(zeroed, 3)
            for l in range(2):
                if l:
                    pool.wait_ge(modr_ready, 9)
                for v in range(2):
                    pool.dma_start(mod_all[v:P:32, 12 * P:24 * P].rearrange("j (u n) -> j u n", u=12),
                                   b_mod[l].rearrange("(u j n) -> j u n", j=4, n=P)).then_inc(bias_in, 16)
            pool.wait_ge(v_full, v0["norm2"] + 4)
            pool.wait_ge(a_full, a0["norm2"] + 4)
            for b in range(2):
                for edge in (0, CTX + 1):
                    pool.memset(raw[:, b, :, edge:edge + 1], 0.0).then_inc(pads_ready, 1)
            pool.wait_ge(da_ready, 1)
            pool.wait_ge(rows_in, 16 * 8)
            pool.wait_ge(h_ready, 2 * T)
            for r in range(2 * LT * SG):
                it, d = r // 2, r % 2
                tt, g = it // SG, it % SG
                if r >= 2:
                    pool.wait_ge(a_full, a0["seg"] + 2 * (r - 2) + 2)
                pool.tensor_tensor(ld[d], (GTm, LTm)[d].unsqueeze(1).to_broadcast([P, HP, P]),
                                   da[:, CT + tt, d * SH + HP * g:d * SH + HP * g + HP].unsqueeze(2).to_broadcast([P, HP, P]),
                                   ALU.mult).then_inc(ld_ready, 1)

        @block.scalar
        def _(act):
            steps = [0]

            def step(ins):
                steps[0] += 1
                ins.then_inc(act_step, 1)
                act.wait_ge(act_step, steps[0])

            act.dma_start(const[:, :], consts).then_inc(rows_in, 16)
            act.dma_start(rows1[0:16, :], norm1_g.rearrange("l (k p) -> (l k) p", p=P)).then_inc(rows_in, 16)
            act.dma_start(rows1[16:32, :], norm2_g.rearrange("l (k p) -> (l k) p", p=P)).then_inc(rows_in, 16)
            act.dma_start(rows1[32:48, :], ssd_norm_g.rearrange("l (k p) -> (l k) p", p=P)).then_inc(rows_in, 16)
            act.dma_start(rows1[48:56, :], c.rearrange("l (k p) -> (l k) p", p=P)).then_inc(rows_in, 16)
            act.dma_start(rows1[56:64, :], c_ctx.rearrange("(k p) -> k p", p=P)).then_inc(rows_in, 16)
            nct = CONV_CH // P
            act.dma_start(rows2[0:3 * nct, :], conv_w[0].rearrange("t (k p) -> (t k) p", p=P)).then_inc(rows_in, 16)
            act.dma_start(rows2[3 * nct:4 * nct, :], conv_b[0].rearrange("(k p) -> k p", p=P)).then_inc(rows_in, 16)
            act.dma_start(H[:, 0:CT, :], ctx_tok[0].rearrange("(t p) d -> p t d", p=P)).then_inc(tokens_in, 16)
            act.dma_start(H[:, CT:T, :], x[0].rearrange("(t p) d -> p t d", p=P)).then_inc(tokens_in, 16)
            for dst, src in ((qg_b[:, :], q_g[0]), (kg_b[:, :], k_g[0]), (dskip_b[:, :], d_skip[0]),
                             (dtb_b[:, 0:SH], dt_bias_f[0]), (dtb_b[:, SH:2 * SH], dt_bias_b[0]),
                             (alog_b[:, 0:SH], a_log_f[0]), (alog_b[:, SH:2 * SH], a_log_b[0])):
                act.dma_start(dst, src.partition_broadcast(P)).then_inc(params_in, 16)
            act.dma_start(rout[:, :, :], router[0].rearrange("(k p) e -> p k e", p=P)).then_inc(params_in, 16)
            act.dma_start(w_dt[:, :, :], ssd_w_in[0][:, INNER + CONV_CH:INNER + CONV_CH + 2 * SH]
                          .rearrange("(k p) e -> p k e", p=P)).then_inc(params_in, 16)

            act.wait_ge(cols_ready, 1)
            act.wait_ge(zeroed, 1)
            nc.scalar.activation(cstat[:, :, 0:2].rearrange("p k v -> p v k"),
                                 cols1[:, 48:64].rearrange("p (v k) -> p v k", v=2), ACT.Silu).then_inc(csil_ready, 1)

            def modb_copies(l):
                stage = "mod1" if l else "mod0t"
                if l:
                    act.wait_ge(h_ready, 2 * T)
                i = 0
                for gate in range(2):
                    for v in range(2 - l):
                        for uu in range(2):
                            g = a0[stage] + i
                            i += 1
                            act.wait_ge(a_full, g + 1)
                            nc.scalar.activation(modb[:, 2 * gate + v, uu * N:uu * N + N], a_bank(g), ACT.Copy)\
                                .then_inc(a_free, 1)

            def norm_act(n):
                l, which = n // 2, n % 2
                tiles = NTILES[n]
                aT = aTs[min(n, 3)]
                if n == 0:
                    act.wait_ge(tokens_in, 32)
                for i, t in enumerate(tiles):
                    if n:
                        act.wait_ge(h_ready, H_DONE[n] + i + 1)
                    nc.scalar.activation(aT_scratch, H[:, t, :], ACT.Square, accum_out=stat[:, t:t + 1]).then_inc(sumsq_ready, 1)
                    act.wait_ge(sumsq_ready, sq_done[n] + i + 1)
                if n == 4:
                    act.wait_ge(meansq_ready, n + 1)
                    nc.scalar.activation(stat[:, 8 + tiles[0]:8 + T], stat[:, 4 + tiles[0]:4 + T], ACT.Sqrt).then_inc(rms_ready, 1)
                    return
                act.wait_ge(meansq_ready, n + 1)
                nc.scalar.activation(stat[:, 8 + tiles[0]:8 + T], stat[:, 4 + tiles[0]:4 + T], ACT.Sqrt).then_inc(rms_ready, 1)
                act.wait_ge(modc_ready, (1, 2, 3, 3)[n])
                for i in range(4):
                    k = 2 * i + 1
                    g = a0[f"norm{n}"] + i
                    act.wait_ge(a_full, g + 1)
                    if tiles[0] == 0:
                        nc.scalar.activation(aT[:, k, 0:CTX], a_bank(g)[:, 0:CTX], ACT.Identity,
                                             scale=gcol[:, which, k, 1:2], bias=modc[:, 24 * which + k, 1:2])
                    nc.scalar.activation(aT[:, k, NTOK - SEQ - aOff[n]:NTOK - aOff[n]], a_bank(g)[:, CTX:NTOK], ACT.Identity,
                                         scale=gcol[:, which, k, 0:1], bias=modc[:, 24 * which + k, 0:1])\
                        .then_inc(a_free, 1)

            aT_scratch = AR[:, 19456:20480]
            norm_act(0)

            for i in range(3 * T):
                t, cc = i // 3, i % 3
                g = a0["qkv"] + i
                act.wait_ge(a_full, g + 1)
                if cc < 2:
                    nc.scalar.activation(qk[:, t, cc * N:cc * N + N], a_bank(g), ACT.Copy).then_inc(a_free, 1)
                else:
                    nc.scalar.activation(qk[:, t, 2 * N:QKW], a_bank(g)[:, 0:QKW - 2 * N], ACT.Copy)
                    nc.scalar.activation(vv[:, t, :], a_bank(g)[:, QKW - 2 * N:N], ACT.Copy).then_inc(a_free, 1)
                if cc == 2:
                    act.wait_ge(qsq_ready, t + 1)
                    nc.scalar.activation(stat[:, 36:46], stat[:, 26:36], ACT.Sqrt).then_inc(qrms_ready, 1)
            for i in range(3 * T):
                t, cc = i // 3, i % 3
                g = a0["qkT"] + i
                act.wait_ge(a_full, g + 1)
                if cc < 2:
                    nc.scalar.activation(qT[:, 4 * cc:4 * cc + 4, t * P:t * P + P],
                                         a_bank(g).rearrange("p (h q) -> p h q", h=4), ACT.Copy).then_inc(a_free, 1)
                else:
                    nc.scalar.activation(kT[:, :, t * P:t * P + P],
                                         a_bank(g)[:, 0:NKV * P].rearrange("p (h q) -> p h q", h=NKV), ACT.Copy)\
                        .then_inc(a_free, 1)
            for kind, m in TSEQ:
                if kind == "S":
                    t, _, _, nk = pair(m)
                    act.wait_ge(nmax_ready, m + 1)
                    if m >= 8:
                        act.wait_ge(p_used, m - 7)
                    nc.scalar.activation(pbuf[:, m % 8, 0:nk * P], a_bank(att_a[kind, m])[:, 0:nk * P], ACT.Exp,
                                         bias=stat[:, 16 + m % 4:17 + m % 4], accum_out=stat[:, 20 + m % 4:21 + m % 4])\
                        .then_inc(p_exp, 1)
                    act.wait_ge(p_exp, m + 1)
                    act.sem_inc(a_free, 1)
                elif kind == "O":
                    t, g = m // NKV, m % NKV
                    act.wait_ge(a_full, att_a[kind, m] + 1)
                    nc.scalar.activation(oT[:, QG * g:QG * g + QG, t * P:t * P + P],
                                         a_bank(att_a[kind, m]).rearrange("p (h q) -> p h q", h=QG), ACT.Copy)\
                        .then_inc(a_free, 1)
            modb_copies(0)
            norm_act(1)
            dve_half = v0["norm1"] + 4
            act.wait_ge(v_free, dve_half)
            act.wait_ge(a_free, a0["norm1"] + 4)
            for q in range(4):
                nc.scalar.activation(a_hi[:, 2 * q:2 * q + 2, :], aT[:, 2 * q:2 * q + 2, :], ACT.Copy).then_inc(ahi_ready, 1)
            act.sem_inc(fa_free, 2)

            def round_weights(v, i):
                act.wait_ge(f_in[v % 3], 16 * (v // 3 + 1) + 32 * i)
                act.wait_ge(*half_used(v - 3, i))
                nc.scalar.activation(f_hi[:, v % 3, :], f_raw[:, v % 3, :], ACT.Copy).then_inc(fhi_ready, 1)

            def gate(ft, i):
                act.wait_ge(fa_full, ft + 1 + 4 * i)
                nc.scalar.activation(hT[:, ft, :], PS[:, 4 + ft % 2, :], ACT.Silu).then_inc(fa_free, 1)

            def round_hidden(ft, i):
                act.wait_ge(v_free, v0["ffn"] + ft + 1 + NFV * i)
                nc.scalar.activation(h_hi[:, ft, :], hT[:, ft, :], ACT.Copy).then_inc(hhi_ready, 1)

            def chunk(i, more):
                round_weights(2, i)
                gate(0, i)
                gate(1, i)
                round_weights(3, i)
                round_hidden(0, i)
                round_weights(4, i)
                gate(2, i)
                round_hidden(1, i)
                gate(3, i)
                round_weights(5, i)
                round_hidden(2, i)
                if more:
                    round_weights(6, i)
                round_hidden(3, i)
                if more:
                    round_weights(7, i)

            round_weights(0, 0)
            round_weights(1, 0)
            with act.Fori(0, FC - 1) as i:
                chunk(i, True)
            chunk(FC - 1, False)
            modb_copies(1)
            norm_act(2)

            act.wait_ge(params_in, 16 * 9)
            nc.scalar.activation(alog_b[:, :], alog_b[:, :], ACT.Exp).then_inc(alog_ready, 1)
            act.wait_ge(sp_in, 1)
            nc.scalar.activation(sp_u, sp_a, ACT.Exp).then_inc(sp_exp, 1)

            def silu_conv(ct):
                act.wait_ge(conv_ready, ct + 1)
                if ct < NXB:
                    if ct >= 2:
                        act.wait_ge(v_full, v0["xbc"] + ct - 1)
                    nc.scalar.activation(convs[:, ct % 2, :], conv[:, ct % 2, :], ACT.Silu).then_inc(convs_ready, 1)
                    if ct >= INNER // P:
                        act.wait_ge(convs_ready, ct + 1)
                        nc.scalar.activation(bT[:, ct - INNER // P, :], convs[:, ct % 2, CTX:NTOK], ACT.Copy).then_inc(bT_ready, 1)
                else:
                    nc.scalar.activation(cT[:, ct - NXB, :], conv[:, ct % 2, CTX:NTOK], ACT.Silu).then_inc(bT_ready, 1)

            act.wait_ge(pads_ready, 4)
            for ct in range(NCT):
                g = a0["xbc"] + ct
                if ct >= 1:
                    silu_conv(ct - 1)
                act.wait_ge(a_full, g + 1)
                if ct >= 2:
                    act.wait_ge(conv_ready, ct - 1)
                if ct < NXB:
                    ins = nc.scalar.activation(raw[:, ct % 2, :, 1:CTX + 1],
                                               a_bank(g).rearrange("p (s n) -> p s n", s=2), ACT.Copy)
                else:
                    ins = nc.scalar.activation(raw[:, ct % 2, 1, 1:CTX + 1], a_bank(g)[:, CTX:NTOK], ACT.Copy)
                ins.then_inc(a_free, 1)
            silu_conv(NCT - 1)
            g = a0["dec"]
            act.wait_ge(a_full, g + 1)
            nc.scalar.activation(ex[:, :], a_bank(g)[:, 0:384], ACT.Exp).then_inc(a_free, 1)
            for i in range(LT * INNER // N):
                u, tt = i // LT, i % LT
                g = a0["z"] + i
                act.wait_ge(a_full, g + 1)
                nc.scalar.activation(zs[:, tt, u * N:u * N + N], a_bank(g), ACT.Silu).then_inc(a_free, 1)
            for i in range(2 * SG):
                d, gg = i // SG, i % SG
                g = a0["st"] + i
                act.wait_ge(a_full, g + 1)
                nc.scalar.activation(hs[d][0][:, gg * N:gg * N + N], a_bank(g), ACT.Copy).then_inc(a_free, 1)
            for i in range(4 * LT * SG):
                it, d, hf = i // 4, i // 2 % 2, i % 2
                g = a0["seg"] + i
                act.wait_ge(a_full, g + 1)
                if it >= 2:
                    act.wait_ge(v_full, v0["ydiag"] + it - 1)
                nc.scalar.activation(mm[it % 2][:, d, 4 * hf:4 * hf + 4, :], a_bank(g).rearrange("p (h l) -> p h l", h=4),
                                     ACT.Exp).then_inc(a_free, 1)
            for tt in range(LT):
                act.wait_ge(y_sum, tt + 1)
                for gg in range(SG):
                    step(nc.scalar.activation(AR[:, 16384:16384 + N], yacc[:, tt, gg * N:gg * N + N], ACT.Square,
                                              accum_out=stat[:, SG * tt + gg:SG * tt + gg + 1]))
                act.sem_inc(y_sq, 1)
                act.wait_ge(y_ms, tt + 1)
                nc.scalar.activation(stat[:, 16 + SG * tt:16 + SG * tt + SG], stat[:, 8 + SG * tt:8 + SG * tt + SG], ACT.Sqrt)\
                    .then_inc(y_rms, 1)
            norm_act(3)
            act.wait_ge(mask_ready, 1)
            act.dma_start(fin_g, final_g.partition_broadcast(P)).then_inc(fin_in, 16)
            act.wait_ge(gap_ready, 1)
            nc.scalar.activation(tabf[:, 2:4], tabf[:, 0:2], ACT.Exp).then_inc(gap_exp, 1)
            act.wait_ge(tables_ready, 1)
            last_job = act.value_load(tabi[0:1, EXTRA + 1:EXTRA + 2], min_val=NE - 1, max_val=NJ - 1)
            def round_half(v, j):
                act.wait_ge(moe_in[v % RS], 16 * (v // RS + 1) + 16 * (NHU // RS) * j)
                act.wait_ge(moe_free, v - HS_ + 1 + RS + NHU * j)
                nc.scalar.activation(m_hi[:, v % HS_, :], m_raw[:, v % RS, :], ACT.Copy).then_inc(moe_hi, 1)

            def fetch(i, bank, g):
                act.wait_ge(ma_full, g)
                for k4 in range(4):
                    k = 4 * i + k4
                    ins = nc.scalar.activation(xe[:, k, :], bank[:, k4 * P:k4 * P + P], ACT.Identity,
                                               scale=gcol[:, 1, k, 0:1], bias=modc[:, 24 + k, 0:1])
                ins.then_inc(ma_free, 1)

            def round_tokens(free, n):
                act.wait_ge(ma_free, free)
                nc.scalar.activation(xe_hi[:, :, :], xe, ACT.Copy).then_inc(xhi_ready, 1)

            act.sem_inc(ma_free, 2)
            for v in range(LEAD):
                round_half(v, 0)
            for i in range(2):
                fetch(i, PS[:, 3 + i, :], i + 1)
            round_tokens(4, 1)

            def job(j, more):
                for it in MSEQ:
                    kind, cc = it
                    if kind in "GUD":
                        for half in range(2):
                            v = 2 * m_u[it] + half + LEAD
                            if v < NHU or more:
                                round_half(v, j)
                    if kind in "GP":
                        act.wait_ge(ma_full, m_a[it] + 3 + NMA * j)
                    if kind == "X" and more:
                        if cc == 0:
                            act.wait_ge(xlo_ready, 1 + j)
                        fetch(cc, ma_bank(it), m_a[it] + 3 + NMA * j)
                        if cc == 1:
                            round_tokens(m_a[it] + 1 + 2 + 2 + NMA * j, j)
                    elif kind == "G":
                        if cc >= 2:
                            act.wait_ge(mv_free, m_v["U", cc - 2] + 1 + 3 + NMV * j)
                        nc.scalar.activation(sgm[:, cc % 2, :], ma_bank(it), ACT.Silu).then_inc(ma_free, 1)
                    elif kind == "P":
                        nc.scalar.activation(permT, ma_bank(it)[:, 0:LT * P], ACT.Copy).then_inc(ma_free, 1)
                    elif kind == "T":
                        act.wait_ge(mv_full, m_v[it] + 1 + NMV * j)
                        nc.scalar.activation(hT_hi[:, cc % 3, :, :], mv_bank(it).rearrange("p (k s) -> p k s", k=4),
                                             ACT.Copy).then_inc(th_ready, 1)
                act.wait_ge(down_full, 1 + j)
                for hf in range(2):
                    nc.scalar.activation(ye[:, hf * N:hf * N + N], PS[:, 6 + hf, :], ACT.Copy).then_inc(ye_ready, 1)

            with act.Fori(0, last_job) as j:
                job(j, True)
            job(last_job, False)
            norm_act(4)

        @block.vector
        def _(dve):
            steps = [0]

            def step(ins):
                steps[0] += 1
                ins.then_inc(dve_step, 1)
                dve.wait_ge(dve_step, steps[0])

            dve.wait_ge(v_full, v0["prep"] + 1)
            step(nc.vector.tensor_copy(cols1[:, :], v_bank(v0["prep"])[:, 0:64]))
            nr = 4 * CONV_CH // P
            nc.vector.tensor_copy(cols2[:, :], v_bank(v0["prep"])[:, 64:64 + nr]).then_inc(v_free, 1)
            dve.wait_ge(v_free, 1)
            dve.sem_inc(cols_ready, 1)

            def mod_columns(l, b, g):
                dve.wait_ge(v_full, g + 1)
                nc.vector.tensor_copy(modc[:, 16 * b:16 * b + 16, :],
                                      v_bank(g).rearrange("p (c v) -> p c v", v=32)[:, :, 0:2]).then_inc(v_free, 1)
                dve.wait_ge(v_free, g + 1)

            def norm_gain(l, which):
                gain = cols1[:, 16 * which + 8 * l:16 * which + 8 * l + 8]
                step(nc.vector.scalar_tensor_tensor(
                    out=gcol[:, which, :, :], in0=modc[:, 24 * which + 8:24 * which + 16, :], scalar=1.0,
                    in1=gain.unsqueeze(2).to_broadcast([P, KD, 2]), op0=ALU.add, op1=ALU.mult))

            def norm_dve(n):
                l, which = n // 2, n % 2
                tiles = NTILES[n]
                aT = aTs[min(n, 3)]
                dve.wait_ge(sumsq_ready, sq_done[n] + len(tiles))
                step(nc.vector.tensor_scalar(stat[:, 4 + tiles[0]:4 + T], stat[:, tiles[0]:T], 1.0 / D, EPS, ALU.mult, ALU.add))
                dve.sem_inc(meansq_ready, 1)
                dve.wait_ge(rms_ready, n + 1)
                step(nc.vector.reciprocal(stat[:, 12 + tiles[0]:12 + T], stat[:, 8 + tiles[0]:8 + T]))
                if n == 4:
                    return
                for t in tiles:
                    dst = xn[:, t, :] if n < 3 else y2[:, t - CT, :]
                    nc.vector.tensor_scalar(dst, H[:, t, :], stat[:, 12 + t:13 + t], None, ALU.mult).then_inc(xn_ready, 1)
                for i in range(4):
                    k = 2 * i
                    g = v0[f"norm{n}"] + i
                    dve.wait_ge(v_full, g + 1)
                    if tiles[0] == 0:
                        nc.vector.tensor_scalar(aT[:, k, 0:CTX], v_bank(g)[:, 0:CTX], gcol[:, which, k, 1:2],
                                                modc[:, 24 * which + k, 1:2], ALU.mult, ALU.add)
                    nc.vector.tensor_scalar(aT[:, k, NTOK - SEQ - aOff[n]:NTOK - aOff[n]], v_bank(g)[:, CTX:NTOK], gcol[:, which, k, 0:1],
                                            modc[:, 24 * which + k, 0:1], ALU.mult, ALU.add).then_inc(v_free, 1)

            dve.wait_ge(bias_in, 32)
            g = v0["mod0"]
            dve.wait_ge(v_full, g + 1)
            nc.vector.tensor_tensor(modr[:, 0:4, :], v_bank(g).rearrange("p (u n) -> p u n", u=4), biasr[:, 0:4, :],
                                    ALU.add).then_inc(v_free, 1)
            dve.wait_ge(v_free, g + 1)
            dve.sem_inc(modr_ready, 1)
            mod_columns(0, 0, g + 1)
            norm_gain(0, 0)
            dve.sem_inc(modc_ready, 1)
            dve.wait_ge(tokens_in, 32)
            norm_dve(0)
            dve.wait_ge(params_in, 16 * 9)
            step(nc.vector.tensor_scalar(qg_b[:, :], qg_b[:, :], float(HD) ** -0.5, None, ALU.mult))
            for t in range(T):
                dve.wait_ge(a_free, a0["qkv"] + 3 * t + 3)
                q3 = qk[:, t, :].rearrange("p (h d) -> p h d", d=HD)
                step(nc.vector.tensor_tensor(sq_t, q3, q3, ALU.mult))
                step(nc.vector.tensor_reduce(stat[:, 46:56], sq_t, AX.X, ALU.add))
                step(nc.vector.tensor_scalar(stat[:, 26:36], stat[:, 46:56], 1.0 / HD, EPS, ALU.mult, ALU.add))
                dve.sem_inc(qsq_ready, 1)
                dve.wait_ge(qrms_ready, t + 1)
                step(nc.vector.reciprocal(stat[:, 46:56], stat[:, 36:46]))
                step(nc.vector.tensor_tensor(q3, q3, stat[:, 46:56].unsqueeze(2).to_broadcast([P, 10, HD]), ALU.mult))
                nc.vector.tensor_tensor(q3[:, NH:10, :], q3[:, NH:10, :],
                                        kg_b[:, :].unsqueeze(1).to_broadcast([P, NKV, HD]), ALU.mult)
                step(nc.vector.tensor_tensor(q3[:, 0:NH, :], q3[:, 0:NH, :],
                                             qg_b[:, :].unsqueeze(1).to_broadcast([P, NH, HD]), ALU.mult))
                if t >= CT:
                    tt = t - CT
                    half = HD // 4
                    q5 = qk[:, t, :].rearrange("p (h a b i) -> p h a b i", a=2, b=2, i=half)
                    r5 = rope_t.rearrange("p h (a b i) -> p h a b i", a=2, b=2, i=half)
                    s4 = rope_s[:, tt, :].rearrange("p (a b i) -> p a b i", a=2, b=2)
                    for b in range(2):
                        for a in range(2):
                            last = nc.vector.tensor_tensor(
                                r5[:, :, a, b, :], q5[:, :, a, 1 - b, :],
                                s4[:, a, b, :].unsqueeze(1).to_broadcast([P, 10, half]), ALU.mult)
                    step(last)
                    step(nc.vector.tensor_tensor(q3, q3, rope_c[:, tt, :].unsqueeze(1).to_broadcast([P, 10, HD]), ALU.mult))
                    step(nc.vector.tensor_tensor(q3, q3, rope_t, ALU.add))
                dve.sem_inc(qk_ready, 1)

            def normalise(m):
                dve.wait_ge(p_exp, m + 1)
                nk = pair(m)[3]
                step(nc.vector.reciprocal(stat[:, 56 + m % 4:57 + m % 4], stat[:, 20 + m % 4:21 + m % 4]))
                nc.vector.tensor_scalar(pbuf[:, m % 8, 0:nk * P], pbuf[:, m % 8, 0:nk * P],
                                        stat[:, 56 + m % 4:57 + m % 4], None, ALU.mult).then_inc(p_norm, 1)

            for kind, m in TSEQ:
                if kind == "S":
                    if m >= 3:
                        normalise(m - 3)
                    nk = pair(m)[3]
                    dve.wait_ge(a_full, att_a[kind, m] + 1)
                    nc.vector.tensor_reduce(stat[:, 16 + m % 4:17 + m % 4], a_bank(att_a[kind, m])[:, 0:nk * P],
                                            AX.X, ALU.max, negate=True).then_inc(nmax_ready, 1)
                elif kind == "M":
                    dve.wait_ge(v_full, att_v[kind, m] + 1)
                    nc.vector.tensor_tensor(modr[:, m, :], v_bank(att_v[kind, m])[:, 0:P], biasr[:, m, :], ALU.add)\
                        .then_inc(v_free, 1)
                    dve.wait_ge(v_free, att_v[kind, m] + 1)
                    dve.sem_inc(modr_ready, 1)
                elif kind == "T":
                    if m >= NPAIR - 3:
                        normalise(m)
                    nk = pair(m)[3]
                    b, hh = m // QG, m % QG
                    dve.wait_ge(v_full, att_v[kind, m] + 1)
                    if b >= 2:
                        dve.wait_ge(a_full, att_a["O", b - 2] + 1)
                    nc.vector.tensor_copy(pT[:, b % 2, 0:nk, hh * P:hh * P + P],
                                          v_bank(att_v[kind, m])[:, 0:nk * P].rearrange("p (k q) -> p k q", k=nk))\
                        .then_inc(v_free, 1)

            def residual(g, t, hf, gate, at=0):
                v = 1 if t < CT else 0
                tmp = AR[:, at:at + N] if g % 2 else AR[:, at + N:at + 2 * N]
                dve.wait_ge(v_full, g + 1)
                nc.vector.tensor_tensor(tmp, v_bank(g), modb[:, 2 * gate + v, hf * N:hf * N + N], ALU.mult).then_inc(v_free, 1)
                dve.wait_ge(v_free, g + 1)
                return nc.vector.tensor_tensor(H[:, t, hf * N:hf * N + N], H[:, t, hf * N:hf * N + N], tmp, ALU.add)

            for b in range(2):
                mod_columns(0, 1 + b, v0["mod0t"] + b)
            norm_gain(0, 1)
            dve.sem_inc(modc_ready, 1)
            dve.wait_ge(a_free, a0["mod0t"] + 8)
            for i in range(2 * T):
                t, hf = i // 2, i % 2
                ins = residual(v0["wo"] + i, t, hf, 0)
                if hf:
                    ins.then_inc(h_ready, 1)
            dve.wait_ge(h_ready, T)
            norm_dve(1)
            step(nc.vector.memset(facc, 0.0))
            for q in range(4):
                dve.wait_ge(ahi_ready, q + 1)
                nc.vector.tensor_tensor(a_lo[:, 2 * q:2 * q + 2, :], aT[:, 2 * q:2 * q + 2, :],
                                        a_hi[:, 2 * q:2 * q + 2, :].bitcast(F32), ALU.subtract).then_inc(alo_ready, 1)

            def rest_weights(v, i):
                dve.wait_ge(fhi_ready, v + 1 + NFH * i)
                nc.vector.tensor_tensor(f_lo[:, v % 3, :], f_raw[:, v % 3, :], f_hi[:, v % 3, :].bitcast(F32), ALU.subtract)\
                    .then_inc(flo_ready, 1)

            def hidden(ft, i):
                g = v0["ffn"] + ft
                dve.wait_ge(fa_free, 2 + ft + 1 + 4 * i)
                dve.wait_ge(v_full, g + 1 + NFV * i)
                nc.vector.tensor_tensor(hT[:, ft, :], hT[:, ft, :], v_bank(g), ALU.mult).then_inc(v_free, 1)

            def rest_hidden(ft, i):
                dve.wait_ge(hhi_ready, ft + 1 + 4 * i)
                nc.vector.tensor_tensor(h_lo[:, ft, :], hT[:, ft, :], h_hi[:, ft, :].bitcast(F32), ALU.subtract).then_inc(hlo_ready, 1)

            def add_down(half, i):
                for j in range(2 * T):
                    t, hf = j // 2, j % 2
                    g = v0["ffn"] + 4 + 2 * T * half + j
                    dve.wait_ge(v_full, g + 1 + NFV * i)
                    f = facc[:, t, hf * N:hf * N + N]
                    nc.vector.tensor_tensor(f, f, v_bank(g), ALU.add).then_inc(v_free, 1)

            def chunk(i, more):
                rest_weights(2, i)
                hidden(0, i)
                hidden(1, i)
                rest_weights(3, i)
                rest_hidden(0, i)
                rest_weights(4, i)
                hidden(2, i)
                rest_hidden(1, i)
                hidden(3, i)
                rest_weights(5, i)
                rest_hidden(2, i)
                if more:
                    rest_weights(6, i)
                rest_hidden(3, i)
                if more:
                    dve.wait_ge(modu_used, 3 + 2 * i)
                    nc.vector.tensor_tensor(modr[:, bass.ds(2 * i, 2), :], PS[:, 6, 0:2 * P].rearrange("p (u n) -> p u n", u=2),
                                            biasr[:, bass.ds(2 * i, 2), :], ALU.add).then_inc(modu_added, 1)
                add_down(0, i)
                if more:
                    rest_weights(7, i)
                add_down(1, i)

            dve.wait_ge(bias_in, 64)
            rest_weights(0, 0)
            rest_weights(1, 0)
            with dve.Fori(0, FC - 1) as i:
                chunk(i, True)
            chunk(FC - 1, False)
            dve.wait_ge(v_free, v0["ffn"] + NFV * FC)
            for t in range(T):
                v = 1 if t < CT else 0
                step(nc.vector.tensor_tensor(facc[:, t, :], facc[:, t, :], modb[:, 2 + v, :], ALU.mult))
                nc.vector.tensor_tensor(H[:, t, :], H[:, t, :], facc[:, t, :], ALU.add).then_inc(h_ready, 1)
            for b in range(3):
                mod_columns(1, b, v0["mod1"] + b)
            norm_gain(1, 0)
            norm_gain(1, 1)
            dve.sem_inc(modc_ready, 1)
            norm_dve(2)

            g = v0["dt"]
            dve.wait_ge(v_full, g + 1)
            nc.vector.tensor_tensor(dt_[:, :, :], v_bank(g)[:, 0:T * 2 * SH].rearrange("p (t h) -> p t h", t=T),
                                    dtb_b[:, :].unsqueeze(1).to_broadcast([P, T, 2 * SH]), ALU.add).then_inc(v_free, 1)
            dve.wait_ge(v_free, g + 1)
            dtf = dt_[:, :, :].rearrange("p t h -> p (t h)")
            nc.vector.scalar_tensor_tensor(out=sp_a, in0=dtf, scalar=-1.0, in1=dtf, op0=ALU.mult, op1=ALU.min).then_inc(sp_in, 1)
            dve.wait_ge(sp_exp, 1)
            step(nc.vector.tensor_scalar(sp_a, sp_u, 2.0, None, ALU.add))
            step(nc.vector.reciprocal(sp_a, sp_a))
            step(nc.vector.tensor_tensor(sp_u, sp_u, sp_a, ALU.mult))
            step(nc.vector.tensor_tensor(sp_a, sp_u, sp_u, ALU.mult))
            step(nc.vector.tensor_scalar(sp_s, sp_a, 1.0 / 17.0, None, ALU.mult))
            for k in range(7, 0, -1):
                step(nc.vector.scalar_tensor_tensor(out=sp_s, in0=sp_s, scalar=1.0 / (2 * k + 1), in1=sp_a,
                                                    op0=ALU.add, op1=ALU.mult))
            step(nc.vector.scalar_tensor_tensor(out=sp_s, in0=sp_s, scalar=1.0, in1=sp_u, op0=ALU.add, op1=ALU.mult))
            step(nc.vector.tensor_scalar(sp_a, dtf, 0.0, None, ALU.max))
            step(nc.vector.scalar_tensor_tensor(out=dtf, in0=sp_s, scalar=2.0, in1=sp_a, op0=ALU.mult, op1=ALU.add))
            dve.wait_ge(alog_ready, 1)
            nc.vector.scalar_tensor_tensor(out=da[:, :, :], in0=dt_[:, :, :], scalar=-1.0,
                                           in1=alog_b[:, :].unsqueeze(1).to_broadcast([P, T, 2 * SH]),
                                           op0=ALU.mult, op1=ALU.mult).then_inc(da_ready, 1)

            def channels_out(ct):
                g = v0["xbc"] + ct
                dve.wait_ge(v_full, g + 1)
                dst = xt[:, :, ct * P:ct * P + P] if ct < INNER // P else btok[:, :, ct * P - INNER:ct * P - INNER + P]
                nc.vector.tensor_copy(dst, v_bank(g).rearrange("p (t c) -> p t c", t=T)).then_inc(v_free, 1)

            for ct in range(NCT):
                dve.wait_ge(a_free, a0["xbc"] + ct + 1)
                if 1 <= ct <= NXB:
                    if ct >= 2:
                        dve.wait_ge(convs_ready, ct - 1)
                elif ct > NXB + 1:
                    dve.wait_ge(bT_ready, ct - 1 - INNER // P)
                lo = 0 if ct < NXB else 1
                dst = conv[:, ct % 2, :].rearrange("p (s n) -> p s n", s=2)[:, lo:, :]
                src = raw[:, ct % 2, lo:, :]

                def w_col(k):
                    return cols2[:, k * NCT + ct:k * NCT + ct + 1]
                step(nc.vector.tensor_scalar(dst, src[:, :, 0:CTX], w_col(0), w_col(3), ALU.mult, ALU.add))
                step(nc.vector.scalar_tensor_tensor(out=dst, in0=src[:, :, 1:CTX + 1], scalar=w_col(1), in1=dst,
                                                    op0=ALU.mult, op1=ALU.add))
                nc.vector.scalar_tensor_tensor(out=dst, in0=src[:, :, 2:CTX + 2], scalar=w_col(2), in1=dst,
                                               op0=ALU.mult, op1=ALU.add).then_inc(conv_ready, 1)
                if 1 <= ct <= NXB:
                    channels_out(ct - 1)
            dve.wait_ge(a_free, a0["dec"] + 1)
            step(nc.vector.tensor_tensor(wsc[:, 0:128], ex[:, 128:256], dt_[:, 0:CT, :].rearrange("p t h -> p (t h)"), ALU.mult))
            step(nc.vector.tensor_tensor(wsc[:, 128:160], ex[:, 256:288], dt_[:, CT, 0:SH], ALU.mult))
            step(nc.vector.tensor_tensor(wsc[:, 160:192], ex[:, 288:320], dt_[:, CT + 1, SH:2 * SH], ALU.mult))

            def by_head(v):
                return v.unsqueeze(2).to_broadcast([P, v.shape[1], HDIM])

            def heads(v):
                return v.rearrange("p (h d) -> p h d", d=HDIM)

            def weigh(q):
                d = (0, 0, 1, 1, 0, 1)[q]
                t = (0, 1, 0, 1, CT, CT + 1)[q]
                w = wsc[:, 64 * t + SH * d:64 * t + SH * d + SH] if q < 4 else wsc[:, 32 * q:32 * q + SH]
                if q in (2, 4):
                    dve.wait_ge(xw_used, q // 2)
                if q in (3, 5):
                    dve.wait_ge(a_full, a0["st"] + SG * (q // 2))
                nc.vector.tensor_tensor(heads(xw[:, q % 2, :]), heads(xt[:, t, :]), by_head(w), ALU.mult).then_inc(xw_ready, 1)

            dve.wait_ge(bT_ready, 2 * SG)
            for q in range(2):
                weigh(q)
            for tt in range(LT):
                g = v0["cb"] + tt
                dve.wait_ge(v_full, g + 1)
                for d in range(2):
                    ins = nc.vector.tensor_tensor(cbm[:, d, tt, :, :], v_bank(g).rearrange("p (g l) -> p g l", g=SG),
                                                  (LE, GE)[d].unsqueeze(1).to_broadcast([P, SG, P]), ALU.mult)
                ins.then_inc(v_free, 1)
            for q in range(2, 6):
                weigh(q)
            dve.wait_ge(a_free, a0["st"] + 2 * SG)
            for d in range(2):
                step(nc.vector.tensor_tensor(heads(hs[d][1]), heads(hs[d][0]), by_head(ex[:, 320 + SH * d:320 + SH * d + SH]), ALU.mult))
                for gg in range(SG):
                    g = v0["st2"] + SG * d + gg
                    dve.wait_ge(v_full, g + 1)
                    part = hs[d][1][:, gg * N:gg * N + N]
                    nc.vector.tensor_tensor(part, part, v_bank(g), ALU.add).then_inc(v_free, 1)
            for i in range(2 * LT * SG):
                tt, gg, d = i // (2 * SG), i // 2 % SG, i % 2
                g = v0["yoff"] + i
                dve.wait_ge(v_full, g + 1)
                dst = yacc[:, tt, gg * N:gg * N + N]
                e1 = by_head(ex[:, 64 * tt + SH * d + HP * gg:64 * tt + SH * d + HP * gg + HP])
                if d == 0:
                    nc.vector.tensor_tensor(heads(dst), heads(v_bank(g)), e1, ALU.mult).then_inc(v_free, 1)
                else:
                    tmp = yoff_t[:, gg % 2, :]
                    nc.vector.tensor_tensor(heads(tmp), heads(v_bank(g)), e1, ALU.mult).then_inc(v_free, 1)
                    dve.wait_ge(v_free, g + 1)
                    step(nc.vector.tensor_tensor(dst, dst, tmp, ALU.add))

            def x_dt(tt):
                for d in range(2):
                    step(nc.vector.tensor_tensor(heads(xdt[tt][:, d, :]), heads(xt[:, CT + tt, :]),
                                                 by_head(dt_[:, CT + tt, SH * d:SH * d + SH]), ALU.mult))
            x_dt(0)
            x_dt(1)

            def y_diag(it):
                tt, gg = it // SG, it % SG
                g = v0["ydiag"] + it
                dve.wait_ge(v_full, g + 1)
                part = yacc[:, tt, gg * N:gg * N + N]
                nc.vector.tensor_tensor(part, part, v_bank(g), ALU.add).then_inc(v_free, 1)

            for it in range(LT * SG):
                tt, gg = it // SG, it % SG
                for d in range(2):
                    dve.wait_ge(a_free, a0["seg"] + 4 * it + 2 * d + 2)
                    m_ = mm[it % 2][:, d, :, :]
                    nc.vector.tensor_tensor(m_, m_, cbm[:, d, tt, gg, :].unsqueeze(1).to_broadcast([P, HP, P]), ALU.mult)\
                        .then_inc(m_ready, 1)
                if it >= 1:
                    y_diag(it - 1)
            y_diag(LT * SG - 1)
            dve.wait_ge(v_free, v0["ydiag"] + LT * SG)
            for tt in range(LT):
                step(nc.vector.tensor_tensor(heads(xt[:, CT + tt, :]), heads(xt[:, CT + tt, :]), by_head(dskip_b[:, :]), ALU.mult))
                step(nc.vector.tensor_tensor(yacc[:, tt, :], yacc[:, tt, :], xt[:, CT + tt, :], ALU.add))
                nc.vector.tensor_tensor(yacc[:, tt, :], yacc[:, tt, :], zs[:, tt, :], ALU.mult).then_inc(y_sum, 1)
            for tt in range(LT):
                dve.wait_ge(y_sq, tt + 1)
                s = SG * tt
                step(nc.vector.tensor_scalar(stat[:, 8 + s:8 + s + SG], stat[:, s:s + SG], 1.0 * SG / INNER, EPS, ALU.mult, ALU.add))
                dve.sem_inc(y_ms, 1)
                dve.wait_ge(y_rms, tt + 1)
                step(nc.vector.reciprocal(stat[:, 24 + s:24 + s + SG], stat[:, 16 + s:16 + s + SG]))
                for gg in range(SG):
                    part = yacc[:, tt, gg * N:gg * N + N]
                    nc.vector.tensor_scalar(part, part, stat[:, 24 + s + gg:25 + s + gg], None, ALU.mult).then_inc(yn_ready, 1)
                for q in range(INNER // N):
                    g = v0["gT"] + tt * (INNER // N) + q
                    dve.wait_ge(v_full, g + 1)
                    nc.vector.tensor_tensor(gT[:, 4 * q:4 * q + 4, tt * P:tt * P + P], v_bank(g).rearrange("p (k l) -> p k l", k=4),
                                            cols1[:, 32 + 4 * q:36 + 4 * q].unsqueeze(2).to_broadcast([P, 4, P]),
                                            ALU.mult).then_inc(v_free, 1)
            dve.wait_ge(a_free, a0["mod1"] + 4)
            for i in range(2 * LT):
                tt, hf = i // 2, i % 2
                ins = residual(v0["sout"] + i, CT + tt, hf, 0, 16384)
                if hf:
                    ins.then_inc(h_ready, 1)
            dve.wait_ge(h_ready, 2 * T + LT)
            norm_dve(3)

            g = v0["route"]
            dve.wait_ge(v_full, g + 1)

            def rts(i, n=2):
                return rt[:, i:i + n, :]
            lg, eq, oh1, lg2, oh2, mask, gate, rank, r1 = (rts(2 * i) for i in range(9))
            cnt, over, cum, sel, tmp1 = (rt[:, 18 + i, :] for i in range(5))
            rev = rev_e.unsqueeze(1).to_broadcast([P, LT, NE])

            def wide(v):
                return v.unsqueeze(2).to_broadcast([P, LT, NE])
            top = tabf[:, 4:6]
            nc.vector.tensor_copy(lg, v_bank(g)[:, 0:LT * NE].rearrange("p (t e) -> p t e", t=LT)).then_inc(v_free, 1)
            dve.wait_ge(v_free, g + 1)

            def largest(x_, value, onehot):
                step(nc.vector.tensor_reduce(value, x_, AX.X, ALU.max))
                step(nc.vector.tensor_tensor(eq, x_, wide(value), ALU.is_equal))
                step(nc.vector.tensor_tensor(eq, eq, rev, ALU.mult))
                step(nc.vector.tensor_reduce(tabf[:, 6:8], eq, AX.X, ALU.max))
                step(nc.vector.tensor_tensor(onehot, eq, wide(tabf[:, 6:8]), ALU.is_equal))
            largest(lg, top, oh1)
            step(nc.vector.scalar_tensor_tensor(out=lg2, in0=oh1, scalar=-3.0e38, in1=lg, op0=ALU.mult, op1=ALU.add))
            largest(lg2, tabf[:, 2:4], oh2)
            step(nc.vector.tensor_tensor(mask, oh1, oh2, ALU.add))
            dve.sem_inc(mask_ready, 1)
            nc.vector.tensor_tensor(tabf[:, 0:2], tabf[:, 2:4], top, ALU.subtract).then_inc(gap_ready, 1)
            dve.wait_ge(gap_exp, 1)
            step(nc.vector.tensor_scalar(tabf[:, 0:2], tabf[:, 2:4], 1.0, None, ALU.add))
            step(nc.vector.reciprocal(tabf[:, 0:2], tabf[:, 0:2]))
            step(nc.vector.tensor_tensor(tabf[:, 2:4], tabf[:, 2:4], tabf[:, 0:2], ALU.mult))
            step(nc.vector.tensor_tensor(oh1, oh1, wide(tabf[:, 0:2]), ALU.mult))
            step(nc.vector.tensor_tensor(oh2, oh2, wide(tabf[:, 2:4]), ALU.mult))
            step(nc.vector.tensor_tensor(gate, oh1, oh2, ALU.add))
            g = v0["route"] + 1
            dve.wait_ge(v_full, g + 1)
            step(nc.vector.tensor_scalar(rank, v_bank(g)[:, 0:LT * NE].rearrange("p (t e) -> p t e", t=LT), 1.0, None, ALU.add))
            nc.vector.tensor_copy(cnt, v_bank(g)[:, LT * NE:LT * NE + NE]).then_inc(v_free, 1)
            dve.wait_ge(v_free, g + 1)
            step(nc.vector.tensor_tensor(rankj[:, :, 0:NE], rank, mask, ALU.mult))
            step(nc.vector.tensor_copy(gatej[:, :, 0:NE], gate))
            step(nc.vector.tensor_scalar(over, cnt, float(P), None, ALU.is_gt))
            step(nc.vector.tensor_copy(cum, over))
            for e in range(1, NE):
                step(nc.vector.tensor_tensor(cum[:, e:e + 1], cum[:, e:e + 1], cum[:, e - 1:e], ALU.add))
            for m in range(EXTRA):
                step(nc.vector.scalar_tensor_tensor(out=sel, in0=cum, scalar=float(m + 1), in1=over, op0=ALU.is_equal, op1=ALU.mult))
                step(nc.vector.tensor_tensor(tmp1, sel, fwd_e, ALU.mult))
                step(nc.vector.tensor_reduce(tabf[:, m:m + 1], tmp1, AX.X, ALU.add))
                for src, dst in ((rankj, rankj), (gatej, gatej)):
                    step(nc.vector.tensor_tensor(r1, src[:, :, 0:NE], sel.unsqueeze(1).to_broadcast([P, LT, NE]), ALU.mult))
                    step(nc.vector.tensor_reduce(dst[:, :, NE + m:NE + m + 1], r1, AX.X, ALU.add))
                step(nc.vector.tensor_scalar(rankj[:, :, NE + m:NE + m + 1], rankj[:, :, NE + m:NE + m + 1], float(-P), None, ALU.add))
            step(nc.vector.tensor_scalar(tabf[:, EXTRA:EXTRA + 1], cum[:, NE - 1:NE], float(NE), None, ALU.add))
            step(nc.vector.tensor_scalar(tabf[:, EXTRA + 1:EXTRA + 2], cum[:, NE - 1:NE], float(NE - 1), None, ALU.add))
            step(nc.vector.tensor_copy(tabi[:, 0:EXTRA + 2], tabf[:, 0:EXTRA + 2]))
            step(nc.vector.memset(macc, 0.0))
            step(nc.vector.memset(permT, 0.0))
            step(nc.vector.memset(ye, 0.0))
            dve.sem_inc(ye_ready, 2)
            dve.sem_inc(tables_ready, 1)

            def rest_half(v, j):
                dve.wait_ge(moe_hi, v + 1 + NHU * j)
                nc.vector.tensor_tensor(m_lo[:, v % RS, :], m_raw[:, v % RS, :], m_hi[:, v % HS_, :].bitcast(F32), ALU.subtract)\
                    .then_inc(moe_lo, 1)

            def find_tokens(j):
                for tt in range(LT):
                    nc.vector.tensor_scalar(perm[:, tt, :], iota1, rankj[:, tt, bass.ds(j, 1)], None, ALU.is_equal)\
                        .then_inc(perm_ready, 1)

            def rest_tokens(j):
                dve.wait_ge(xhi_ready, j + 1)
                nc.vector.tensor_tensor(xe_lo[:, :, :], xe, xe_hi[:, :, :].bitcast(F32), ALU.subtract).then_inc(xlo_ready, 1)

            def give_back(cc, bank, g):
                dve.wait_ge(mv_full, g)
                part = macc[:, cc // 2, (cc % 2) * N:(cc % 2) * N + N]
                nc.vector.tensor_tensor(part, part, bank, ALU.add).then_inc(mv_free, 1)

            dve.sem_inc(mv_free, 3)
            find_tokens(0)
            for v in range(LEAD):
                rest_half(v, 0)
            rest_tokens(0)

            def job(j, more):
                for tt in range(LT):
                    nc.vector.tensor_scalar(permg[:, tt, :], iota1, rankj[:, tt, bass.ds(j, 1)], gatej[:, tt, bass.ds(j, 1)],
                                            ALU.is_equal, ALU.mult).then_inc(permg_ready, 1)
                if more:
                    find_tokens(j + 1)
                for it in MSEQ:
                    kind, cc = it
                    if kind in "GUD":
                        for half in range(2):
                            v = 2 * m_u[it] + half + LEAD
                            if v < NHU or more:
                                rest_half(v, j)
                    if kind == "U":
                        dve.wait_ge(ma_free, m_a["G", cc] + 1 + 2 + 2 + NMA * j)
                        dve.wait_ge(mv_full, m_v[it] + 1 + NMV * j)
                        nc.vector.tensor_tensor(hm[:, cc % 2, :], sgm[:, cc % 2, :], mv_bank(it), ALU.mult).then_inc(mv_free, 1)
                    elif kind == "T":
                        dve.wait_ge(th_ready, cc + 1 + FC * j)
                        nc.vector.tensor_tensor(hT_lo[:, cc % 3, :, :], mv_bank(it).rearrange("p (k s) -> p k s", k=4),
                                                hT_hi[:, cc % 3, :, :].bitcast(F32), ALU.subtract).then_inc(mv_free, 1)
                    elif kind == "C":
                        give_back(cc, mv_bank(it), m_v[it] + 1 + NMV * j)
                    elif kind == "X" and cc == 1 and more:
                        rest_tokens(j + 1)

            last_job = dve.value_load(tabi[0:1, EXTRA + 1:EXTRA + 2], min_val=NE - 1, max_val=NJ - 1)
            with dve.Fori(0, last_job) as j:
                job(j, True)
            job(last_job, False)
            for i in range(2 * LT):
                give_back(i, PS[:, i % 3, :], i + 1 + NMV + NMV * last_job)
            dve.wait_ge(mv_free, 3 + 2 * LT + NMV + NMV * last_job)
            for tt in range(LT):
                step(nc.vector.tensor_tensor(macc[:, tt, :], macc[:, tt, :], modb[:, 2, :], ALU.mult))
                nc.vector.tensor_tensor(H[:, CT + tt, :], H[:, CT + tt, :], macc[:, tt, :], ALU.add).then_inc(h_ready, 1)
            norm_dve(4)
            dve.wait_ge(fin_in, 16)
            for t in range(CT, T):
                step(nc.vector.tensor_scalar(H[:, t, :], H[:, t, :], stat[:, 12 + t:13 + t], None, ALU.mult))
                nc.vector.tensor_tensor(H[:, t, :], H[:, t, :], fin_g, ALU.mult).then_inc(h_ready, 1)

        @block.tensor
        def _(pe):
            def open_v(g, shift=None):
                if shift is not None:
                    pe.wait_ge(v_free, g - 3 + shift)
                elif g >= 4:
                    pe.wait_ge(v_free, g - 3)
                return v_bank(g)

            def open_a(g, shift=None):
                if shift is not None:
                    pe.wait_ge(a_free, g - 3 + shift)
                elif g >= 4:
                    pe.wait_ge(a_free, g - 3)
                return a_bank(g)

            def unit(n):
                pe.wait_ge(unit_in[n % 3], 16 * (n // 3 + 1))
                return WR[:, n % 3, :]

            def accumulate(bank, pairs):
                for i, (a, b) in enumerate(pairs):
                    last = nc.tensor.matmul(bank, a, b, start=(i == 0), stop=(i == len(pairs) - 1))
                return last

            pe.wait_ge(rows_in, 16 * 8)
            b = open_v(0)
            nc.tensor.transpose(b[:, 0:64], rows1[:, :], ident[0:64, 0:64])
            nr = 4 * CONV_CH // P
            nc.tensor.transpose(b[:, 64:64 + nr], rows2[:, :], ident[0:nr, 0:nr]).then_inc(v_full, 1)

            def mod_products(dst, w):
                for k in range(KD):
                    for j in range(4):
                        last = nc.tensor.matmul(dst[32 * j:32 * j + 32, :], cstat[:, k, :],
                                                w[:, k, j * P:j * P + P], start=(k == 0), stop=(k == KD - 1),
                                                tile_position=(0, 32 * j), skip_group_check=True)
                return last

            def mod_columns(b, g):
                bank = open_v(g)
                for u4 in range(4):
                    last = nc.tensor.transpose(bank[:, u4 * P:u4 * P + P], modr[:, 4 * b + u4, :], ident)
                last.then_inc(v_full, 1)

            def mod_gates(l):
                i = 0
                for gate in range(2):
                    for v in range(2 - l):
                        for uu in range(2):
                            bank = open_a(a0["mod1" if l else "mod0t"] + i)
                            i += 1
                            for j in range(4):
                                pick = ident[:, 32 * j + v:32 * j + v + 1].to_broadcast([P, P])
                                last = nc.tensor.matmul(bank[:, j * P:j * P + P], pick, modr[:, 4 + 6 * gate + uu, :],
                                                        start=True, stop=True)
                            last.then_inc(a_full, 1)

            def norm_pe(n):
                tiles = NTILES[n]
                pe.wait_ge(xn_ready, sq_done[n] + len(tiles))
                for i in range(4):
                    for odd in range(2):
                        k = 2 * i + odd
                        g = (a0 if odd else v0)[f"norm{n}"] + i
                        bank = (open_a if odd else open_v)(g)
                        for t in tiles:
                            src = xn[:, t, :] if n < 3 else y2[:, t - CT, :]
                            last = nc.tensor.transpose(bank[:, t * P:t * P + P], src[:, k * P:k * P + P], ident)
                        last.then_inc(a_full if odd else v_full, 1)

            def at_ready(n):
                pe.wait_ge(v_free, v0[f"norm{n}"] + 4)
                pe.wait_ge(a_free, a0[f"norm{n}"] + 4)

            pe.wait_ge(csil_ready, 1)
            pe.wait_ge(zeroed, 3)
            bank = open_v(v0["mod0"])
            for u4 in range(4):
                n = first["mod0"] + u4
                last = mod_products(bank[:, u4 * P:u4 * P + P], unit(n).rearrange("p (k n) -> p k n", k=KD))
                if u4 < 3:
                    last.then_inc(unit_used, 1)
            last.then_inc(v_full, 1)
            pe.wait_ge(v_full, v0["mod0"] + 1)
            pe.sem_inc(unit_used, 1)
            pe.wait_ge(modr_ready, 1)
            mod_columns(0, v0["mod0"] + 1)
            norm_pe(0)
            at_ready(0)
            for i in range(3 * T):
                t, cc = i // 3, i % 3
                g = a0["qkv"] + i
                bank = open_a(g)
                w = unit(first["qkv"] + cc).rearrange("p (k n) -> p k n", k=KD)
                last = accumulate(bank, [(aT[:, k, t * P:t * P + P], w[:, k, :]) for k in range(KD)])
                last.then_inc(a_full, 1)
                if t == T - 1:
                    pe.wait_ge(a_full, g + 1)
                    pe.sem_inc(unit_used, 1)
            for i in range(3 * T):
                t, cc = i // 3, i % 3
                g = a0["qkT"] + i
                pe.wait_ge(qk_ready, t + 1)
                bank = open_a(g)
                for h in range(4 if cc < 2 else NKV):
                    last = nc.tensor.transpose(bank[:, h * P:h * P + P], qk[:, t, (4 * cc + h) * HD:(4 * cc + h + 1) * HD], ident)
                last.then_inc(a_full, 1)
            pe.wait_ge(a_free, a0["qkT"] + 3 * T)
            for kind, m in TSEQ:
                if kind == "S":
                    t, g, h, nk = pair(m)
                    bank = open_a(att_a[kind, m])
                    nc.tensor.matmul(bank[:, 0:nk * P], qT[:, h, t * P:t * P + P], kT[:, g, 0:nk * P], start=True, stop=True)\
                        .then_inc(a_full, 1)
                elif kind == "T":
                    nk = pair(m)[3]
                    bank = open_v(att_v[kind, m])
                    pe.wait_ge(p_norm, m + 1)
                    for k in range(nk):
                        last = nc.tensor.transpose(bank[:, k * P:k * P + P], pbuf[:, m % 8, k * P:k * P + P], ident)
                    last.then_inc(v_full, 1)
                    pe.wait_ge(v_full, att_v[kind, m] + 1)
                    pe.sem_inc(p_used, 1)
                elif kind == "M":
                    bank = open_v(att_v[kind, m])
                    mod_products(bank[:, 0:P], unit(first["mod0b"] + m - 4).rearrange("p (k n) -> p k n", k=KD)).then_inc(v_full, 1)
                    pe.wait_ge(v_full, att_v[kind, m] + 1)
                    pe.sem_inc(unit_used, 1)
                else:
                    t, g, _, nk = pair(QG * m)
                    bank = open_a(att_a[kind, m])
                    pe.wait_ge(v_free, att_v["T", QG * m + QG - 1] + 1)
                    last = accumulate(bank, [(vv[:, k, g * HD:g * HD + HD], pT[:, m % 2, k, :]) for k in range(nk)])
                    last.then_inc(a_full, 1)
            pe.wait_ge(modr_ready, 9)
            mod_columns(1, v0["mod0t"])
            mod_columns(2, v0["mod0t"] + 1)
            mod_gates(0)
            pe.wait_ge(a_free, a0["attn"] + n_s + n_o)
            for i in range(2 * T):
                t, hf = i // 2, i % 2
                g = v0["wo"] + i
                bank = open_v(g)
                w = unit(first["wo"] + hf).rearrange("p (k n) -> p k n", k=KD)
                last = accumulate(bank, [(oT[:, k, t * P:t * P + P], w[:, k, :]) for k in range(KD)])
                last.then_inc(v_full, 1)
                if t == T - 1:
                    pe.wait_ge(v_full, g + 1)
                    pe.sem_inc(unit_used, 1)
            norm_pe(1)
            at_ready(1)
            pe.wait_ge(alo_ready, 4)

            def three(bank, pairs):
                for i_, ((ah, al), (bh, bl)) in enumerate(pairs):
                    nc.tensor.matmul(bank, ah, bh, start=(i_ == 0), stop=False)
                    nc.tensor.matmul(bank, ah, bl, start=False, stop=False)
                    last = nc.tensor.matmul(bank, al, bh, start=False, stop=(i_ == len(pairs) - 1))
                return last

            def halves(v, k):
                return (f_hi[:, v % 3, :].rearrange("p (k n) -> p k n", k=k), f_lo[:, v % 3, :].rearrange("p (k n) -> p k n", k=k))

            def hidden(v, bank, q):
                hi, lo = halves(v, KD)
                c_ = slice(q * P, q * P + P)
                return three(bank, [((hi[:, k, c_], lo[:, k, c_]), (a_hi[:, k, :], a_lo[:, k, :])) for k in range(KD)])

            def chunk(i, more):
                for half in range(2):
                    for q in range(2):
                        ft = 2 * half + q
                        pe.wait_ge(flo_ready, 2 * half + 1 + NFH * i)
                        pe.wait_ge(fa_free, ft + 1 + 4 * i)
                        hidden(2 * half, PS[:, 4 + ft % 2, :], q).then_inc(fa_full, 1)
                        pe.wait_ge(flo_ready, 2 * half + 2 + NFH * i)
                        g = v0["ffn"] + ft
                        hidden(2 * half + 1, open_v(g, NFV * i), q).then_inc(v_full, 1)
                    if more:
                        pe.wait_ge(modu_in, 16 * (half + 1) + 32 * i)
                        if half == 0:
                            pe.wait_ge(modu_added, 1 + i)
                        mod_products(PS[:, 6, half * P:half * P + P], mod_unit).then_inc(modu_used, 1)
                for half in range(2):
                    hi, lo = halves(4 + half, 2)
                    pe.wait_ge(flo_ready, 5 + half + NFH * i)
                    pe.wait_ge(hlo_ready, 2 + 2 * half + 4 * i)
                    for j in range(2 * T):
                        t, hf = j // 2, j % 2
                        c_ = slice(hf * N, hf * N + N)
                        r_ = slice(t * P, t * P + P)
                        bank = open_v(v0["ffn"] + 4 + 2 * T * half + j, NFV * i)
                        three(bank, [((h_hi[:, 2 * half + k, r_], h_lo[:, 2 * half + k, r_]), (hi[:, k, c_], lo[:, k, c_]))
                                     for k in range(2)]).then_inc(v_full, 1)

            pe.wait_ge(a_free, a0["norm1"] + 4)
            pe.sem_inc(modu_added, 1)
            with pe.Fori(0, FC - 1) as i:
                chunk(i, True)
            chunk(FC - 1, False)
            pe.wait_ge(modu_added, FC)
            for b in range(3):
                mod_columns(b, v0["mod1"] + b)
            mod_gates(1)
            norm_pe(2)
            at_ready(2)
            pe.wait_ge(params_in, 16 * 9)
            g = v0["dt"]
            bank = open_v(g)
            for t in range(T):
                last = accumulate(bank[:, t * 2 * SH:(t + 1) * 2 * SH], [(aT[:, k, t * P:t * P + P], w_dt[:, k, :]) for k in range(KD)])
            last.then_inc(v_full, 1)

            def channels(ct):
                g = v0["xbc"] + ct
                bank = open_v(g)
                pe.wait_ge(convs_ready, ct + 1)
                for t in range(T):
                    last = nc.tensor.transpose(bank[:, t * P:t * P + P], convs[:, ct % 2, t * P:t * P + P], ident)
                last.then_inc(v_full, 1)

            for ct in range(NCT):
                g = a0["xbc"] + ct
                n = first["xbc"] + ct // 4
                w = unit(n).rearrange("p (k n) -> p k n", k=KD)
                bank = open_a(g)
                lo = 0 if ct < NXB else CTX
                last = accumulate(bank[:, lo:NTOK], [(w[:, k, ct % 4 * P:ct % 4 * P + P], aT[:, k, lo:NTOK]) for k in range(KD)])
                last.then_inc(a_full, 1)
                if ct % 4 == 3:
                    pe.wait_ge(a_full, g + 1)
                    pe.sem_inc(unit_used, 1)
                if 1 <= ct <= NXB:
                    channels(ct - 1)
            g = a0["dec"]
            bank = open_a(g)
            pe.wait_ge(da_ready, 1)
            pe.wait_ge(zeroed, 3)

            def sums(o, tri, t, d, other=None):
                pairs = [(tri, da[:, t, SH * d:SH * d + SH])]
                if other is not None:
                    pairs.append((ones[:, :], da[:, other, SH * d:SH * d + SH]))
                return accumulate(bank[:, o:o + SH], pairs)
            for tt in range(LT):
                for d in range(2):
                    sums(64 * tt + SH * d, (LE, GE)[d], CT + tt, d)
            for t in range(CT):
                for d in range(2):
                    sums(128 + 64 * t + SH * d, (GTm, LTm)[d], t, d, 1 - t if t == d else None)
            for d in range(2):
                sums(256 + SH * d, (GTm, LTm)[d], CT + d, d)
            for d in range(2):
                last = sums(320 + SH * d, ones[:, :], CT + d, d)
            last.then_inc(a_full, 1)
            for i in range(LT * INNER // N):
                u, tt = i // LT, i % LT
                g = a0["z"] + i
                w = unit(first["z"] + u).rearrange("p (k n) -> p k n", k=KD)
                bank = open_a(g)
                last = accumulate(bank, [(aT[:, k, CTX + tt * P:CTX + tt * P + P], w[:, k, :]) for k in range(KD)])
                last.then_inc(a_full, 1)
                if tt == LT - 1:
                    pe.wait_ge(a_full, g + 1)
                    pe.sem_inc(unit_used, 1)
            pe.wait_ge(bT_ready, 2 * SG)
            for tt in range(LT):
                g = v0["cb"] + tt
                bank = open_v(g)
                for gg in range(SG):
                    last = nc.tensor.matmul(bank[:, gg * P:gg * P + P], bT[:, gg, tt * P:tt * P + P], cT[:, gg, tt * P:tt * P + P],
                                            start=True, stop=True)
                last.then_inc(v_full, 1)
            pe.wait_ge(v_free, v0["xbc"] + NXB)
            for q in range(6):
                d = (0, 0, 1, 1, 0, 1)[q]
                t = (0, 1, 0, 1, CT, CT + 1)[q]
                pe.wait_ge(xw_ready, q + 1)
                for gg in range(SG):
                    if q < 4:
                        g = a0["st"] + SG * d + gg
                        bank = open_a(g) if q % 2 == 0 else a_bank(g)
                    else:
                        g = v0["st2"] + SG * d + gg
                        bank = open_v(g)
                    last = nc.tensor.matmul(bank, btok[:, t, gg * P:gg * P + P], xw[:, q % 2, gg * N:gg * N + N],
                                            start=(q % 2 == 0 or q >= 4), stop=(q % 2 == 1 or q >= 4))
                    if q >= 4:
                        last.then_inc(v_full, 1)
                    elif q % 2:
                        last.then_inc(a_full, 1)
                if q in (0, 2):
                    last.then_inc(xw_used, 1)
            pe.wait_ge(a_free, a0["st"] + 2 * SG)
            pe.wait_ge(v_free, v0["st2"] + 2 * SG)
            for i in range(2 * LT * SG):
                tt, gg, d = i // (2 * SG), i // 2 % SG, i % 2
                g = v0["yoff"] + i
                bank = open_v(g)
                nc.tensor.matmul(bank, cT[:, gg, tt * P:tt * P + P], hs[d][tt if d == 0 else LT - 1 - tt][:, gg * N:gg * N + N],
                                 start=True, stop=True).then_inc(v_full, 1)
            pe.wait_ge(v_full, v0["yoff"] + 2 * LT * SG)
            pe.sem_inc(states_used, 1)

            def segments(it):
                for d in range(2):
                    pe.wait_ge(ld_ready, 2 * it + d + 1)
                    for hf in range(2):
                        bank = open_a(a0["seg"] + 4 * it + 2 * d + hf)
                        for h4 in range(4):
                            last = nc.tensor.matmul(bank[:, h4 * P:h4 * P + P], ld[d][:, 4 * hf + h4, :], (LE, GE)[d],
                                                    start=True, stop=True)
                        last.then_inc(a_full, 1)

            segments(0)
            for it in range(LT * SG):
                tt, gg = it // SG, it % SG
                if it + 1 < LT * SG:
                    segments(it + 1)
                pe.wait_ge(m_ready, 2 * it + 2)
                bank = open_v(v0["ydiag"] + it)
                for h in range(HP):
                    for d in range(2):
                        o_ = (HP * gg + h) * HDIM
                        last = nc.tensor.matmul(bank[:, h * HDIM:(h + 1) * HDIM], mm[it % 2][:, d, h, :],
                                                xdt[tt][:, d, o_:o_ + HDIM], start=(d == 0), stop=(d == 1))
                last.then_inc(v_full, 1)
            for tt in range(LT):
                for q in range(INNER // N):
                    bank = open_v(v0["gT"] + tt * (INNER // N) + q)
                    pe.wait_ge(yn_ready, SG * tt + q + 1)
                    for k4 in range(4):
                        last = nc.tensor.transpose(bank[:, k4 * P:k4 * P + P], yacc[:, tt, (4 * q + k4) * P:(4 * q + k4 + 1) * P], ident)
                    last.then_inc(v_full, 1)
            pe.wait_ge(v_free, v0["gT"] + LT * INNER // N)
            nu = INNER // (4 * P)
            for u in range(nu):
                w = unit(first["sout"] + u).rearrange("p (k n) -> p k n", k=4)
                for i in range(2 * LT):
                    tt, hf = i // 2, i % 2
                    bank = open_v(v0["sout"] + i) if u == 0 else v_bank(v0["sout"] + i)
                    for k in range(4):
                        last = nc.tensor.matmul(bank, gT[:, 4 * u + k, tt * P:tt * P + P], w[:, k, hf * N:hf * N + N],
                                                start=(u == 0 and k == 0), stop=(u == nu - 1 and k == 3))
                    if u == nu - 1:
                        last.then_inc(v_full, 1)
                    elif i == 2 * LT - 1:
                        last.then_inc(unit_used, 1)
            pe.wait_ge(v_full, v0["sout"] + 2 * LT)
            pe.sem_inc(moe_free, RS)
            norm_pe(3)
            at_ready(3)
            bank = open_v(v0["route"])
            for tt in range(LT):
                last = accumulate(bank[:, tt * NE:(tt + 1) * NE], [(aTl[:, k, tt * P:tt * P + P], rout[:, k, :]) for k in range(KD)])
            last.then_inc(v_full, 1)
            pe.wait_ge(mask_ready, 1)
            bank = open_v(v0["route"] + 1)
            m_ = [rt[:, 10 + tt, :] for tt in range(LT)]
            accumulate(bank[:, 0:NE], [(LTm, m_[0])])
            accumulate(bank[:, NE:2 * NE], [(ones[:, :], m_[0]), (LTm, m_[1])])
            accumulate(bank[:, 2 * NE:3 * NE], [(ones[:, :], m_[0]), (ones[:, :], m_[1])]).then_inc(v_full, 1)

            pe.wait_ge(v_free, v0["end"])
            pe.wait_ge(a_free, a0["end"])
            pe.wait_ge(tables_ready, 1)
            last_job = pe.value_load(tabi[0:1, EXTRA + 1:EXTRA + 2], min_val=NE - 1, max_val=NJ - 1)

            def fetch(i, bank, n, free):
                pe.wait_ge(ma_free, free)
                pe.wait_ge(perm_ready, n)
                for k4 in range(4):
                    k = 4 * i + k4
                    last = accumulate(bank[:, k4 * P:k4 * P + P],
                                      [(y2[:, tt, k * P:k * P + P], perm[:, tt, :]) for tt in range(LT)])
                last.then_inc(ma_full, 1)

            def give_back(cc, bank, free, n):
                pe.wait_ge(mv_free, free)
                pe.wait_ge(ye_ready, n)
                hf = cc % 2
                nc.tensor.matmul(bank, permT[:, cc // 2 * P:cc // 2 * P + P], ye[:, hf * N:hf * N + N],
                                 start=True, stop=True).then_inc(mv_full, 1)

            def three_of(bank, hi, lo, w_hi, w_lo, start, stop):
                nc.tensor.matmul(bank, hi, w_hi, start=start, stop=False)
                nc.tensor.matmul(bank, hi, w_lo, start=False, stop=False)
                return nc.tensor.matmul(bank, lo, w_hi, start=False, stop=stop)

            for i in range(2):
                fetch(i, PS[:, 3 + i, :], LT, i + 1)

            def job(j, more):
                for it in MSEQ:
                    kind, cc = it
                    if kind in "GP":
                        pe.wait_ge(ma_free, m_a[it] - 1 + 4 + NMA * j)
                        bank = ma_bank(it)
                    elif kind in "UT":
                        pe.wait_ge(mv_free, m_v[it] - 2 + 3 + NMV * j)
                        bank = mv_bank(it)
                    if it == ("G", 0):
                        pe.wait_ge(xlo_ready, 1 + j)
                    if kind in "GU":
                        for half in range(2):
                            v = 2 * m_u[it] + half
                            pe.wait_ge(moe_lo, v + 1 + NHU * j)
                            hi = m_hi[:, v % HS_, :].rearrange("p (k n) -> p k n", k=4)
                            lo = m_lo[:, v % RS, :].rearrange("p (k n) -> p k n", k=4)
                            for k in range(4):
                                kk = 4 * half + k
                                last = three_of(bank, xe_hi[:, kk, :], xe_lo[:, kk, :], hi[:, k, :], lo[:, k, :],
                                             kk == 0, kk == KD - 1)
                            if half == 0:
                                last.then_inc(moe_free, 1)
                        last.then_inc(ma_full if kind == "G" else mv_full, 1)
                        pe.wait_ge(*((ma_full, m_a[it] + 3 + NMA * j) if kind == "G" else (mv_full, m_v[it] + 1 + NMV * j)))
                        pe.sem_inc(moe_free, 1)
                    elif kind == "T":
                        pe.wait_ge(mv_free, m_v["U", cc] + 1 + 3 + NMV * j)
                        for k4 in range(4):
                            last = nc.tensor.transpose(bank[:, k4 * P:k4 * P + P], hm[:, cc % 2, k4 * P:k4 * P + P], ident)
                        last.then_inc(mv_full, 1)
                    elif kind == "P":
                        pe.wait_ge(permg_ready, LT + LT * j)
                        for tt in range(LT):
                            last = nc.tensor.transpose(bank[:, tt * P:tt * P + P], permg[:, tt, :], ident)
                        last.then_inc(ma_full, 1)
                    elif kind == "D":
                        pe.wait_ge(mv_free, m_v["T", cc] + 1 + 3 + NMV * j)
                        for half in range(2):
                            v = 2 * m_u[it] + half
                            pe.wait_ge(moe_lo, v + 1 + NHU * j)
                            hi = m_hi[:, v % HS_, :].rearrange("p (k n) -> p k n", k=2)
                            lo = m_lo[:, v % RS, :].rearrange("p (k n) -> p k n", k=2)
                            for k in range(2):
                                kk = 2 * half + k
                                for hf in range(2):
                                    c_ = slice(hf * N, hf * N + N)
                                    last = three_of(PS[:, 6 + hf, :], hT_hi[:, cc % 3, kk, :], hT_lo[:, cc % 3, kk, :],
                                                 hi[:, k, c_], lo[:, k, c_], cc == 0 and kk == 0, cc == FC - 1 and kk == 3)
                            last.then_inc(moe_free, 1)
                        if cc == FC - 1:
                            pe.wait_ge(moe_free, RS + NHU + NHU * j)
                            pe.sem_inc(down_full, 1)
                    elif kind == "C":
                        give_back(cc, mv_bank(it), m_v[it] - 2 + 3 + NMV * j, 2 + 2 * j)
                    elif kind == "X" and more:
                        fetch(cc, ma_bank(it), 2 * LT + LT * j, m_a[it] - 1 + 4 + NMA * j)

            with pe.Fori(0, last_job) as j:
                job(j, True)
            job(last_job, False)
            for i in range(2 * LT):
                give_back(i, PS[:, i % 3, :], i - 2 + 3 + NMV + NMV * last_job, 4 + 2 * last_job)


_NAMES = ['x', 'c', 'ctx', 'c_ctx', 'w_mod', 'b_mod', 'norm1_g', 'norm2_g', 'attn_w_qkv', 'attn_q_g', 'attn_k_g', 'attn_w_o',
          'ssd_w_in', 'ssd_conv_w', 'ssd_conv_b', 'ssd_dt_bias_f', 'ssd_dt_bias_b', 'ssd_a_log_f', 'ssd_a_log_b',
          'ssd_d_skip', 'ssd_norm_g', 'ssd_w_out', 'ffn_w_gate', 'ffn_w_up', 'ffn_w_down', 'moe_router',
          'moe_w_gate', 'moe_w_up', 'moe_w_down', 'final_g']


def kernel(**inputs):
    import concourse.bacc as _bacc
    from concourse.bass_utils import run_bass_kernel_spmd as _run

    nc = _bacc.Bacc("TRN2", target_bir_lowering=False, num_devices=1)
    seq = inputs['x'].shape[1]
    arrays = {"consts": constants(seq, 64, inputs['attn_q_g'].shape[1], inputs['moe_router'].shape[2])}
    for name in _NAMES:
        arrays[f"in_{name}"] = np.ascontiguousarray(inputs[name])
    args = [nc.dram_tensor(n, a.shape, mybir.dt.from_np(a.dtype), kind="ExternalInput").ap() for n, a in arrays.items()]
    args.append(nc.dram_tensor("out", inputs['x'].shape, F32, kind="ExternalOutput").ap())
    backbone(nc, *args)
    r = _run(nc, [arrays], core_ids=[0])
    return r.results[0]["out"]
```

```python
from contextlib import ExitStack

import numpy as np

import concourse.bass as bass
from concourse import mybir

P = 128
ALU = mybir.AluOpType
ACT = mybir.ActivationFunctionType
F32 = mybir.dt.float32
I32 = mybir.dt.int32
F32R = mybir.dt.float32r
AX = mybir.AxisListType


def constants(seq, grid_w, head_dim, n_experts):
    p = np.arange(P)[:, None]
    f = np.arange(P)[None, :]
    parts = [p == f, p <= f, p >= f, p < f, p > f, np.broadcast_to(f + 1, (P, P))]
    e = np.arange(n_experts)[None, :]
    parts += [np.broadcast_to(n_experts - e, (P, n_experts)), np.broadcast_to(e, (P, n_experts))]
    axis_dim = head_dim // 2
    inv_freq = (1.0 / (10000.0 ** (np.arange(0, axis_dim, 2, dtype=np.float32) / axis_dim))).astype(np.float32)
    tok = np.arange(seq)
    tables = []
    for ids in (tok // grid_w, tok % grid_w):
        ang = ids.astype(np.float32)[:, None] * inv_freq
        tables.append((np.cos(ang), np.sin(ang)))
    cos = np.concatenate([np.concatenate([c, c], 1) for c, _ in tables], 1)
    sin = np.concatenate([np.concatenate([-s, s], 1) for _, s in tables], 1)
    for table in (cos, sin):
        parts.append(table.reshape(seq // P, P, head_dim).transpose(1, 0, 2).reshape(P, -1))
    return np.ascontiguousarray(np.concatenate([np.asarray(x, np.float32) for x in parts], 1))


def backbone(nc, consts, x, c, ctx_tok, c_ctx, w_mod, b_mod, norm1_g, norm2_g,
             w_qkv, q_g, k_g, w_o,
             ssd_w_in, conv_w, conv_b, dt_bias_f, dt_bias_b, a_log_f, a_log_b, d_skip, ssd_norm_g, ssd_w_out,
             ffn_gate, ffn_up, ffn_down, router, moe_gate, moe_up, moe_down, final_g, out):
    _, SEQ, D = x.shape
    CTX = ctx_tok.shape[1]
    KD = D // P
    CT, LT = CTX // P, SEQ // P
    T = CT + LT
    NTOK = CTX + SEQ
    N = 512
    HD = q_g.shape[1]
    NH = w_o.shape[1] // HD
    NKV = (w_qkv.shape[2] // HD - NH) // 2
    QG = NH // NKV
    QKVW = w_qkv.shape[2]
    DFF = ffn_gate.shape[2]
    FC = DFF // N
    INNER = ssd_w_out.shape[1]
    CONV_CH = conv_w.shape[2]
    GN = (CONV_CH - INNER) // 2
    SG = GN // P
    SH = dt_bias_f.shape[1]
    HP = SH // SG
    HDIM = INNER // SH
    NE = router.shape[2]
    EPS = 1e-6
    EXTRA = (2 * SEQ) // (P + 1)
    assert D == 1024 and T == 4 and CT == 2 and LT == 2 and HD == P and QKVW == 3 * N and GN == N and HP * HDIM == N

    es = ExitStack()
    with es:
        def sb(name, shape, dt=F32):
            return es.enter_context(nc.sbuf_tensor(name, shape, dt))

        def sem(name):
            return es.enter_context(nc.semaphore(name))

        NC_ = consts.shape[1]
        const = sb("const", [P, NC_])
        ident = const[:, 0:P]
        LE, GE, LTm, GTm = (const[:, P * i:P * i + P] for i in range(1, 5))
        iota1 = const[:, 5 * P:6 * P]
        o = 6 * P
        rev_e = const[:, o:o + NE]
        fwd_e = const[:, o + NE:o + 2 * NE]
        o += 2 * NE
        rope_c = const[:, o:o + LT * HD].rearrange("p (t d) -> p t d", t=LT)
        rope_s = const[:, o + LT * HD:o + 2 * LT * HD].rearrange("p (t d) -> p t d", t=LT)
        ones = sb("ones", [P, P])
        rows1 = sb("rows1", [64, P])
        rows2 = sb("rows2", [4 * CONV_CH // P, P])
        cols1 = sb("cols1", [P, 64])
        cols2 = sb("cols2", [P, 4 * CONV_CH // P])
        cstat = sb("cstat", [P, KD, 32])
        qg_b = sb("qg_b", [P, HD])
        kg_b = sb("kg_b", [P, HD])
        dskip_b = sb("dskip_b", [P, SH])
        dtb_b = sb("dtb_b", [P, 2 * SH])
        alog_b = sb("alog_b", [P, 2 * SH])
        rout = sb("rout", [P, KD, NE])
        w_dt = sb("w_dt", [P, KD, 2 * SH])
        mod_all = sb("mod_all", [P, 24 * P])
        mod_all_at = nc.sbuf_base - 4 * 24 * P
        modr = mod_all[:, 0:12 * P].rearrange("p (u n) -> p u n", u=12)
        biasr = mod_all[:, 12 * P:24 * P].rearrange("p (u n) -> p u n", u=12)
        modc = sb("modc", [P, 48, 2])
        gcol = sb("gcol", [P, 2, KD, 2])
        stat = sb("stat", [P, 64])
        H = sb("H", [P, T, D])
        modb = sb("modb", [P, 4, D])
        AT_ = sb("AT", [P, 4096])
        aT_at = nc.sbuf_base - 4 * 4096
        aT = AT_[:, :].rearrange("p (k n) -> p k n", k=KD)
        slab = sb("slab", [P, 8 * 4096])
        slab_at = nc.sbuf_base - 4 * 8 * 4096

        def at(name, o, shape, dt=F32):
            return nc.alloc_sbuf_tensor_at(name, [P] + shape, dt, offset=slab_at + 4 * o)

        WR = slab[:, 0:3 * 4096].rearrange("p (a n) -> p a n", a=3)
        AR0 = 3 * 4096
        AR = slab[:, 3 * 4096:8 * 4096]

        def ar(o, *dims):
            n = 1
            for d_ in dims:
                n *= d_
            v = AR[:, o:o + n]
            if len(dims) == 2:
                v = v.rearrange("p (a b) -> p a b", a=dims[0])
            if len(dims) == 3:
                v = v.rearrange("p (a b c) -> p a b c", a=dims[0], b=dims[1])
            return v

        QKW = (NH + NKV) * HD
        qk = ar(0, T, QKW)
        pbuf = ar(0, 8, N)
        vv = ar(5120, T, NKV * HD)
        qT = ar(6144, NH, NTOK)
        kT = ar(10240, NKV, NTOK)
        oT = ar(11264, NH, NTOK)
        pT = ar(15360, 2, T, N)
        xn = ar(15360, T, D)
        rope_t = ar(11264, 10, HD)
        sq_t = ar(12544, 10, HD)
        HALF = 2048
        hT = ar(4096, 4, N)
        facc = ar(8192, T, D)
        FSL = 4
        h_lo = at("h_lo", AR0 + 4096, [4, N], F32R)
        h_hi = at("h_hi", AR0 + 6144, [4, N], F32R)
        a_lo = nc.alloc_sbuf_tensor_at("a_lo", [P, KD, NTOK], F32R, offset=aT_at)
        a_hi = at("a_hi", AR0 + 12288, [KD, NTOK], F32R)
        f_raw = at("f_raw", 0, [FSL, HALF])
        f_lo = at("f_lo", 0, [FSL, HALF], F32R)
        f_hi = at("f_hi", FSL * HALF, [FSL, HALF], F32R)
        mod_unit = ar(16384, KD, N)

        xt = ar(0, T, INNER)
        btok = ar(8192, T, GN)
        bT = ar(10240, SG, SEQ)
        cT = ar(11264, SG, SEQ)
        zs = ar(12288, LT, INNER)
        raw = ar(16384, 2, 2, CTX + 2)
        conv = ar(17416, 2, NTOK)
        convs = ar(18440, 2, NTOK)
        xw = ar(16384, 2, INNER)
        s_raw = at("s_raw", 0, [3, HALF])
        s_lo = at("s_lo", 0, [3, HALF], F32R)
        s_hi = at("s_hi", 3 * HALF, [3, HALF], F32R)
        a_hi_lat = nc.alloc_sbuf_tensor_at("a_hi_lat", [P, KD, SEQ], F32R, offset=mod_all_at)
        hs = [[WR[:, d, 0:INNER], WR[:, d, INNER:2 * INNER]] for d in range(2)]
        yacc = AT_[:, :].rearrange("p (t n) -> p t n", t=LT)
        xdt = [ar(0, 2, INNER), ar(16384, 2, INNER)]
        ld = [modb[:, 1, :].rearrange("p (h s) -> p h s", h=HP), modb[:, 3, :].rearrange("p (h s) -> p h s", h=HP)]
        mm = [H[:, 0:CT, :].rearrange("p a (h s) -> p a h s", h=HP), ar(8192, 2, HP, P)]
        cbm = mod_all[:, 0:16 * P].rearrange("p (d t g l) -> p d t g l", d=2, t=LT, g=SG)
        spare = mod_all[:, 16 * P:24 * P]
        yoff_t = spare.rearrange("p (b n) -> p b n", b=2)
        gT = [ar(10240, INNER // P, P), ar(8192, INNER // P, P)]
        sp_a, sp_u, sp_s = (spare[:, 256 * i:256 * i + 256] for i in range(3))
        dt_ = sb("dt", [P, T, 2 * SH])
        da = sb("da", [P, T, 2 * SH])
        ex = sb("ex", [P, 384])
        wsc = sb("wsc", [P, 192])
        aTl = AT_[:, 0:2048].rearrange("p (k n) -> p k n", k=KD)
        y2 = AT_[:, 2048:4096].rearrange("p (t d) -> p t d", t=LT)
        fin_g = AT_[:, 0:D]
        RS, HS_, LEAD, NHU = 7, 6, 3, 2 * 3 * FC
        m_raw = at("m_raw", 0, [RS, HALF])
        m_lo = at("m_lo", 0, [RS, HALF], F32R)
        m_hi = at("m_hi", RS * HALF, [HS_, HALF], F32R)
        o_m = (RS + HS_) * HALF
        hT_hi = at("hT_hi", o_m, [3, 4, P], F32R)
        hT_lo = at("hT_lo", o_m + 1536, [3, 4, P], F32R)
        xe_hi = at("xe_hi", o_m + 3072, [KD, P], F32R)
        xe_lo = at("xe_lo", o_m + 4096, [KD, P], F32R)
        assert o_m + 5120 <= 8 * 4096 and NHU % RS == 0 and NHU % HS_ == 0
        xe = H[:, 0, :].rearrange("p (k s) -> p k s", k=KD)
        ye = H[:, 1, :]
        hm = modb[:, 1, :].rearrange("p (b n) -> p b n", b=2)
        sgm = modb[:, 3, :].rearrange("p (b n) -> p b n", b=2)
        macc = mod_all[:, 0:2 * D].rearrange("p (t d) -> p t d", t=LT)
        perm = spare[:, 0:2 * P].rearrange("p (t s) -> p t s", t=LT)
        permg = spare[:, 2 * P:4 * P].rearrange("p (t s) -> p t s", t=LT)
        permT = spare[:, 4 * P:6 * P]
        NJ = NE + EXTRA
        rt = sb("rt", [P, 24, NE])
        rankj = sb("rankj", [P, LT, NJ])
        gatej = sb("gatej", [P, LT, NJ])
        tabf = sb("tabf", [P, 8])
        tabi = sb("tabi", [P, 8], I32)

        PS = es.enter_context(nc.psum_tensor("PS", [P, 8, N], F32))

        params_in = sem("params_in")
        rows_in = sem("rows_in")
        tokens_in = sem("tokens_in")
        bias_in = sem("bias_in")
        unit_in = [sem(f"unit_in{i}") for i in range(3)]
        unit_used = sem("unit_used")
        zeroed = sem("zeroed")
        v_full, v_free, a_full, a_free = sem("v_full"), sem("v_free"), sem("a_full"), sem("a_free")
        cols_ready, csil_ready = sem("cols_ready"), sem("csil_ready")
        modr_ready, modc_ready, modb_ready = sem("modr_ready"), sem("modc_ready"), sem("modb_ready")
        sumsq_ready, meansq_ready, rms_ready = sem("sumsq_ready"), sem("meansq_ready"), sem("rms_ready")
        xn_ready, at_dve, at_act = sem("xn_ready"), sem("at_dve"), sem("at_act")
        h_ready = sem("h_ready")
        qkv_copied, qsum_ready, qsq_ready, qrms_ready = sem("qkv_copied"), sem("qsum_ready"), sem("qsq_ready"), sem("qrms_ready")
        qk_ready, qkT_ready = sem("qk_ready"), sem("qkT_ready")
        nmax_ready, p_exp, p_norm, p_used, pT_ready, oT_ready = (sem(n) for n in (
            "nmax_ready", "p_exp", "p_norm", "p_used", "pT_ready", "oT_ready"))
        fa_full, fa_free = sem("fa_full"), sem("fa_free")
        facc_done, facc_gated = sem("facc_done"), sem("facc_gated")
        f_in = [sem(f"f_in{i}") for i in range(FSL)]
        fhi_ready, flo_ready, ahi_ready, alo_ready, hhi_ready, hlo_ready = (sem(n) for n in (
            "fhi_ready", "flo_ready", "ahi_ready", "alo_ready", "hhi_ready", "hlo_ready"))
        s_in = [sem(f"s_in{i}") for i in range(3)]
        shi_ready, slo_ready, z_half, a_lat_ready = sem("shi_ready"), sem("slo_ready"), sem("z_half"), sem("a_lat_ready")
        modu_in, modu_used, modu_added = sem("modu_in"), sem("modu_used"), sem("modu_added")
        dve_step, act_step = sem("dve_step"), sem("act_step")
        pads_ready, raw_ready, conv_ready, convs_ready, bT_ready = (sem(n) for n in (
            "pads_ready", "raw_ready", "conv_ready", "convs_ready", "bT_ready"))
        sp_in, sp_exp, alog_ready, da_ready, ex_ready = (sem(n) for n in ("sp_in", "sp_exp", "alog_ready", "da_ready", "ex_ready"))
        xdt_ready = sem("xdt_ready")
        xw_ready, xw_used, ld_ready, states_used, m_ready = (sem(n) for n in ("xw_ready", "xw_used", "ld_ready", "states_used", "m_ready"))
        y_sum, y_sq, y_ms, y_rms, yn_ready = (sem(n) for n in ("y_sum", "y_sq", "y_ms", "y_rms", "yn_ready"))
        mask_ready, gap_ready, gap_exp, tables_ready = (sem(n) for n in ("mask_ready", "gap_ready", "gap_exp", "tables_ready"))
        moe_in = [sem(f"moe_in{i}") for i in range(RS)]
        moe_free, moe_hi, moe_lo = sem("moe_free"), sem("moe_hi"), sem("moe_lo")
        xe_ready, xhi_ready, xlo_ready, th_ready = sem("xe_ready"), sem("xhi_ready"), sem("xlo_ready"), sem("th_ready")
        permg_ready, zero_out = sem("permg_ready"), sem("zero_out")
        mv_full, mv_free, ma_full, ma_free = sem("mv_full"), sem("mv_free"), sem("ma_full"), sem("ma_free")
        perm_ready, down_full, ye_ready, fin_in = sem("perm_ready"), sem("down_full"), sem("ye_ready"), sem("fin_in")
        out_written = sem("out_written")

        units = []

        def cols_unit(w, c0):
            return w[:, c0:c0 + N].rearrange("(k p) n -> p k n", p=P)

        def rows_unit(w, r0):
            return w[r0:r0 + 4 * P, :].rearrange("(k p) n -> p k n", p=P)

        first = {}
        first["mod0"] = len(units)
        units += [cols_unit(w_mod[0], N * u) for u in range(4)]
        first["qkv"] = len(units)
        units += [cols_unit(w_qkv[0], N * u) for u in range(3)]
        first["mod0b"] = len(units)
        units += [cols_unit(w_mod[0], N * u) for u in range(4, 12)]
        first["wo"] = len(units)
        units += [cols_unit(w_o[0], N * u) for u in range(2)]
        units_b = []
        first["sout"] = len(units)
        assert first["sout"] % 3 == 2
        units_b += [rows_unit(ssd_w_out[0], 4 * P * u) for u in range(INNER // (4 * P))]
        NCT = CONV_CH // P
        NXB = (INNER + GN) // P
        NSX, NSZ = 2 * CONV_CH // N, 2 * INNER // N
        scan_halves = [ssd_w_in[0][:, INNER + N // 2 * h:INNER + N // 2 * (h + 1)].rearrange("(k p) n -> p k n", p=P)
                       for h in range(NSX)]
        scan_halves += [ssd_w_in[0][D // 2 * (h % 2):D // 2 * (h % 2 + 1), N * (h // 2):N * (h // 2) + N]
                        .rearrange("(k p) n -> p k n", p=P) for h in range(NSZ)]

        TSEQ = []
        NPAIR = T * NH
        for m in range(NPAIR + 3):
            if m < NPAIR:
                TSEQ.append(("S", m))
            if m >= 3:
                TSEQ.append(("T", m - 3))
                if (m - 3) % QG == QG - 1:
                    TSEQ.append(("M", 4 + (m - 3) // QG))
                if m - 3 >= 5 and (m - 3) % QG == 1:
                    TSEQ.append(("O", (m - 3) // QG - 1))
        TSEQ.append(("O", NPAIR // QG - 1))
        n_s = sum(k == "S" for k, _ in TSEQ)
        n_t = sum(k in "TM" for k, _ in TSEQ)
        n_o = sum(k == "O" for k, _ in TSEQ)
        NFV = 4 + 4 * T
        v0, a0 = {}, {}
        nv = na = 0
        for stage, more_v, more_a in (("prep", 1, 0), ("mod0", 2, 0), ("norm0", 4, 4), ("qkv", 0, 3 * T), ("qkT", 0, 3 * T),
                              ("attn", n_t, n_s + n_o), ("mod0t", 2, 8), ("wo", 2 * T, 0), ("norm1", 4, 4),
                              ("ffn", NFV * FC, 0), ("mod1", 3, 4), ("norm2", 4, 4),
                              ("dt", 1, 0), ("xbc", NXB, NCT), ("dec", 0, 1), ("z", 0, LT * INNER // N),
                              ("cb", LT, 0), ("st", 0, 2 * SG), ("st2", 2 * SG, 0), ("yoff", 2 * LT * SG, 0),
                              ("seg", 0, 4 * LT * SG), ("ydiag", LT * SG, 0), ("gT", LT * INNER // N, 0),
                              ("sout", 0, 2 * LT), ("norm3", 4, 4), ("route", 2, 0), ("end", 0, 0)):
            v0[stage], a0[stage] = nv, na
            nv, na = nv + more_v, na + more_a
        att_a, att_v = {}, {}
        for item in TSEQ:
            if item[0] in "TM":
                att_v[item] = v0["attn"] + len(att_v)
            else:
                att_a[item] = a0["attn"] + len(att_a)

        def v_bank(g):
            return PS[:, g % 4, :]

        def a_bank(g):
            return PS[:, 4 + g % 4, :]

        NTILES = {0: range(T), 1: range(T), 2: range(T), 3: range(CT, T), 4: range(CT, T)}
        sq_done = {0: 0, 1: T, 2: 2 * T, 3: 3 * T, 4: 3 * T + LT}
        H_DONE = {1: 0, 2: T, 3: 2 * T, 4: 2 * T + LT}
        aTs = [aT, aT, aT, aTl]
        aOff = [0, 0, 0, CTX]

        def pair(m):
            batch, hh = m // QG, m % QG
            t, g = batch // NKV, batch % NKV
            return t, g, QG * g + hh, (CT if t < CT else T)

        MSEQ = []
        for cc in range(FC):
            MSEQ += [("G", cc), ("U", cc)]
            if cc == 0:
                MSEQ += [("C", i) for i in range(2 * LT)]
            if cc >= 1:
                MSEQ.append(("T", cc - 1))
            if cc == 3:
                MSEQ.append(("P", 0))
            if cc >= 2:
                MSEQ.append(("D", cc - 2))
        MSEQ += [("X", 0), ("X", 1), ("T", FC - 1), ("D", FC - 2), ("D", FC - 1)]
        m_a = {it: i for i, it in enumerate(x_ for x_ in MSEQ if x_[0] in "XGP")}
        m_v = {it: i for i, it in enumerate(x_ for x_ in MSEQ if x_[0] in "UTC")}
        m_u = {it: i for i, it in enumerate(x_ for x_ in MSEQ if x_[0] in "GUD")}
        NMA, NMV, NMU = len(m_a), len(m_v), len(m_u)
        assert NMA % 2 == 0 and NMV % 3 == 0 and 2 * NMU == NHU

        def mv_bank(it):
            return PS[:, m_v[it] % 3, :]

        def ma_bank(it):
            return PS[:, 3 + m_a[it] % 2, :]

        NFH = 6

        def f_slot(v, p):
            return (NFH * p + v) % FSL

        def f_landed(v, ip, p):
            return f_in[f_slot(v, p)], 16 * ((NFH * p + v) // FSL + 1) + 32 * NFH // FSL * ip

        def half_used(v, i):
            if v < 0:
                v, i = v + NFH, i - 1
            V = v0["ffn"] + NFV * i
            return {0: (fa_full, 4 + 4 * i), 1: (v_full, V + 2), 2: (fa_full, 6 + 4 * i), 3: (v_full, V + 4),
                    4: (v_full, V + 4 + 2 * T), 5: (v_full, V + 4 + 4 * T)}[v]

        assert 2 * NFH % FSL == 0 and FC % 2 == 1

        def by_head(v):
            return v.unsqueeze(2).to_broadcast([P, v.shape[1], HDIM])

        def heads(v):
            return v.rearrange("p (h d) -> p h d", d=HDIM)

        def scan_used(h):
            if h < NSX:
                return a_full, a0["xbc"] + 2 * h + 2
            u, second = (h - NSX) // 2, (h - NSX) % 2
            return (a_full, a0["z"] + LT * (u + 1)) if second else (z_half, u + 1)

        block = es.enter_context(nc.Block())

        @block.sync
        def _(sp):
            def load(n, src):
                if n >= 3:
                    sp.wait_ge(unit_used, n - 2)
                dst = WR[:, n % 3, :].rearrange("p (k n) -> p k n", k=src.shape[1])
                sp.dma_start(dst, src).then_inc(unit_in[n % 3], 16)

            for n, src in enumerate(units):
                load(n, src)
            sp.wait_ge(v_full, v0["norm1"] + 4)
            sp.wait_ge(a_full, a0["norm1"] + 4)

            def chunk(ip, p, more):
                i = 2 * ip + p
                for v in range(NFH):
                    w = (ffn_gate, ffn_up, ffn_gate, ffn_up, ffn_down, ffn_down)[v][0]
                    o_ = i * N + (N // 2) * (v // 2 % 2 if v < 4 else v - 4)
                    src = w[:, bass.ds(o_, N // 2)] if v < 4 else w[bass.ds(o_, N // 2), :]
                    src = src.rearrange("(k p) n -> p k n", p=P)
                    sp.wait_ge(*half_used(v - FSL, i))
                    slot = f_slot(v, p)
                    sp.dma_start(f_raw[:, slot, :].rearrange("p (k n) -> p k n", k=src.shape[1]), src).then_inc(f_in[slot], 16)
                    if more and v in (1, 5):
                        u = 2 * i + v // 4
                        sp.wait_ge(modu_used, u + 1)
                        sp.dma_start(mod_unit, w_mod[1][:, bass.ds(u * N, N)].rearrange("(k p) n -> p k n", p=P))\
                            .then_inc(modu_in, 16)

            sp.sem_inc(modu_used, 1)
            sp.sem_inc(fa_full, 2)
            with sp.Fori(0, FC // 2) as ip:
                chunk(ip, 0, True)
                chunk(ip, 1, True)
            chunk(FC // 2, 0, False)
            sp.wait_ge(v_full, v0["ffn"] + NFV * FC)
            for h, src in enumerate(scan_halves):
                if h >= 3:
                    sp.wait_ge(*scan_used(h - 3))
                sp.dma_start(s_raw[:, h % 3, :].rearrange("p (k n) -> p k n", k=src.shape[1]), src).then_inc(s_in[h % 3], 16)
            sp.wait_ge(*scan_used(NSX + NSZ - 1))
            for n, src in enumerate(units_b):
                if n == 1:
                    sp.wait_ge(states_used, 1)
                load(n + first["sout"], src)

            def expert_loads(j, e):
                for it, u in m_u.items():
                    w = {"G": moe_gate, "U": moe_up, "D": moe_down}[it[0]][0][bass.ds(e, 1), :, :]\
                        .rearrange("a k n -> (a k) n")
                    for half in range(2):
                        v = 2 * u + half
                        if it[0] == "D":
                            r = 4 * P * it[1] + 2 * P * half
                            src = w[r:r + 2 * P, :]
                        else:
                            src = w[4 * P * half:4 * P * half + 4 * P, N * it[1]:N * it[1] + N]
                        src = src.rearrange("(k p) n -> p k n", p=P)
                        sp.wait_ge(moe_free, v + 1 + NHU * j)
                        sp.dma_start(m_raw[:, v % RS, :].rearrange("p (k n) -> p k n", k=src.shape[1]), src)\
                            .then_inc(moe_in[v % RS], 16)

            with sp.Fori(0, NE) as j:
                expert_loads(j, j)
            sp.wait_ge(tables_ready, 1)
            jobs = sp.value_load(tabi[0:1, EXTRA:EXTRA + 1], min_val=NE, max_val=NJ)
            with sp.If(jobs > NE):
                with sp.Fori(NE, jobs) as j:
                    e = sp.value_load(tabi[0:1, bass.ds(j - NE, 1)], min_val=0, max_val=NE - 1)
                    expert_loads(j, e)
            sp.wait_ge(h_ready, 2 * T + 3 * LT)
            sp.dma_start(out[0].rearrange("(t p) d -> p t d", p=P), H[:, CT:T, :]).then_inc(out_written, 16)
            sp.wait_ge(out_written, 16)

        @block.gpsimd
        def _(pool):
            pool.memset(cstat[:, :, :], 0.0).then_inc(zeroed, 1)
            pool.memset(ones[:, :], 1.0).then_inc(zeroed, 1)
            pool.memset(biasr, 0.0).then_inc(zeroed, 1)
            pool.wait_ge(zeroed, 3)
            for l in range(2):
                if l:
                    pool.wait_ge(modr_ready, 9)
                for v in range(2):
                    pool.dma_start(mod_all[v:P:32, 12 * P:24 * P].rearrange("j (u n) -> j u n", u=12),
                                   b_mod[l].rearrange("(u j n) -> j u n", j=4, n=P)).then_inc(bias_in, 16)
            for t in range(CT):
                pool.wait_ge(facc_done, t + 1)
                pool.tensor_tensor(facc[:, t, :], facc[:, t, :], modb[:, 3, :], ALU.mult).then_inc(facc_gated, 1)
                pool.wait_ge(facc_gated, t + 1)
                pool.tensor_tensor(H[:, t, :], H[:, t, :], facc[:, t, :], ALU.add).then_inc(h_ready, 1)
            pool.wait_ge(v_full, v0["norm2"] + 4)
            pool.wait_ge(a_full, a0["norm2"] + 4)
            for b in range(2):
                for edge in (0, CTX + 1):
                    pool.memset(raw[:, b, :, edge:edge + 1], 0.0).then_inc(pads_ready, 1)
            pool.wait_ge(da_ready, 1)
            pool.wait_ge(rows_in, 16 * 8)
            pool.wait_ge(h_ready, 2 * T)
            for r in range(2 * LT * SG):
                it, d = r // 2, r % 2
                tt, g = it // SG, it % SG
                if r == 2:
                    for i in range(2 * LT):
                        if i == 0:
                            pool.wait_ge(xw_ready, 4)
                        if i == 2:
                            pool.wait_ge(v_full, v0["st2"] + 2 * SG)
                        pool.tensor_tensor(heads(xdt[i // 2][:, i % 2, :]), heads(xt[:, CT + i // 2, :]),
                                           by_head(dt_[:, CT + i // 2, SH * (i % 2):SH * (i % 2) + SH]), ALU.mult)\
                            .then_inc(xdt_ready, 1)
                if r >= 2:
                    pool.wait_ge(a_full, a0["seg"] + 2 * (r - 2) + 2)
                pool.tensor_tensor(ld[d], (GTm, LTm)[d].unsqueeze(1).to_broadcast([P, HP, P]),
                                   da[:, CT + tt, d * SH + HP * g:d * SH + HP * g + HP].unsqueeze(2).to_broadcast([P, HP, P]),
                                   ALU.mult).then_inc(ld_ready, 1)
            pool.wait_ge(m_ready, 2 * LT * SG)
            pool.wait_ge(v_full, v0["ydiag"] + LT * SG)
            pool.memset(macc, 0.0).then_inc(zero_out, 1)
            pool.memset(permT, 0.0).then_inc(zero_out, 1)
            pool.memset(ye, 0.0).then_inc(zero_out, 1)
            pool.wait_ge(zero_out, 3)
            pool.sem_inc(ye_ready, 2)

        @block.scalar
        def _(act):
            steps = [0]

            def step(ins):
                steps[0] += 1
                ins.then_inc(act_step, 1)
                act.wait_ge(act_step, steps[0])

            act.dma_start(const[:, :], consts).then_inc(rows_in, 16)
            act.dma_start(rows1[0:16, :], norm1_g.rearrange("l (k p) -> (l k) p", p=P)).then_inc(rows_in, 16)
            act.dma_start(rows1[16:32, :], norm2_g.rearrange("l (k p) -> (l k) p", p=P)).then_inc(rows_in, 16)
            act.dma_start(rows1[32:48, :], ssd_norm_g.rearrange("l (k p) -> (l k) p", p=P)).then_inc(rows_in, 16)
            act.dma_start(rows1[48:56, :], c.rearrange("l (k p) -> (l k) p", p=P)).then_inc(rows_in, 16)
            act.dma_start(rows1[56:64, :], c_ctx.rearrange("(k p) -> k p", p=P)).then_inc(rows_in, 16)
            nct = CONV_CH // P
            act.dma_start(rows2[0:3 * nct, :], conv_w[0].rearrange("t (k p) -> (t k) p", p=P)).then_inc(rows_in, 16)
            act.dma_start(rows2[3 * nct:4 * nct, :], conv_b[0].rearrange("(k p) -> k p", p=P)).then_inc(rows_in, 16)
            act.dma_start(H[:, 0:CT, :], ctx_tok[0].rearrange("(t p) d -> p t d", p=P)).then_inc(tokens_in, 16)
            act.dma_start(H[:, CT:T, :], x[0].rearrange("(t p) d -> p t d", p=P)).then_inc(tokens_in, 16)
            for dst, src in ((qg_b[:, :], q_g[0]), (kg_b[:, :], k_g[0]), (dskip_b[:, :], d_skip[0]),
                             (dtb_b[:, 0:SH], dt_bias_f[0]), (dtb_b[:, SH:2 * SH], dt_bias_b[0]),
                             (alog_b[:, 0:SH], a_log_f[0]), (alog_b[:, SH:2 * SH], a_log_b[0])):
                act.dma_start(dst, src.partition_broadcast(P)).then_inc(params_in, 16)
            act.dma_start(rout[:, :, :], router[0].rearrange("(k p) e -> p k e", p=P)).then_inc(params_in, 16)
            act.dma_start(w_dt[:, :, :], ssd_w_in[0][:, INNER + CONV_CH:INNER + CONV_CH + 2 * SH]
                          .rearrange("(k p) e -> p k e", p=P)).then_inc(params_in, 16)

            act.wait_ge(cols_ready, 1)
            act.wait_ge(zeroed, 1)
            nc.scalar.activation(cstat[:, :, 0:2].rearrange("p k v -> p v k"),
                                 cols1[:, 48:64].rearrange("p (v k) -> p v k", v=2), ACT.Silu).then_inc(csil_ready, 1)

            def modb_copies(l):
                stage = "mod1" if l else "mod0t"
                if l:
                    act.wait_ge(h_ready, 2 * T)
                i = 0
                for gate in range(2):
                    for v in range(2 - l):
                        for uu in range(2):
                            g = a0[stage] + i
                            i += 1
                            act.wait_ge(a_full, g + 1)
                            nc.scalar.activation(modb[:, 2 * gate + v, uu * N:uu * N + N], a_bank(g), ACT.Copy)\
                                .then_inc(a_free, 1)

            def norm_act(n):
                l, which = n // 2, n % 2
                tiles = NTILES[n]
                aT = aTs[min(n, 3)]
                act.wait_ge(zeroed, 3)
                nc.scalar.activation(stat[:, 62:63], ones[:, 0:1], ACT.Sqrt)
                if n == 0:
                    act.wait_ge(tokens_in, 32)
                for i, t in enumerate(tiles):
                    if n:
                        act.wait_ge(h_ready, H_DONE[n] + i + 1)
                    nc.scalar.activation(aT_scratch, H[:, t, :], ACT.Square, accum_out=stat[:, t:t + 1]).then_inc(sumsq_ready, 1)
                    act.wait_ge(sumsq_ready, sq_done[n] + i + 1)
                if n == 4:
                    act.wait_ge(meansq_ready, n + 1)
                    nc.scalar.activation(stat[:, 8 + tiles[0]:8 + T], stat[:, 4 + tiles[0]:4 + T], ACT.Sqrt).then_inc(rms_ready, 1)
                    return
                act.wait_ge(meansq_ready, n + 1)
                nc.scalar.activation(stat[:, 8 + tiles[0]:8 + T], stat[:, 4 + tiles[0]:4 + T], ACT.Sqrt).then_inc(rms_ready, 1)
                act.wait_ge(modc_ready, (1, 2, 3, 3)[n])
                for i in range(4):
                    k = 2 * i + 1
                    g = a0[f"norm{n}"] + i
                    act.wait_ge(a_full, g + 1)
                    if tiles[0] == 0:
                        nc.scalar.activation(aT[:, k, 0:CTX], a_bank(g)[:, 0:CTX], ACT.Identity,
                                             scale=gcol[:, which, k, 1:2], bias=modc[:, 24 * which + k, 1:2])
                    nc.scalar.activation(aT[:, k, NTOK - SEQ - aOff[n]:NTOK - aOff[n]], a_bank(g)[:, CTX:NTOK], ACT.Identity,
                                         scale=gcol[:, which, k, 0:1], bias=modc[:, 24 * which + k, 0:1])\
                        .then_inc(a_free, 1)

            aT_scratch = AR[:, 19456:20480]
            norm_act(0)

            for i in range(3 * T):
                t, cc = i // 3, i % 3
                g = a0["qkv"] + i
                act.wait_ge(a_full, g + 1)
                if cc < 2:
                    nc.scalar.activation(qk[:, t, cc * N:cc * N + N], a_bank(g), ACT.Copy).then_inc(a_free, 1)
                else:
                    nc.scalar.activation(qk[:, t, 2 * N:QKW], a_bank(g)[:, 0:QKW - 2 * N], ACT.Copy)
                    nc.scalar.activation(vv[:, t, :], a_bank(g)[:, QKW - 2 * N:N], ACT.Copy).then_inc(a_free, 1)
                if cc == 2:
                    act.wait_ge(qsq_ready, t + 1)
                    nc.scalar.activation(stat[:, 36:46], stat[:, 26:36], ACT.Sqrt).then_inc(qrms_ready, 1)
            for i in range(3 * T):
                t, cc = i // 3, i % 3
                g = a0["qkT"] + i
                act.wait_ge(a_full, g + 1)
                if cc < 2:
                    nc.scalar.activation(qT[:, 4 * cc:4 * cc + 4, t * P:t * P + P],
                                         a_bank(g).rearrange("p (h q) -> p h q", h=4), ACT.Copy).then_inc(a_free, 1)
                else:
                    nc.scalar.activation(kT[:, :, t * P:t * P + P],
                                         a_bank(g)[:, 0:NKV * P].rearrange("p (h q) -> p h q", h=NKV), ACT.Copy)\
                        .then_inc(a_free, 1)
            for kind, m in TSEQ:
                if kind == "S":
                    t, _, _, nk = pair(m)
                    act.wait_ge(nmax_ready, m + 1)
                    if m >= 8:
                        act.wait_ge(p_used, m - 7)
                    nc.scalar.activation(pbuf[:, m % 8, 0:nk * P], a_bank(att_a[kind, m])[:, 0:nk * P], ACT.Exp,
                                         bias=stat[:, 16 + m % 4:17 + m % 4], accum_out=stat[:, 20 + m % 4:21 + m % 4])\
                        .then_inc(p_exp, 1)
                    act.wait_ge(p_exp, m + 1)
                    act.sem_inc(a_free, 1)
                elif kind == "O":
                    t, g = m // NKV, m % NKV
                    act.wait_ge(a_full, att_a[kind, m] + 1)
                    nc.scalar.activation(oT[:, QG * g:QG * g + QG, t * P:t * P + P],
                                         a_bank(att_a[kind, m]).rearrange("p (h q) -> p h q", h=QG), ACT.Copy)\
                        .then_inc(a_free, 1)
            modb_copies(0)
            norm_act(1)
            dve_half = v0["norm1"] + 4
            act.wait_ge(v_free, dve_half)
            act.wait_ge(a_free, a0["norm1"] + 4)
            for q in range(4):
                nc.scalar.activation(a_hi[:, 2 * q:2 * q + 2, :], aT[:, 2 * q:2 * q + 2, :], ACT.Copy).then_inc(ahi_ready, 1)
            act.sem_inc(fa_free, 2)

            def round_weights(v, ip, p):
                act.wait_ge(*f_landed(v, ip, p))
                act.wait_ge(*half_used(v - FSL, 2 * ip + p))
                slot = f_slot(v, p)
                nc.scalar.activation(f_hi[:, slot, :], f_raw[:, slot, :], ACT.Copy).then_inc(fhi_ready, 1)

            def gate(ft, i):
                act.wait_ge(fa_full, 2 + ft + 1 + 4 * i)
                nc.scalar.activation(hT[:, ft, :], PS[:, 4 + ft % 2, :], ACT.Silu).then_inc(fa_free, 1)

            def round_hidden(ft, i):
                act.wait_ge(v_free, v0["ffn"] + ft + 1 + NFV * i)
                nc.scalar.activation(h_hi[:, ft, :], hT[:, ft, :], ACT.Copy).then_inc(hhi_ready, 1)

            def chunk(ip, p, more):
                i = 2 * ip + p
                gate(0, i)
                round_weights(3, ip, p)
                round_hidden(0, i)
                gate(1, i)
                round_hidden(1, i)
                round_weights(4, ip, p)
                round_weights(5, ip, p)
                gate(2, i)
                round_hidden(2, i)
                gate(3, i)
                round_hidden(3, i)
                if more:
                    for v in range(NFH, NFH + 3):
                        round_weights(v, ip, p)

            act.wait_ge(fa_full, 2)
            for v in range(3):
                round_weights(v, 0, 0)
            with act.Fori(0, FC // 2) as ip:
                chunk(ip, 0, True)
                chunk(ip, 1, True)
            chunk(FC // 2, 0, False)
            def round_scan(h):
                act.wait_ge(s_in[h % 3], 16 * (h // 3 + 1))
                if h >= 3:
                    act.wait_ge(*scan_used(h - 3))
                nc.scalar.activation(s_hi[:, h % 3, :], s_raw[:, h % 3, :], ACT.Copy).then_inc(shi_ready, 1)

            modb_copies(1)
            act.wait_ge(v_full, v0["mod1"])
            round_scan(0)
            norm_act(2)
            act.wait_ge(v_free, v0["norm2"] + 4)
            act.wait_ge(a_free, a0["norm2"] + 4)
            for q in range(4):
                nc.scalar.activation(a_hi[:, 2 * q:2 * q + 2, :], aT[:, 2 * q:2 * q + 2, :], ACT.Copy).then_inc(ahi_ready, 1)
            round_scan(1)
            act.wait_ge(ahi_ready, 8)
            nc.scalar.activation(a_hi_lat[:, :, :], a_hi[:, :, CTX:NTOK].bitcast(F32), ACT.Copy).then_inc(a_lat_ready, 1)
            round_scan(2)

            act.wait_ge(params_in, 16 * 9)
            nc.scalar.activation(alog_b[:, :], alog_b[:, :], ACT.Exp).then_inc(alog_ready, 1)
            act.wait_ge(sp_in, 1)
            nc.scalar.activation(sp_u, sp_a, ACT.Exp).then_inc(sp_exp, 1)

            def silu_conv(ct):
                act.wait_ge(conv_ready, ct + 1)
                if ct < NXB:
                    if ct >= 2:
                        act.wait_ge(v_full, v0["xbc"] + ct - 1)
                    nc.scalar.activation(convs[:, ct % 2, :], conv[:, ct % 2, :], ACT.Silu).then_inc(convs_ready, 1)
                    if ct >= INNER // P:
                        act.wait_ge(convs_ready, ct + 1)
                        nc.scalar.activation(bT[:, ct - INNER // P, :], convs[:, ct % 2, CTX:NTOK], ACT.Copy).then_inc(bT_ready, 1)
                else:
                    nc.scalar.activation(cT[:, ct - NXB, :], conv[:, ct % 2, CTX:NTOK], ACT.Silu).then_inc(bT_ready, 1)

            act.wait_ge(pads_ready, 4)
            for ct in range(NCT):
                g = a0["xbc"] + ct
                if ct >= 1:
                    silu_conv(ct - 1)
                act.wait_ge(a_full, g + 1)
                if ct >= 2:
                    act.wait_ge(conv_ready, ct - 1)
                if ct < NXB:
                    ins = nc.scalar.activation(raw[:, ct % 2, :, 1:CTX + 1],
                                               a_bank(g).rearrange("p (s n) -> p s n", s=2), ACT.Copy)
                else:
                    ins = nc.scalar.activation(raw[:, ct % 2, 1, 1:CTX + 1], a_bank(g)[:, CTX:NTOK], ACT.Copy)
                ins.then_inc(a_free, 1)
                if ct % 2 == 0 and ct >= 2:
                    round_scan(ct // 2 + 2)
            silu_conv(NCT - 1)
            round_scan(NSX + 2)
            g = a0["dec"]
            act.wait_ge(a_full, g + 1)
            nc.scalar.activation(ex[:, :], a_bank(g)[:, 0:384], ACT.Exp).then_inc(a_free, 1)
            for i in range(LT * INNER // N):
                u, tt = i // LT, i % LT
                g = a0["z"] + i
                if i == 0:
                    round_scan(NSX + 3)
                act.wait_ge(a_full, g + 1)
                nc.scalar.activation(zs[:, tt, u * N:u * N + N], a_bank(g), ACT.Silu).then_inc(a_free, 1)
                if tt == LT - 1 and NSX + 2 * u + 5 < NSX + NSZ:
                    round_scan(NSX + 2 * u + 4)
                    round_scan(NSX + 2 * u + 5)
            for i in range(2 * SG):
                d, gg = i // SG, i % SG
                g = a0["st"] + i
                act.wait_ge(a_full, g + 1)
                nc.scalar.activation(hs[d][0][:, gg * N:gg * N + N], a_bank(g), ACT.Copy).then_inc(a_free, 1)
            def square_group(it):
                act.wait_ge(y_sum, it + 1)
                step(nc.scalar.activation(spare[:, 0:N], yacc[:, it // SG, it % SG * N:it % SG * N + N], ACT.Square,
                                          accum_out=stat[:, it:it + 1]))
                if it % SG == SG - 1:
                    act.sem_inc(y_sq, 1)

            def y_root(tt):
                act.wait_ge(y_ms, tt + 1)
                nc.scalar.activation(stat[:, 16 + SG * tt:16 + SG * tt + SG], stat[:, 8 + SG * tt:8 + SG * tt + SG], ACT.Sqrt)\
                    .then_inc(y_rms, 1)

            for i in range(4 * LT * SG):
                it, d, hf = i // 4, i // 2 % 2, i % 2
                g = a0["seg"] + i
                act.wait_ge(a_full, g + 1)
                if it >= 2:
                    act.wait_ge(v_full, v0["ydiag"] + it - 1)
                nc.scalar.activation(mm[it % 2][:, d, 4 * hf:4 * hf + 4, :], a_bank(g).rearrange("p (h l) -> p h l", h=4),
                                     ACT.Exp).then_inc(a_free, 1)
                if i % 4 == 3 and it >= 2:
                    square_group(it - 2)
                if i % 4 == 3 and it == SG + 2:
                    y_root(0)
            square_group(LT * SG - 2)
            square_group(LT * SG - 1)
            y_root(1)

            def round_half(v, j):
                act.wait_ge(moe_in[v % RS], 16 * (v // RS + 1) + 16 * (NHU // RS) * j)
                act.wait_ge(moe_free, v - HS_ + 1 + RS + NHU * j)
                nc.scalar.activation(m_hi[:, v % HS_, :], m_raw[:, v % RS, :], ACT.Copy).then_inc(moe_hi, 1)

            for v in range(LEAD):
                round_half(v, 0)
            norm_act(3)
            act.wait_ge(mask_ready, 1)
            act.dma_start(fin_g, final_g.partition_broadcast(P)).then_inc(fin_in, 16)
            act.wait_ge(gap_ready, 1)
            nc.scalar.activation(tabf[:, 2:4], tabf[:, 0:2], ACT.Exp).then_inc(gap_exp, 1)
            def fetch(i, bank, g):
                act.wait_ge(ma_full, g)
                for k4 in range(4):
                    k = 4 * i + k4
                    ins = nc.scalar.activation(xe[:, k, :], bank[:, k4 * P:k4 * P + P], ACT.Identity,
                                               scale=gcol[:, 1, k, 0:1], bias=modc[:, 24 + k, 0:1])
                ins.then_inc(ma_free, 1)

            def round_tokens(free):
                act.wait_ge(ma_free, free)
                nc.scalar.activation(xe_hi[:, :, :], xe, ACT.Copy).then_inc(xhi_ready, 1)

            act.sem_inc(ma_free, 2)
            for i in range(2):
                fetch(i, PS[:, 3 + i, :], i + 1)
            round_tokens(4)
            act.wait_ge(tables_ready, 1)
            last_job = act.value_load(tabi[0:1, EXTRA + 1:EXTRA + 2], min_val=NE - 1, max_val=NJ - 1)

            def job(j, more):
                for it in MSEQ:
                    kind, cc = it
                    if kind in "GUD":
                        for half in range(2):
                            v = 2 * m_u[it] + half + LEAD
                            if v < NHU or more:
                                round_half(v, j)
                    if kind in "GP":
                        act.wait_ge(ma_full, m_a[it] + 3 + NMA * j)
                    if kind == "X" and more:
                        if cc == 0:
                            act.wait_ge(xlo_ready, 1 + j)
                        fetch(cc, ma_bank(it), m_a[it] + 3 + NMA * j)
                        if cc == 1:
                            round_tokens(m_a[it] + 1 + 2 + 2 + NMA * j)
                    elif kind == "G":
                        if cc >= 2:
                            act.wait_ge(mv_free, m_v["U", cc - 2] + 1 + 3 + NMV * j)
                        nc.scalar.activation(sgm[:, cc % 2, :], ma_bank(it), ACT.Silu).then_inc(ma_free, 1)
                    elif kind == "P":
                        nc.scalar.activation(permT, ma_bank(it)[:, 0:LT * P], ACT.Copy).then_inc(ma_free, 1)
                    elif kind == "T":
                        act.wait_ge(mv_full, m_v[it] + 1 + NMV * j)
                        nc.scalar.activation(hT_hi[:, cc % 3, :, :], mv_bank(it).rearrange("p (k s) -> p k s", k=4),
                                             ACT.Copy).then_inc(th_ready, 1)
                act.wait_ge(down_full, 1 + j)
                for hf in range(2):
                    nc.scalar.activation(ye[:, hf * N:hf * N + N], PS[:, 6 + hf, :], ACT.Copy).then_inc(ye_ready, 1)

            with act.Fori(0, last_job) as j:
                job(j, True)
            job(last_job, False)
            norm_act(4)

        @block.vector
        def _(dve):
            steps = [0]

            def step(ins):
                steps[0] += 1
                ins.then_inc(dve_step, 1)
                dve.wait_ge(dve_step, steps[0])

            dve.wait_ge(v_full, v0["prep"] + 1)
            step(nc.vector.tensor_copy(cols1[:, :], v_bank(v0["prep"])[:, 0:64]))
            nr = 4 * CONV_CH // P
            nc.vector.tensor_copy(cols2[:, :], v_bank(v0["prep"])[:, 64:64 + nr]).then_inc(v_free, 1)
            dve.wait_ge(v_free, 1)
            dve.sem_inc(cols_ready, 1)

            def mod_columns(l, b, g):
                dve.wait_ge(v_full, g + 1)
                nc.vector.tensor_copy(modc[:, 16 * b:16 * b + 16, :],
                                      v_bank(g).rearrange("p (c v) -> p c v", v=32)[:, :, 0:2]).then_inc(v_free, 1)
                dve.wait_ge(v_free, g + 1)

            def norm_gain(l, which):
                gain = cols1[:, 16 * which + 8 * l:16 * which + 8 * l + 8]
                step(nc.vector.scalar_tensor_tensor(
                    out=gcol[:, which, :, :], in0=modc[:, 24 * which + 8:24 * which + 16, :], scalar=1.0,
                    in1=gain.unsqueeze(2).to_broadcast([P, KD, 2]), op0=ALU.add, op1=ALU.mult))

            def norm_dve(n):
                l, which = n // 2, n % 2
                tiles = NTILES[n]
                aT = aTs[min(n, 3)]
                dve.wait_ge(sumsq_ready, sq_done[n] + len(tiles))
                step(nc.vector.tensor_scalar(stat[:, 4 + tiles[0]:4 + T], stat[:, tiles[0]:T], 1.0 / D, EPS, ALU.mult, ALU.add))
                dve.sem_inc(meansq_ready, 1)
                dve.wait_ge(rms_ready, n + 1)
                step(nc.vector.reciprocal(stat[:, 12 + tiles[0]:12 + T], stat[:, 8 + tiles[0]:8 + T]))
                if n == 4:
                    return
                for t in tiles:
                    dst = xn[:, t, :] if n < 3 else y2[:, t - CT, :]
                    nc.vector.tensor_scalar(dst, H[:, t, :], stat[:, 12 + t:13 + t], None, ALU.mult).then_inc(xn_ready, 1)
                for i in range(4):
                    k = 2 * i
                    g = v0[f"norm{n}"] + i
                    dve.wait_ge(v_full, g + 1)
                    if tiles[0] == 0:
                        nc.vector.tensor_scalar(aT[:, k, 0:CTX], v_bank(g)[:, 0:CTX], gcol[:, which, k, 1:2],
                                                modc[:, 24 * which + k, 1:2], ALU.mult, ALU.add)
                    nc.vector.tensor_scalar(aT[:, k, NTOK - SEQ - aOff[n]:NTOK - aOff[n]], v_bank(g)[:, CTX:NTOK], gcol[:, which, k, 0:1],
                                            modc[:, 24 * which + k, 0:1], ALU.mult, ALU.add).then_inc(v_free, 1)

            dve.wait_ge(bias_in, 32)
            g = v0["mod0"]
            dve.wait_ge(v_full, g + 1)
            nc.vector.tensor_tensor(modr[:, 0:4, :], v_bank(g).rearrange("p (u n) -> p u n", u=4), biasr[:, 0:4, :],
                                    ALU.add).then_inc(v_free, 1)
            dve.wait_ge(v_free, g + 1)
            dve.sem_inc(modr_ready, 1)
            mod_columns(0, 0, g + 1)
            norm_gain(0, 0)
            dve.sem_inc(modc_ready, 1)
            dve.wait_ge(tokens_in, 32)
            norm_dve(0)
            dve.wait_ge(params_in, 16 * 9)
            step(nc.vector.tensor_scalar(qg_b[:, :], qg_b[:, :], float(HD) ** -0.5, None, ALU.mult))
            for t in range(T):
                dve.wait_ge(a_free, a0["qkv"] + 3 * t + 3)
                q3 = qk[:, t, :].rearrange("p (h d) -> p h d", d=HD)
                step(nc.vector.tensor_tensor(sq_t, q3, q3, ALU.mult))
                step(nc.vector.tensor_reduce(stat[:, 46:56], sq_t, AX.X, ALU.add))
                step(nc.vector.tensor_scalar(stat[:, 26:36], stat[:, 46:56], 1.0 / HD, EPS, ALU.mult, ALU.add))
                dve.sem_inc(qsq_ready, 1)
                dve.wait_ge(qrms_ready, t + 1)
                step(nc.vector.reciprocal(stat[:, 46:56], stat[:, 36:46]))
                step(nc.vector.tensor_tensor(q3, q3, stat[:, 46:56].unsqueeze(2).to_broadcast([P, 10, HD]), ALU.mult))
                nc.vector.tensor_tensor(q3[:, NH:10, :], q3[:, NH:10, :],
                                        kg_b[:, :].unsqueeze(1).to_broadcast([P, NKV, HD]), ALU.mult)
                step(nc.vector.tensor_tensor(q3[:, 0:NH, :], q3[:, 0:NH, :],
                                             qg_b[:, :].unsqueeze(1).to_broadcast([P, NH, HD]), ALU.mult))
                if t >= CT:
                    tt = t - CT
                    half = HD // 4
                    q5 = qk[:, t, :].rearrange("p (h a b i) -> p h a b i", a=2, b=2, i=half)
                    r5 = rope_t.rearrange("p h (a b i) -> p h a b i", a=2, b=2, i=half)
                    s4 = rope_s[:, tt, :].rearrange("p (a b i) -> p a b i", a=2, b=2)
                    for b in range(2):
                        for a in range(2):
                            last = nc.vector.tensor_tensor(
                                r5[:, :, a, b, :], q5[:, :, a, 1 - b, :],
                                s4[:, a, b, :].unsqueeze(1).to_broadcast([P, 10, half]), ALU.mult)
                    step(last)
                    step(nc.vector.tensor_tensor(q3, q3, rope_c[:, tt, :].unsqueeze(1).to_broadcast([P, 10, HD]), ALU.mult))
                    step(nc.vector.tensor_tensor(q3, q3, rope_t, ALU.add))
                dve.sem_inc(qk_ready, 1)

            def normalise(m):
                dve.wait_ge(p_exp, m + 1)
                nk = pair(m)[3]
                step(nc.vector.reciprocal(stat[:, 56 + m % 4:57 + m % 4], stat[:, 20 + m % 4:21 + m % 4]))
                nc.vector.tensor_scalar(pbuf[:, m % 8, 0:nk * P], pbuf[:, m % 8, 0:nk * P],
                                        stat[:, 56 + m % 4:57 + m % 4], None, ALU.mult).then_inc(p_norm, 1)

            for kind, m in TSEQ:
                if kind == "S":
                    if m >= 3:
                        normalise(m - 3)
                    nk = pair(m)[3]
                    dve.wait_ge(a_full, att_a[kind, m] + 1)
                    nc.vector.tensor_reduce(stat[:, 16 + m % 4:17 + m % 4], a_bank(att_a[kind, m])[:, 0:nk * P],
                                            AX.X, ALU.max, negate=True).then_inc(nmax_ready, 1)
                elif kind == "M":
                    dve.wait_ge(v_full, att_v[kind, m] + 1)
                    nc.vector.tensor_tensor(modr[:, m, :], v_bank(att_v[kind, m])[:, 0:P], biasr[:, m, :], ALU.add)\
                        .then_inc(v_free, 1)
                    dve.wait_ge(v_free, att_v[kind, m] + 1)
                    dve.sem_inc(modr_ready, 1)
                elif kind == "T":
                    if m >= NPAIR - 3:
                        normalise(m)
                    nk = pair(m)[3]
                    b, hh = m // QG, m % QG
                    dve.wait_ge(v_full, att_v[kind, m] + 1)
                    if b >= 2:
                        dve.wait_ge(a_full, att_a["O", b - 2] + 1)
                    nc.vector.tensor_copy(pT[:, b % 2, 0:nk, hh * P:hh * P + P],
                                          v_bank(att_v[kind, m])[:, 0:nk * P].rearrange("p (k q) -> p k q", k=nk))\
                        .then_inc(v_free, 1)

            def residual(g, t, hf, gate, at=0, ring=(v_full, v_free, v_bank)):
                full, free, bank = ring
                v = 1 if t < CT else 0
                tmp = AR[:, at:at + N] if g % 2 else AR[:, at + N:at + 2 * N]
                dve.wait_ge(full, g + 1)
                nc.vector.tensor_tensor(tmp, bank(g), modb[:, 2 * gate + v, hf * N:hf * N + N], ALU.mult).then_inc(free, 1)
                dve.wait_ge(free, g + 1)
                return nc.vector.tensor_tensor(H[:, t, hf * N:hf * N + N], H[:, t, hf * N:hf * N + N], tmp, ALU.add)

            for b in range(2):
                mod_columns(0, 1 + b, v0["mod0t"] + b)
            norm_gain(0, 1)
            dve.sem_inc(modc_ready, 1)
            dve.wait_ge(a_free, a0["mod0t"] + 8)
            for i in range(2 * T):
                t, hf = i // 2, i % 2
                ins = residual(v0["wo"] + i, t, hf, 0)
                if hf:
                    ins.then_inc(h_ready, 1)
            dve.wait_ge(h_ready, T)
            norm_dve(1)
            step(nc.vector.memset(facc, 0.0))
            for q in range(4):
                dve.wait_ge(ahi_ready, q + 1)
                nc.vector.tensor_tensor(a_lo[:, 2 * q:2 * q + 2, :], aT[:, 2 * q:2 * q + 2, :],
                                        a_hi[:, 2 * q:2 * q + 2, :].bitcast(F32), ALU.subtract).then_inc(alo_ready, 1)

            def rest_weights(v, ip, p):
                dve.wait_ge(fhi_ready, v + 1 + NFH * (2 * ip + p))
                slot = f_slot(v, p)
                nc.vector.tensor_tensor(f_lo[:, slot, :], f_raw[:, slot, :], f_hi[:, slot, :].bitcast(F32), ALU.subtract)\
                    .then_inc(flo_ready, 1)

            def hidden(ft, i):
                g = v0["ffn"] + ft
                dve.wait_ge(fa_free, 2 + ft + 1 + 4 * i)
                dve.wait_ge(v_full, g + 1 + NFV * i)
                nc.vector.tensor_tensor(hT[:, ft, :], hT[:, ft, :], v_bank(g), ALU.mult).then_inc(v_free, 1)

            def rest_hidden(ft, i):
                dve.wait_ge(hhi_ready, ft + 1 + 4 * i)
                nc.vector.tensor_tensor(h_lo[:, ft, :], hT[:, ft, :], h_hi[:, ft, :].bitcast(F32), ALU.subtract).then_inc(hlo_ready, 1)

            def add_down(half, js, i):
                for j in js:
                    t, hf = j // 2, j % 2
                    g = v0["ffn"] + 4 + 2 * T * half + j
                    dve.wait_ge(v_full, g + 1 + NFV * i)
                    f = facc[:, t, hf * N:hf * N + N]
                    nc.vector.tensor_tensor(f, f, v_bank(g), ALU.add).then_inc(v_free, 1)

            def last_down():
                for t in range(T):
                    add_down(1, (2 * t, 2 * t + 1), FC - 1)
                    dve.wait_ge(v_free, v0["ffn"] + NFV * (FC - 1) + 4 + 2 * T + 2 * t + 2)
                    if t < CT:
                        dve.sem_inc(facc_done, 1)
                    else:
                        step(nc.vector.tensor_tensor(facc[:, t, :], facc[:, t, :], modb[:, 2, :], ALU.mult))
                        dve.wait_ge(h_ready, T + t)
                        nc.vector.tensor_tensor(H[:, t, :], H[:, t, :], facc[:, t, :], ALU.add).then_inc(h_ready, 1)

            def chunk(ip, p, more):
                i = 2 * ip + p
                rest_weights(3, ip, p)
                hidden(0, i)
                rest_hidden(0, i)
                hidden(1, i)
                rest_hidden(1, i)
                rest_weights(4, ip, p)
                rest_weights(5, ip, p)
                hidden(2, i)
                rest_hidden(2, i)
                hidden(3, i)
                rest_hidden(3, i)
                if more:
                    rest_weights(6, ip, p)
                    dve.wait_ge(modu_used, 3 + 2 * i)
                    nc.vector.tensor_tensor(modr[:, bass.ds(2 * i, 2), :], PS[:, 6, 0:2 * P].rearrange("p (u n) -> p u n", u=2),
                                            biasr[:, bass.ds(2 * i, 2), :], ALU.add).then_inc(modu_added, 1)
                add_down(0, range(T), i)
                if more:
                    rest_weights(7, ip, p)
                add_down(0, range(T, 2 * T), i)
                if more:
                    add_down(1, range(2 * T), i)
                    rest_weights(8, ip, p)
                else:
                    last_down()

            dve.wait_ge(bias_in, 64)
            for v in range(3):
                rest_weights(v, 0, 0)
            with dve.Fori(0, FC // 2) as ip:
                chunk(ip, 0, True)
                chunk(ip, 1, True)
            chunk(FC // 2, 0, False)
            for b in range(3):
                mod_columns(1, b, v0["mod1"] + b)
            norm_gain(1, 0)
            norm_gain(1, 1)
            dve.sem_inc(modc_ready, 1)

            def rest_scan(h):
                dve.wait_ge(shi_ready, h + 1)
                nc.vector.tensor_tensor(s_lo[:, h % 3, :], s_raw[:, h % 3, :], s_hi[:, h % 3, :].bitcast(F32), ALU.subtract)\
                    .then_inc(slo_ready, 1)

            rest_scan(0)
            norm_dve(2)

            g = v0["dt"]
            dve.wait_ge(v_full, g + 1)
            nc.vector.tensor_tensor(dt_[:, :, :], v_bank(g)[:, 0:T * 2 * SH].rearrange("p (t h) -> p t h", t=T),
                                    dtb_b[:, :].unsqueeze(1).to_broadcast([P, T, 2 * SH]), ALU.add).then_inc(v_free, 1)
            for q in range(4):
                dve.wait_ge(ahi_ready, 4 + q + 1)
                nc.vector.tensor_tensor(a_lo[:, 2 * q:2 * q + 2, :], aT[:, 2 * q:2 * q + 2, :],
                                        a_hi[:, 2 * q:2 * q + 2, :].bitcast(F32), ALU.subtract).then_inc(alo_ready, 1)
            rest_scan(1)
            rest_scan(2)
            dve.wait_ge(v_free, g + 1)
            dtf = dt_[:, :, :].rearrange("p t h -> p (t h)")
            nc.vector.scalar_tensor_tensor(out=sp_a, in0=dtf, scalar=-1.0, in1=dtf, op0=ALU.mult, op1=ALU.min).then_inc(sp_in, 1)
            dve.wait_ge(sp_exp, 1)
            step(nc.vector.tensor_scalar(sp_a, sp_u, 2.0, None, ALU.add))
            step(nc.vector.reciprocal(sp_a, sp_a))
            step(nc.vector.tensor_tensor(sp_u, sp_u, sp_a, ALU.mult))
            step(nc.vector.tensor_tensor(sp_a, sp_u, sp_u, ALU.mult))
            step(nc.vector.tensor_scalar(sp_s, sp_a, 1.0 / 17.0, None, ALU.mult))
            for k in range(7, 0, -1):
                step(nc.vector.scalar_tensor_tensor(out=sp_s, in0=sp_s, scalar=1.0 / (2 * k + 1), in1=sp_a,
                                                    op0=ALU.add, op1=ALU.mult))
            step(nc.vector.scalar_tensor_tensor(out=sp_s, in0=sp_s, scalar=1.0, in1=sp_u, op0=ALU.add, op1=ALU.mult))
            step(nc.vector.tensor_scalar(sp_a, dtf, 0.0, None, ALU.max))
            step(nc.vector.scalar_tensor_tensor(out=dtf, in0=sp_s, scalar=2.0, in1=sp_a, op0=ALU.mult, op1=ALU.add))
            dve.wait_ge(alog_ready, 1)
            nc.vector.scalar_tensor_tensor(out=da[:, :, :], in0=dt_[:, :, :], scalar=-1.0,
                                           in1=alog_b[:, :].unsqueeze(1).to_broadcast([P, T, 2 * SH]),
                                           op0=ALU.mult, op1=ALU.mult).then_inc(da_ready, 1)

            def channels_out(ct):
                g = v0["xbc"] + ct
                dve.wait_ge(v_full, g + 1)
                dst = xt[:, :, ct * P:ct * P + P] if ct < INNER // P else btok[:, :, ct * P - INNER:ct * P - INNER + P]
                nc.vector.tensor_copy(dst, v_bank(g).rearrange("p (t c) -> p t c", t=T)).then_inc(v_free, 1)

            for ct in range(NCT):
                dve.wait_ge(a_free, a0["xbc"] + ct + 1)
                if 2 <= ct <= NXB + 1:
                    dve.wait_ge(convs_ready, ct - 1)
                elif ct > NXB + 1:
                    dve.wait_ge(bT_ready, ct - 1 - INNER // P)
                lo = 0 if ct < NXB else 1
                dst = conv[:, ct % 2, :].rearrange("p (s n) -> p s n", s=2)[:, lo:, :]
                src = raw[:, ct % 2, lo:, :]

                def w_col(k):
                    return cols2[:, k * NCT + ct:k * NCT + ct + 1]
                step(nc.vector.tensor_scalar(dst, src[:, :, 0:CTX], w_col(0), w_col(3), ALU.mult, ALU.add))
                step(nc.vector.scalar_tensor_tensor(out=dst, in0=src[:, :, 1:CTX + 1], scalar=w_col(1), in1=dst,
                                                    op0=ALU.mult, op1=ALU.add))
                nc.vector.scalar_tensor_tensor(out=dst, in0=src[:, :, 2:CTX + 2], scalar=w_col(2), in1=dst,
                                               op0=ALU.mult, op1=ALU.add).then_inc(conv_ready, 1)
                if 2 <= ct <= NXB + 1:
                    channels_out(ct - 2)
                if ct % 2 == 0 and ct >= 2:
                    rest_scan(ct // 2 + 2)
            rest_scan(NSX + 2)
            dve.wait_ge(a_free, a0["dec"] + 1)
            step(nc.vector.tensor_tensor(wsc[:, 0:128], ex[:, 128:256], dt_[:, 0:CT, :].rearrange("p t h -> p (t h)"), ALU.mult))
            step(nc.vector.tensor_tensor(wsc[:, 128:160], ex[:, 256:288], dt_[:, CT, 0:SH], ALU.mult))
            step(nc.vector.tensor_tensor(wsc[:, 160:192], ex[:, 288:320], dt_[:, CT + 1, SH:2 * SH], ALU.mult))

            def weigh(q):
                d = (0, 0, 1, 1, 0, 1)[q]
                t = (0, 1, 0, 1, CT, CT + 1)[q]
                w = wsc[:, 64 * t + SH * d:64 * t + SH * d + SH] if q < 4 else wsc[:, 32 * q:32 * q + SH]
                if q in (2, 4):
                    dve.wait_ge(xw_used, q // 2)
                if q in (3, 5):
                    dve.wait_ge(a_full, a0["st"] + SG * (q // 2))
                nc.vector.tensor_tensor(heads(xw[:, q % 2, :]), heads(xt[:, t, :]), by_head(w), ALU.mult).then_inc(xw_ready, 1)

            dve.wait_ge(bT_ready, 2 * SG)
            weigh(0)
            rest_scan(NSX + 3)
            weigh(1)
            for h in range(NSX + 4, NSX + NSZ):
                rest_scan(h)
            for tt in range(LT):
                g = v0["cb"] + tt
                dve.wait_ge(v_full, g + 1)
                for d in range(2):
                    ins = nc.vector.tensor_tensor(cbm[:, d, tt, :, :], v_bank(g).rearrange("p (g l) -> p g l", g=SG),
                                                  (LE, GE)[d].unsqueeze(1).to_broadcast([P, SG, P]), ALU.mult)
                ins.then_inc(v_free, 1)
            for q in range(2, 6):
                weigh(q)
            dve.wait_ge(a_free, a0["st"] + 2 * SG)
            for d in range(2):
                step(nc.vector.tensor_tensor(heads(hs[d][1]), heads(hs[d][0]), by_head(ex[:, 320 + SH * d:320 + SH * d + SH]), ALU.mult))
                for gg in range(SG):
                    g = v0["st2"] + SG * d + gg
                    dve.wait_ge(v_full, g + 1)
                    part = hs[d][1][:, gg * N:gg * N + N]
                    nc.vector.tensor_tensor(part, part, v_bank(g), ALU.add).then_inc(v_free, 1)
            for i in range(2 * LT * SG):
                tt, gg, d = i // (2 * SG), i // 2 % SG, i % 2
                g = v0["yoff"] + i
                dve.wait_ge(v_full, g + 1)
                dst = yacc[:, tt, gg * N:gg * N + N]
                e1 = by_head(ex[:, 64 * tt + SH * d + HP * gg:64 * tt + SH * d + HP * gg + HP])
                if d == 0:
                    nc.vector.tensor_tensor(heads(dst), heads(v_bank(g)), e1, ALU.mult).then_inc(v_free, 1)
                else:
                    tmp = yoff_t[:, gg % 2, :]
                    nc.vector.tensor_tensor(heads(tmp), heads(v_bank(g)), e1, ALU.mult).then_inc(v_free, 1)
                    dve.wait_ge(v_free, g + 1)
                    step(nc.vector.tensor_tensor(dst, dst, tmp, ALU.add))

            def skip(it):
                tt, gg = it // SG, it % SG
                part = xt[:, CT + tt, gg * N:gg * N + N]
                step(nc.vector.tensor_tensor(heads(part), heads(part), by_head(dskip_b[:, HP * gg:HP * gg + HP]), ALU.mult))
                y = yacc[:, tt, gg * N:gg * N + N]
                step(nc.vector.tensor_tensor(y, y, part, ALU.add))

            def y_diag(it):
                tt, gg = it // SG, it % SG
                g = v0["ydiag"] + it
                dve.wait_ge(v_full, g + 1)
                part = yacc[:, tt, gg * N:gg * N + N]
                nc.vector.tensor_tensor(part, part, v_bank(g), ALU.add).then_inc(v_free, 1)
                dve.wait_ge(v_free, g + 1)
                nc.vector.tensor_tensor(part, part, zs[:, tt, gg * N:gg * N + N], ALU.mult).then_inc(y_sum, 1)

            def y_mean(tt):
                dve.wait_ge(y_sq, tt + 1)
                s = SG * tt
                step(nc.vector.tensor_scalar(stat[:, 8 + s:8 + s + SG], stat[:, s:s + SG], 1.0 * SG / INNER, EPS, ALU.mult, ALU.add))
                dve.sem_inc(y_ms, 1)

            def y_norm(tt):
                s = SG * tt
                dve.wait_ge(y_rms, tt + 1)
                step(nc.vector.reciprocal(stat[:, 24 + s:24 + s + SG], stat[:, 16 + s:16 + s + SG]))
                for gg in range(SG):
                    part = yacc[:, tt, gg * N:gg * N + N]
                    nc.vector.tensor_scalar(part, part, stat[:, 24 + s + gg:25 + s + gg], None, ALU.mult).then_inc(yn_ready, 1)

            def y_by_channel(tt):
                for q in range(INNER // N):
                    g = v0["gT"] + tt * (INNER // N) + q
                    dve.wait_ge(v_full, g + 1)
                    nc.vector.tensor_tensor(gT[tt][:, 4 * q:4 * q + 4, :], v_bank(g).rearrange("p (k l) -> p k l", k=4),
                                            cols1[:, 32 + 4 * q:36 + 4 * q].unsqueeze(2).to_broadcast([P, 4, P]),
                                            ALU.mult).then_inc(v_free, 1)

            dve.wait_ge(xdt_ready, 2 * LT)
            for it in range(LT * SG):
                tt, gg = it // SG, it % SG
                for d in range(2):
                    dve.wait_ge(a_free, a0["seg"] + 4 * it + 2 * d + 2)
                    m_ = mm[it % 2][:, d, :, :]
                    nc.vector.tensor_tensor(m_, m_, cbm[:, d, tt, gg, :].unsqueeze(1).to_broadcast([P, HP, P]), ALU.mult)\
                        .then_inc(m_ready, 1)
                if it >= 1:
                    y_diag(it - 1)
                if it == SG + 2:
                    y_mean(0)
                if it == SG + 3:
                    y_norm(0)
                skip(it)
            y_diag(LT * SG - 1)
            y_by_channel(0)
            y_mean(1)
            y_norm(1)
            y_by_channel(1)

            def rest_half(v, j):
                dve.wait_ge(moe_hi, v + 1 + NHU * j)
                nc.vector.tensor_tensor(m_lo[:, v % RS, :], m_raw[:, v % RS, :], m_hi[:, v % HS_, :].bitcast(F32), ALU.subtract)\
                    .then_inc(moe_lo, 1)

            for v in range(LEAD - 1):
                rest_half(v, 0)
            dve.wait_ge(a_free, a0["mod1"] + 4)
            for i in range(2 * LT):
                tt, hf = i // 2, i % 2
                ins = residual(a0["sout"] + i, CT + tt, hf, 0, 16384, (a_full, a_free, a_bank))
                if hf:
                    ins.then_inc(h_ready, 1)
                if i == 1:
                    rest_half(LEAD - 1, 0)
            dve.wait_ge(h_ready, 2 * T + LT)
            norm_dve(3)

            g = v0["route"]
            dve.wait_ge(v_full, g + 1)

            def rts(i, n=2):
                return rt[:, i:i + n, :]
            def find_tokens(j):
                for tt in range(LT):
                    nc.vector.tensor_scalar(perm[:, tt, :], iota1, rankj[:, tt, bass.ds(j, 1)], None, ALU.is_equal)\
                        .then_inc(perm_ready, 1)

            lg, eq, oh1, lg2, oh2, mask, gate, rank, r1 = (rts(2 * i) for i in range(9))
            cnt, over, cum, sel, tmp1 = (rt[:, 18 + i, :] for i in range(5))
            rev = rev_e.unsqueeze(1).to_broadcast([P, LT, NE])

            def wide(v):
                return v.unsqueeze(2).to_broadcast([P, LT, NE])
            top = tabf[:, 4:6]
            nc.vector.tensor_copy(lg, v_bank(g)[:, 0:LT * NE].rearrange("p (t e) -> p t e", t=LT)).then_inc(v_free, 1)
            dve.wait_ge(v_free, g + 1)

            def largest(x_, value, onehot):
                step(nc.vector.tensor_reduce(value, x_, AX.X, ALU.max))
                step(nc.vector.tensor_tensor(eq, x_, wide(value), ALU.is_equal))
                step(nc.vector.tensor_tensor(eq, eq, rev, ALU.mult))
                step(nc.vector.tensor_reduce(tabf[:, 6:8], eq, AX.X, ALU.max))
                step(nc.vector.tensor_tensor(onehot, eq, wide(tabf[:, 6:8]), ALU.is_equal))
            largest(lg, top, oh1)
            step(nc.vector.scalar_tensor_tensor(out=lg2, in0=oh1, scalar=-3.0e38, in1=lg, op0=ALU.mult, op1=ALU.add))
            largest(lg2, tabf[:, 2:4], oh2)
            step(nc.vector.tensor_tensor(mask, oh1, oh2, ALU.add))
            dve.sem_inc(mask_ready, 1)
            nc.vector.tensor_tensor(tabf[:, 0:2], tabf[:, 2:4], top, ALU.subtract).then_inc(gap_ready, 1)
            g = v0["route"] + 1
            dve.wait_ge(v_full, g + 1)
            step(nc.vector.tensor_scalar(rank, v_bank(g)[:, 0:LT * NE].rearrange("p (t e) -> p t e", t=LT), 1.0, None, ALU.add))
            nc.vector.tensor_copy(cnt, v_bank(g)[:, LT * NE:LT * NE + NE]).then_inc(v_free, 1)
            dve.wait_ge(v_free, g + 1)
            step(nc.vector.tensor_tensor(rankj[:, :, 0:NE], rank, mask, ALU.mult))
            find_tokens(0)
            dve.wait_ge(gap_exp, 1)
            step(nc.vector.tensor_scalar(tabf[:, 0:2], tabf[:, 2:4], 1.0, None, ALU.add))
            step(nc.vector.reciprocal(tabf[:, 0:2], tabf[:, 0:2]))
            step(nc.vector.tensor_tensor(tabf[:, 2:4], tabf[:, 2:4], tabf[:, 0:2], ALU.mult))
            step(nc.vector.tensor_tensor(oh1, oh1, wide(tabf[:, 0:2]), ALU.mult))
            step(nc.vector.tensor_tensor(oh2, oh2, wide(tabf[:, 2:4]), ALU.mult))
            step(nc.vector.tensor_tensor(gate, oh1, oh2, ALU.add))
            step(nc.vector.tensor_copy(gatej[:, :, 0:NE], gate))
            step(nc.vector.tensor_scalar(over, cnt, float(P), None, ALU.is_gt))
            step(nc.vector.tensor_copy(cum, over))
            for e in range(1, NE):
                step(nc.vector.tensor_tensor(cum[:, e:e + 1], cum[:, e:e + 1], cum[:, e - 1:e], ALU.add))
            for m in range(EXTRA):
                step(nc.vector.scalar_tensor_tensor(out=sel, in0=cum, scalar=float(m + 1), in1=over, op0=ALU.is_equal, op1=ALU.mult))
                step(nc.vector.tensor_tensor(tmp1, sel, fwd_e, ALU.mult))
                step(nc.vector.tensor_reduce(tabf[:, m:m + 1], tmp1, AX.X, ALU.add))
                for src, dst in ((rankj, rankj), (gatej, gatej)):
                    step(nc.vector.tensor_tensor(r1, src[:, :, 0:NE], sel.unsqueeze(1).to_broadcast([P, LT, NE]), ALU.mult))
                    step(nc.vector.tensor_reduce(dst[:, :, NE + m:NE + m + 1], r1, AX.X, ALU.add))
                step(nc.vector.tensor_scalar(rankj[:, :, NE + m:NE + m + 1], rankj[:, :, NE + m:NE + m + 1], float(-P), None, ALU.add))
            step(nc.vector.tensor_scalar(tabf[:, EXTRA:EXTRA + 1], cum[:, NE - 1:NE], float(NE), None, ALU.add))
            step(nc.vector.tensor_scalar(tabf[:, EXTRA + 1:EXTRA + 2], cum[:, NE - 1:NE], float(NE - 1), None, ALU.add))
            step(nc.vector.tensor_copy(tabi[:, 0:EXTRA + 2], tabf[:, 0:EXTRA + 2]))
            dve.sem_inc(tables_ready, 1)

            def rest_tokens(j):
                dve.wait_ge(xhi_ready, j + 1)
                nc.vector.tensor_tensor(xe_lo[:, :, :], xe, xe_hi[:, :, :].bitcast(F32), ALU.subtract).then_inc(xlo_ready, 1)

            def give_back(cc, bank, g):
                dve.wait_ge(mv_full, g)
                part = macc[:, cc // 2, (cc % 2) * N:(cc % 2) * N + N]
                nc.vector.tensor_tensor(part, part, bank, ALU.add).then_inc(mv_free, 1)

            dve.sem_inc(mv_free, 3)
            rest_tokens(0)

            def job(j, more):
                for tt in range(LT):
                    nc.vector.tensor_scalar(permg[:, tt, :], iota1, rankj[:, tt, bass.ds(j, 1)], gatej[:, tt, bass.ds(j, 1)],
                                            ALU.is_equal, ALU.mult).then_inc(permg_ready, 1)
                if more:
                    find_tokens(j + 1)
                for it in MSEQ:
                    kind, cc = it
                    if kind in "GUD":
                        for half in range(2):
                            v = 2 * m_u[it] + half + LEAD
                            if v < NHU or more:
                                rest_half(v, j)
                    if kind == "U":
                        dve.wait_ge(ma_free, m_a["G", cc] + 1 + 2 + 2 + NMA * j)
                        dve.wait_ge(mv_full, m_v[it] + 1 + NMV * j)
                        nc.vector.tensor_tensor(hm[:, cc % 2, :], sgm[:, cc % 2, :], mv_bank(it), ALU.mult).then_inc(mv_free, 1)
                    elif kind == "T":
                        dve.wait_ge(th_ready, cc + 1 + FC * j)
                        nc.vector.tensor_tensor(hT_lo[:, cc % 3, :, :], mv_bank(it).rearrange("p (k s) -> p k s", k=4),
                                                hT_hi[:, cc % 3, :, :].bitcast(F32), ALU.subtract).then_inc(mv_free, 1)
                    elif kind == "C":
                        give_back(cc, mv_bank(it), m_v[it] + 1 + NMV * j)
                    elif kind == "X" and cc == 1 and more:
                        rest_tokens(j + 1)

            last_job = dve.value_load(tabi[0:1, EXTRA + 1:EXTRA + 2], min_val=NE - 1, max_val=NJ - 1)
            with dve.Fori(0, last_job) as j:
                job(j, True)
            job(last_job, False)
            for i in range(2 * LT):
                give_back(i, PS[:, i % 3, :], i + 1 + NMV + NMV * last_job)
            dve.wait_ge(mv_free, 3 + 2 * LT + NMV + NMV * last_job)
            for tt in range(LT):
                step(nc.vector.tensor_tensor(macc[:, tt, :], macc[:, tt, :], modb[:, 2, :], ALU.mult))
                nc.vector.tensor_tensor(H[:, CT + tt, :], H[:, CT + tt, :], macc[:, tt, :], ALU.add).then_inc(h_ready, 1)
            norm_dve(4)
            dve.wait_ge(fin_in, 16)
            for t in range(CT, T):
                step(nc.vector.tensor_scalar(H[:, t, :], H[:, t, :], stat[:, 12 + t:13 + t], None, ALU.mult))
                nc.vector.tensor_tensor(H[:, t, :], H[:, t, :], fin_g, ALU.mult).then_inc(h_ready, 1)

        @block.tensor
        def _(pe):
            def open_v(g, shift=None):
                if shift is not None:
                    pe.wait_ge(v_free, g - 3 + shift)
                elif g >= 4:
                    pe.wait_ge(v_free, g - 3)
                return v_bank(g)

            def open_a(g, shift=None):
                if shift is not None:
                    pe.wait_ge(a_free, g - 3 + shift)
                elif g >= 4:
                    pe.wait_ge(a_free, g - 3)
                return a_bank(g)

            def unit(n):
                pe.wait_ge(unit_in[n % 3], 16 * (n // 3 + 1))
                return WR[:, n % 3, :]

            def accumulate(bank, pairs):
                for i, (a, b) in enumerate(pairs):
                    last = nc.tensor.matmul(bank, a, b, start=(i == 0), stop=(i == len(pairs) - 1))
                return last

            pe.wait_ge(rows_in, 16 * 8)
            b = open_v(0)
            nc.tensor.transpose(b[:, 0:64], rows1[:, :], ident[0:64, 0:64])
            nr = 4 * CONV_CH // P
            nc.tensor.transpose(b[:, 64:64 + nr], rows2[:, :], ident[0:nr, 0:nr]).then_inc(v_full, 1)

            def mod_products(dst, w):
                for k in range(KD):
                    for j in range(4):
                        last = nc.tensor.matmul(dst[32 * j:32 * j + 32, :], cstat[:, k, :],
                                                w[:, k, j * P:j * P + P], start=(k == 0), stop=(k == KD - 1),
                                                tile_position=(0, 32 * j), skip_group_check=True)
                return last

            def mod_columns(b, g):
                bank = open_v(g)
                for u4 in range(4):
                    last = nc.tensor.transpose(bank[:, u4 * P:u4 * P + P], modr[:, 4 * b + u4, :], ident)
                last.then_inc(v_full, 1)

            def mod_gates(l):
                i = 0
                for gate in range(2):
                    for v in range(2 - l):
                        for uu in range(2):
                            bank = open_a(a0["mod1" if l else "mod0t"] + i)
                            i += 1
                            for j in range(4):
                                pick = ident[:, 32 * j + v:32 * j + v + 1].to_broadcast([P, P])
                                last = nc.tensor.matmul(bank[:, j * P:j * P + P], pick, modr[:, 4 + 6 * gate + uu, :],
                                                        start=True, stop=True)
                            last.then_inc(a_full, 1)

            def norm_pe(n):
                tiles = NTILES[n]
                pe.wait_ge(xn_ready, sq_done[n] + len(tiles))
                for i in range(4):
                    for odd in range(2):
                        k = 2 * i + odd
                        g = (a0 if odd else v0)[f"norm{n}"] + i
                        bank = (open_a if odd else open_v)(g)
                        for t in tiles:
                            src = xn[:, t, :] if n < 3 else y2[:, t - CT, :]
                            last = nc.tensor.transpose(bank[:, t * P:t * P + P], src[:, k * P:k * P + P], ident)
                        last.then_inc(a_full if odd else v_full, 1)

            def at_ready(n):
                pe.wait_ge(v_free, v0[f"norm{n}"] + 4)
                pe.wait_ge(a_free, a0[f"norm{n}"] + 4)

            pe.wait_ge(csil_ready, 1)
            pe.wait_ge(zeroed, 3)
            bank = open_v(v0["mod0"])
            for u4 in range(4):
                n = first["mod0"] + u4
                last = mod_products(bank[:, u4 * P:u4 * P + P], unit(n).rearrange("p (k n) -> p k n", k=KD))
                if u4 < 3:
                    last.then_inc(unit_used, 1)
            last.then_inc(v_full, 1)
            pe.wait_ge(v_full, v0["mod0"] + 1)
            pe.sem_inc(unit_used, 1)
            pe.wait_ge(modr_ready, 1)
            mod_columns(0, v0["mod0"] + 1)
            norm_pe(0)
            at_ready(0)
            for i in range(3 * T):
                t, cc = i // 3, i % 3
                g = a0["qkv"] + i
                bank = open_a(g)
                w = unit(first["qkv"] + cc).rearrange("p (k n) -> p k n", k=KD)
                last = accumulate(bank, [(aT[:, k, t * P:t * P + P], w[:, k, :]) for k in range(KD)])
                last.then_inc(a_full, 1)
                if t == T - 1:
                    pe.wait_ge(a_full, g + 1)
                    pe.sem_inc(unit_used, 1)
            for i in range(3 * T):
                t, cc = i // 3, i % 3
                g = a0["qkT"] + i
                pe.wait_ge(qk_ready, t + 1)
                bank = open_a(g)
                for h in range(4 if cc < 2 else NKV):
                    last = nc.tensor.transpose(bank[:, h * P:h * P + P], qk[:, t, (4 * cc + h) * HD:(4 * cc + h + 1) * HD], ident)
                last.then_inc(a_full, 1)
            pe.wait_ge(a_free, a0["qkT"] + 3 * T)
            for kind, m in TSEQ:
                if kind == "S":
                    t, g, h, nk = pair(m)
                    bank = open_a(att_a[kind, m])
                    nc.tensor.matmul(bank[:, 0:nk * P], qT[:, h, t * P:t * P + P], kT[:, g, 0:nk * P], start=True, stop=True)\
                        .then_inc(a_full, 1)
                elif kind == "T":
                    nk = pair(m)[3]
                    bank = open_v(att_v[kind, m])
                    pe.wait_ge(p_norm, m + 1)
                    for k in range(nk):
                        last = nc.tensor.transpose(bank[:, k * P:k * P + P], pbuf[:, m % 8, k * P:k * P + P], ident)
                    last.then_inc(v_full, 1)
                    pe.wait_ge(v_full, att_v[kind, m] + 1)
                    pe.sem_inc(p_used, 1)
                elif kind == "M":
                    bank = open_v(att_v[kind, m])
                    mod_products(bank[:, 0:P], unit(first["mod0b"] + m - 4).rearrange("p (k n) -> p k n", k=KD)).then_inc(v_full, 1)
                    pe.wait_ge(v_full, att_v[kind, m] + 1)
                    pe.sem_inc(unit_used, 1)
                else:
                    t, g, _, nk = pair(QG * m)
                    bank = open_a(att_a[kind, m])
                    pe.wait_ge(v_free, att_v["T", QG * m + QG - 1] + 1)
                    last = accumulate(bank, [(vv[:, k, g * HD:g * HD + HD], pT[:, m % 2, k, :]) for k in range(nk)])
                    last.then_inc(a_full, 1)
            pe.wait_ge(modr_ready, 9)
            mod_columns(1, v0["mod0t"])
            mod_columns(2, v0["mod0t"] + 1)
            mod_gates(0)
            pe.wait_ge(a_free, a0["attn"] + n_s + n_o)
            for i in range(2 * T):
                t, hf = i // 2, i % 2
                g = v0["wo"] + i
                bank = open_v(g)
                w = unit(first["wo"] + hf).rearrange("p (k n) -> p k n", k=KD)
                last = accumulate(bank, [(oT[:, k, t * P:t * P + P], w[:, k, :]) for k in range(KD)])
                last.then_inc(v_full, 1)
                if t == T - 1:
                    pe.wait_ge(v_full, g + 1)
                    pe.sem_inc(unit_used, 1)
            norm_pe(1)
            at_ready(1)
            pe.wait_ge(alo_ready, 4)

            def three(bank, pairs, start=True, stop=True, lo_from=None):
                for i_, ((ah, al), (bh, bl)) in enumerate(pairs):
                    if lo_from is not None and i_ % 2 == 0:
                        pe.wait_ge(alo_ready, lo_from + i_ // 2 + 1)
                    nc.tensor.matmul(bank, ah, bh, start=(start and i_ == 0), stop=False)
                    nc.tensor.matmul(bank, ah, bl, start=False, stop=False)
                    last = nc.tensor.matmul(bank, al, bh, start=False, stop=(stop and i_ == len(pairs) - 1))
                return last

            def halves(slot, k):
                return (f_hi[:, slot, :].rearrange("p (k n) -> p k n", k=k), f_lo[:, slot, :].rearrange("p (k n) -> p k n", k=k))

            def hidden(slot, bank, q):
                hi, lo = halves(slot, KD)
                c_ = slice(q * P, q * P + P)
                return three(bank, [((hi[:, k, c_], lo[:, k, c_]), (a_hi[:, k, :], a_lo[:, k, :])) for k in range(KD)])

            def chunk(ip, p, more):
                i = 2 * ip + p
                for half in range(2):
                    for q in range(2):
                        ft = 2 * half + q
                        pe.wait_ge(flo_ready, 2 * half + 1 + NFH * i)
                        pe.wait_ge(fa_free, ft + 1 + 4 * i)
                        hidden(f_slot(2 * half, p), PS[:, 4 + ft % 2, :], q).then_inc(fa_full, 1)
                        pe.wait_ge(flo_ready, 2 * half + 2 + NFH * i)
                        g = v0["ffn"] + ft
                        hidden(f_slot(2 * half + 1, p), open_v(g, NFV * i), q).then_inc(v_full, 1)
                    if more:
                        pe.wait_ge(modu_in, 16 * (half + 1) + 32 * i)
                        if half == 0:
                            pe.wait_ge(modu_added, 1 + i)
                        mod_products(PS[:, 6, half * P:half * P + P], mod_unit).then_inc(modu_used, 1)
                for half in range(2):
                    hi, lo = halves(f_slot(4 + half, p), 2)
                    pe.wait_ge(flo_ready, 5 + half + NFH * i)
                    pe.wait_ge(hlo_ready, 2 + 2 * half + 4 * i)
                    for j in range(2 * T):
                        t, hf = j // 2, j % 2
                        c_ = slice(hf * N, hf * N + N)
                        r_ = slice(t * P, t * P + P)
                        bank = open_v(v0["ffn"] + 4 + 2 * T * half + j, NFV * i)
                        three(bank, [((h_hi[:, 2 * half + k, r_], h_lo[:, 2 * half + k, r_]), (hi[:, k, c_], lo[:, k, c_]))
                                     for k in range(2)]).then_inc(v_full, 1)

            pe.wait_ge(a_free, a0["norm1"] + 4)
            pe.sem_inc(modu_added, 1)
            with pe.Fori(0, FC // 2) as ip:
                chunk(ip, 0, True)
                chunk(ip, 1, True)
            chunk(FC // 2, 0, False)
            pe.wait_ge(modu_added, FC)
            for b in range(3):
                mod_columns(b, v0["mod1"] + b)
            mod_gates(1)
            norm_pe(2)
            at_ready(2)
            pe.wait_ge(params_in, 16 * 9)
            g = v0["dt"]
            bank = open_v(g)
            for t in range(T):
                last = accumulate(bank[:, t * 2 * SH:(t + 1) * 2 * SH], [(aT[:, k, t * P:t * P + P], w_dt[:, k, :]) for k in range(KD)])
            last.then_inc(v_full, 1)

            def channels(ct):
                g = v0["xbc"] + ct
                bank = open_v(g)
                pe.wait_ge(convs_ready, ct + 1)
                for t in range(T):
                    last = nc.tensor.transpose(bank[:, t * P:t * P + P], convs[:, ct % 2, t * P:t * P + P], ident)
                last.then_inc(v_full, 1)

            def scan_half(h, k):
                pe.wait_ge(slo_ready, h + 1)
                return (s_hi[:, h % 3, :].rearrange("p (k n) -> p k n", k=k), s_lo[:, h % 3, :].rearrange("p (k n) -> p k n", k=k))

            for ct in range(NCT):
                g = a0["xbc"] + ct
                hi, lo = scan_half(ct // 2, KD)
                bank = open_a(g)
                c_ = slice(ct % 2 * P, ct % 2 * P + P)
                t_ = slice(0 if ct < NXB else CTX, NTOK)
                three(bank[:, t_], [((hi[:, k, c_], lo[:, k, c_]), (a_hi[:, k, t_], a_lo[:, k, t_])) for k in range(KD)],
                      lo_from=4 if ct == 0 else None)\
                    .then_inc(a_full, 1)
                if 3 <= ct <= NXB + 2:
                    channels(ct - 3)
            g = a0["dec"]
            bank = open_a(g)
            pe.wait_ge(da_ready, 1)
            pe.wait_ge(zeroed, 3)

            def sums(o, tri, t, d, other=None):
                pairs = [(tri, da[:, t, SH * d:SH * d + SH])]
                if other is not None:
                    pairs.append((ones[:, :], da[:, other, SH * d:SH * d + SH]))
                return accumulate(bank[:, o:o + SH], pairs)
            for tt in range(LT):
                for d in range(2):
                    sums(64 * tt + SH * d, (LE, GE)[d], CT + tt, d)
            for t in range(CT):
                for d in range(2):
                    sums(128 + 64 * t + SH * d, (GTm, LTm)[d], t, d, 1 - t if t == d else None)
            for d in range(2):
                sums(256 + SH * d, (GTm, LTm)[d], CT + d, d)
            for d in range(2):
                last = sums(320 + SH * d, ones[:, :], CT + d, d)
            last.then_inc(a_full, 1)
            pe.wait_ge(a_lat_ready, 1)
            for u in range(INNER // N):
                for half in range(2):
                    hi, lo = scan_half(NSX + 2 * u + half, 4)
                    for tt in range(LT):
                        g = a0["z"] + LT * u + tt
                        bank = a_bank(g) if half else open_a(g)
                        t_ = slice(tt * P, tt * P + P)
                        tc_ = slice(CTX + tt * P, CTX + tt * P + P)
                        last = three(bank, [((a_hi_lat[:, 4 * half + k, t_], a_lo[:, 4 * half + k, tc_]), (hi[:, k, :], lo[:, k, :]))
                                            for k in range(4)], half == 0, half == 1)
                        if half:
                            last.then_inc(a_full, 1)
                    if not half:
                        last.then_inc(z_half, 1)
            pe.wait_ge(bT_ready, 2 * SG)
            for tt in range(LT):
                g = v0["cb"] + tt
                bank = open_v(g)
                for gg in range(SG):
                    last = nc.tensor.matmul(bank[:, gg * P:gg * P + P], bT[:, gg, tt * P:tt * P + P], cT[:, gg, tt * P:tt * P + P],
                                            start=True, stop=True)
                last.then_inc(v_full, 1)
            pe.wait_ge(v_free, v0["xbc"] + NXB)
            for q in range(6):
                d = (0, 0, 1, 1, 0, 1)[q]
                t = (0, 1, 0, 1, CT, CT + 1)[q]
                pe.wait_ge(xw_ready, q + 1)
                for gg in range(SG):
                    if q < 4:
                        g = a0["st"] + SG * d + gg
                        bank = open_a(g) if q % 2 == 0 else a_bank(g)
                    else:
                        g = v0["st2"] + SG * d + gg
                        bank = open_v(g)
                    last = nc.tensor.matmul(bank, btok[:, t, gg * P:gg * P + P], xw[:, q % 2, gg * N:gg * N + N],
                                            start=(q % 2 == 0 or q >= 4), stop=(q % 2 == 1 or q >= 4))
                    if q >= 4:
                        last.then_inc(v_full, 1)
                    elif q % 2:
                        last.then_inc(a_full, 1)
                if q in (0, 2):
                    last.then_inc(xw_used, 1)
            pe.wait_ge(a_free, a0["st"] + 2 * SG)
            pe.wait_ge(v_free, v0["st2"] + 2 * SG)
            for i in range(2 * LT * SG):
                tt, gg, d = i // (2 * SG), i // 2 % SG, i % 2
                g = v0["yoff"] + i
                bank = open_v(g)
                nc.tensor.matmul(bank, cT[:, gg, tt * P:tt * P + P], hs[d][tt if d == 0 else LT - 1 - tt][:, gg * N:gg * N + N],
                                 start=True, stop=True).then_inc(v_full, 1)
            pe.wait_ge(v_full, v0["yoff"] + 2 * LT * SG)
            pe.sem_inc(states_used, 1)

            def segments(it):
                for d in range(2):
                    pe.wait_ge(ld_ready, 2 * it + d + 1)
                    for hf in range(2):
                        bank = open_a(a0["seg"] + 4 * it + 2 * d + hf)
                        for h4 in range(4):
                            last = nc.tensor.matmul(bank[:, h4 * P:h4 * P + P], ld[d][:, 4 * hf + h4, :], (LE, GE)[d],
                                                    start=True, stop=True)
                        last.then_inc(a_full, 1)

            segments(0)
            pe.wait_ge(xdt_ready, 2 * LT)
            for it in range(LT * SG):
                tt, gg = it // SG, it % SG
                if it + 1 < LT * SG:
                    segments(it + 1)
                pe.wait_ge(m_ready, 2 * it + 2)
                bank = open_v(v0["ydiag"] + it)
                for h in range(HP):
                    for d in range(2):
                        o_ = (HP * gg + h) * HDIM
                        last = nc.tensor.matmul(bank[:, h * HDIM:(h + 1) * HDIM], mm[it % 2][:, d, h, :],
                                                xdt[tt][:, d, o_:o_ + HDIM], start=(d == 0), stop=(d == 1))
                last.then_inc(v_full, 1)
            def y_by_channel(tt):
                for q in range(INNER // N):
                    bank = open_v(v0["gT"] + tt * (INNER // N) + q)
                    pe.wait_ge(yn_ready, SG * tt + q + 1)
                    for k4 in range(4):
                        last = nc.tensor.transpose(bank[:, k4 * P:k4 * P + P], yacc[:, tt, (4 * q + k4) * P:(4 * q + k4 + 1) * P], ident)
                    last.then_inc(v_full, 1)
                pe.wait_ge(v_free, v0["gT"] + (tt + 1) * (INNER // N))

            nu = INNER // (4 * P)
            for u in range(nu):
                for i in range(2 * LT):
                    tt, hf = i // 2, i % 2
                    if u == 0 and hf == 0:
                        y_by_channel(tt)
                    w = unit(first["sout"] + u).rearrange("p (k n) -> p k n", k=4)
                    bank = open_a(a0["sout"] + i) if u == 0 else a_bank(a0["sout"] + i)
                    for k in range(4):
                        last = nc.tensor.matmul(bank, gT[tt][:, 4 * u + k, :], w[:, k, hf * N:hf * N + N],
                                                start=(u == 0 and k == 0), stop=(u == nu - 1 and k == 3))
                    if u == nu - 1:
                        last.then_inc(a_full, 1)
                    elif i == 2 * LT - 1:
                        if u == 0:
                            last.then_inc(unit_used, 1)
                        else:
                            last.then_inc(moe_free, 2)
            pe.wait_ge(a_full, a0["sout"] + 2 * LT)
            pe.sem_inc(moe_free, RS - 4)
            norm_pe(3)
            at_ready(3)
            bank = open_v(v0["route"])
            for tt in range(LT):
                last = accumulate(bank[:, tt * NE:(tt + 1) * NE], [(aTl[:, k, tt * P:tt * P + P], rout[:, k, :]) for k in range(KD)])
            last.then_inc(v_full, 1)
            pe.wait_ge(mask_ready, 1)
            bank = open_v(v0["route"] + 1)
            m_ = [rt[:, 10 + tt, :] for tt in range(LT)]
            accumulate(bank[:, 0:NE], [(LTm, m_[0])])
            accumulate(bank[:, NE:2 * NE], [(ones[:, :], m_[0]), (LTm, m_[1])])
            accumulate(bank[:, 2 * NE:3 * NE], [(ones[:, :], m_[0]), (ones[:, :], m_[1])]).then_inc(v_full, 1)

            pe.wait_ge(v_free, v0["end"])
            pe.wait_ge(a_free, a0["end"])
            def fetch(i, bank, n, free):
                pe.wait_ge(ma_free, free)
                pe.wait_ge(perm_ready, n)
                for k4 in range(4):
                    k = 4 * i + k4
                    last = accumulate(bank[:, k4 * P:k4 * P + P],
                                      [(y2[:, tt, k * P:k * P + P], perm[:, tt, :]) for tt in range(LT)])
                last.then_inc(ma_full, 1)

            def give_back(cc, bank, free, n):
                pe.wait_ge(mv_free, free)
                pe.wait_ge(ye_ready, n)
                hf = cc % 2
                nc.tensor.matmul(bank, permT[:, cc // 2 * P:cc // 2 * P + P], ye[:, hf * N:hf * N + N],
                                 start=True, stop=True).then_inc(mv_full, 1)

            def three_of(bank, hi, lo, w_hi, w_lo, start, stop):
                nc.tensor.matmul(bank, hi, w_hi, start=start, stop=False)
                nc.tensor.matmul(bank, hi, w_lo, start=False, stop=False)
                return nc.tensor.matmul(bank, lo, w_hi, start=False, stop=stop)

            for i in range(2):
                fetch(i, PS[:, 3 + i, :], LT, i + 1)
            pe.wait_ge(tables_ready, 1)
            last_job = pe.value_load(tabi[0:1, EXTRA + 1:EXTRA + 2], min_val=NE - 1, max_val=NJ - 1)

            def job(j, more):
                for it in MSEQ:
                    kind, cc = it
                    if kind in "GP":
                        pe.wait_ge(ma_free, m_a[it] - 1 + 4 + NMA * j)
                        bank = ma_bank(it)
                    elif kind in "UT":
                        pe.wait_ge(mv_free, m_v[it] - 2 + 3 + NMV * j)
                        bank = mv_bank(it)
                    if it == ("G", 0):
                        pe.wait_ge(xlo_ready, 1 + j)
                    if kind in "GU":
                        for half in range(2):
                            v = 2 * m_u[it] + half
                            pe.wait_ge(moe_lo, v + 1 + NHU * j)
                            hi = m_hi[:, v % HS_, :].rearrange("p (k n) -> p k n", k=4)
                            lo = m_lo[:, v % RS, :].rearrange("p (k n) -> p k n", k=4)
                            for k in range(4):
                                kk = 4 * half + k
                                last = three_of(bank, xe_hi[:, kk, :], xe_lo[:, kk, :], hi[:, k, :], lo[:, k, :],
                                             kk == 0, kk == KD - 1)
                            if half == 0:
                                last.then_inc(moe_free, 1)
                        last.then_inc(ma_full if kind == "G" else mv_full, 1)
                        pe.wait_ge(*((ma_full, m_a[it] + 3 + NMA * j) if kind == "G" else (mv_full, m_v[it] + 1 + NMV * j)))
                        pe.sem_inc(moe_free, 1)
                    elif kind == "T":
                        pe.wait_ge(mv_free, m_v["U", cc] + 1 + 3 + NMV * j)
                        for k4 in range(4):
                            last = nc.tensor.transpose(bank[:, k4 * P:k4 * P + P], hm[:, cc % 2, k4 * P:k4 * P + P], ident)
                        last.then_inc(mv_full, 1)
                    elif kind == "P":
                        pe.wait_ge(permg_ready, LT + LT * j)
                        for tt in range(LT):
                            last = nc.tensor.transpose(bank[:, tt * P:tt * P + P], permg[:, tt, :], ident)
                        last.then_inc(ma_full, 1)
                    elif kind == "D":
                        pe.wait_ge(mv_free, m_v["T", cc] + 1 + 3 + NMV * j)
                        for half in range(2):
                            v = 2 * m_u[it] + half
                            pe.wait_ge(moe_lo, v + 1 + NHU * j)
                            hi = m_hi[:, v % HS_, :].rearrange("p (k n) -> p k n", k=2)
                            lo = m_lo[:, v % RS, :].rearrange("p (k n) -> p k n", k=2)
                            for k in range(2):
                                kk = 2 * half + k
                                for hf in range(2):
                                    c_ = slice(hf * N, hf * N + N)
                                    last = three_of(PS[:, 6 + hf, :], hT_hi[:, cc % 3, kk, :], hT_lo[:, cc % 3, kk, :],
                                                 hi[:, k, c_], lo[:, k, c_], cc == 0 and kk == 0, cc == FC - 1 and kk == 3)
                            last.then_inc(moe_free, 1)
                        if cc == FC - 1:
                            pe.wait_ge(moe_free, RS + NHU + NHU * j)
                            pe.sem_inc(down_full, 1)
                    elif kind == "C":
                        give_back(cc, mv_bank(it), m_v[it] - 2 + 3 + NMV * j, 2 + 2 * j)
                    elif kind == "X" and more:
                        fetch(cc, ma_bank(it), 2 * LT + LT * j, m_a[it] - 1 + 4 + NMA * j)

            with pe.Fori(0, last_job) as j:
                job(j, True)
            job(last_job, False)
            for i in range(2 * LT):
                give_back(i, PS[:, i % 3, :], i - 2 + 3 + NMV + NMV * last_job, 4 + 2 * last_job)


_NAMES = ['x', 'c', 'ctx', 'c_ctx', 'w_mod', 'b_mod', 'norm1_g', 'norm2_g', 'attn_w_qkv', 'attn_q_g', 'attn_k_g', 'attn_w_o',
          'ssd_w_in', 'ssd_conv_w', 'ssd_conv_b', 'ssd_dt_bias_f', 'ssd_dt_bias_b', 'ssd_a_log_f', 'ssd_a_log_b',
          'ssd_d_skip', 'ssd_norm_g', 'ssd_w_out', 'ffn_w_gate', 'ffn_w_up', 'ffn_w_down', 'moe_router',
          'moe_w_gate', 'moe_w_up', 'moe_w_down', 'final_g']


def kernel(**inputs):
    import concourse.bacc as _bacc
    from concourse.bass_utils import run_bass_kernel_spmd as _run

    nc = _bacc.Bacc("TRN2", target_bir_lowering=False, num_devices=1)
    seq = inputs['x'].shape[1]
    arrays = {"consts": constants(seq, 64, inputs['attn_q_g'].shape[1], inputs['moe_router'].shape[2])}
    for name in _NAMES:
        arrays[f"in_{name}"] = np.ascontiguousarray(inputs[name])
    args = [nc.dram_tensor(n, a.shape, mybir.dt.from_np(a.dtype), kind="ExternalInput").ap() for n, a in arrays.items()]
    args.append(nc.dram_tensor("out", inputs['x'].shape, F32, kind="ExternalOutput").ap())
    backbone(nc, *args)
    r = _run(nc, [arrays], core_ids=[0])
    return r.results[0]["out"]
```
